# Optimizing a Trainium2 kernel written in Bass

```python
import math
import jax, jax.numpy as jnp
from jax import lax
import numpy as np
import jax
import jax.numpy as jnp

D_MODEL = 1024
BATCH = 1
SEQ = 512
DEPTH = 1

BRANCH_WIDTH = D_MODEL
N_BRANCH = 3
EPS = 1e-6
NEG_INF = -1e30
FORCED = 1e4

LRU_WIDTH = BRANCH_WIDTH
LRU_BLOCKS = 8
LRU_BLOCK = LRU_WIDTH // LRU_BLOCKS
CONV_WIDTH = 4
LRU_C = 8.0

NSA_HEADS = 16
NSA_KV_HEADS = 4
NSA_GROUP = NSA_HEADS // NSA_KV_HEADS
NSA_HEAD_DIM = BRANCH_WIDTH // NSA_HEADS
NSA_WIDTH = NSA_HEADS * NSA_HEAD_DIM
CMP_BLOCK = 32
CMP_STRIDE = 16
CMP_HIDDEN = 256
SLC_BLOCK = 64
SLC_TOP_N = 8
SLC_Q_BLOCK = 64
WINDOW = 256
Q_BLOCK = 128

GLA_HEADS = 4
GLA_KEY_WIDTH = D_MODEL // 2
GLA_VALUE_WIDTH = BRANCH_WIDTH
GLA_DK = GLA_KEY_WIDTH // GLA_HEADS
GLA_DV = GLA_VALUE_WIDTH // GLA_HEADS
GLA_GATE_RANK = 16
GLA_TAU = 16.0
GLA_CHUNK = 32

REL_BUCKETS = 32
REL_MAX_EXACT = 16
REL_MAX_DIST = 128

D_FF = -(-8 * D_MODEL // (3 * 256)) * 256

IN_SIZES = (
    LRU_WIDTH,
    LRU_WIDTH,
    NSA_WIDTH,
    6 * NSA_KV_HEADS * NSA_HEAD_DIM,
    3 * NSA_HEADS,
    GLA_KEY_WIDTH,
    GLA_KEY_WIDTH,
    GLA_VALUE_WIDTH,
    GLA_VALUE_WIDTH,
    GLA_GATE_RANK,
    N_BRANCH * D_MODEL,
)
IN_WIDTH = sum(IN_SIZES)


def rms_norm(x, g):
    xf = x.astype(jnp.float32)
    y = xf * lax.rsqrt(jnp.mean(xf * xf, axis=-1, keepdims=True) + EPS)
    return (y * g.astype(jnp.float32)).astype(x.dtype)

def rel_bucket(dist):
    n = jnp.maximum(dist, 0)
    nf = jnp.maximum(n, REL_MAX_EXACT).astype(jnp.float32)
    large = REL_MAX_EXACT + (jnp.log(nf / REL_MAX_EXACT) / math.log(REL_MAX_DIST / REL_MAX_EXACT)
                             * (REL_BUCKETS - REL_MAX_EXACT)).astype(jnp.int32)
    large = jnp.minimum(large, REL_BUCKETS - 1)
    return jnp.where(n < REL_MAX_EXACT, n, large)

def rglru_mixer(xa, ga, conv_w, conv_b, w_gates, b_gates, lam):
    B_, S_, _ = xa.shape
    f32 = jnp.float32
    xc = lax.conv_general_dilated(
        xa, conv_w[:, None, :].astype(xa.dtype), window_strides=(1,),
        padding=[(CONV_WIDTH - 1, 0)], dimension_numbers=("NWC", "WIO", "NWC"),
        feature_group_count=LRU_WIDTH) + conv_b
    xb = xc.reshape(B_, S_, LRU_BLOCKS, LRU_BLOCK)
    gates = jnp.einsum("bsnc,knce->kbsne", xb, w_gates).reshape(2, B_, S_, LRU_WIDTH) + b_gates[:, None, None, :]
    r = jax.nn.sigmoid(gates[0].astype(f32))
    i = jax.nn.sigmoid(gates[1].astype(f32))
    log_a = -LRU_C * r * jax.nn.softplus(-lam.astype(f32))
    a = jnp.exp(log_a)
    u = jnp.sqrt(-jnp.expm1(2.0 * log_a)) * (i * xc.astype(f32))

    def combine(left, right):
        a1, b1 = left
        a2, b2 = right
        return a1 * a2, a2 * b1 + b2

    _, h = lax.associative_scan(combine, (a, u), axis=1)
    return h.astype(xa.dtype) * jax.nn.gelu(ga)

def compress_blocks(t, pos_emb, w1, w2):
    B_, G_, S_, hd = t.shape
    r = CMP_BLOCK // CMP_STRIDE
    n_cmp = S_ // CMP_STRIDE - r + 1
    ch = t.reshape(B_, G_, S_ // CMP_STRIDE, CMP_STRIDE, hd)
    blocks = jnp.concatenate([ch[:, :, j:j + n_cmp] for j in range(r)], axis=3) + pos_emb
    return jax.nn.gelu(blocks.reshape(B_, G_, n_cmp, CMP_BLOCK * hd) @ w1) @ w2

def nsa_mixer(q, kv, gate, rel_table, cmp_pos, cmp_w1, cmp_w2):
    B_, S_, _ = q.shape
    G, R, hd = NSA_KV_HEADS, NSA_GROUP, NSA_HEAD_DIM
    f32 = jnp.float32
    q = q.reshape(B_, S_, G, R, hd).transpose(0, 2, 3, 1, 4) * (hd ** -0.5)
    kv = kv.reshape(B_, S_, 6, G, hd).transpose(2, 0, 3, 1, 4)
    k_cmp, v_cmp, k_slc, v_slc, k_win, v_win = kv[0], kv[1], kv[2], kv[3], kv[4], kv[5]
    tbl = rel_table.reshape(REL_BUCKETS, G, R)
    pos = jnp.arange(S_)

    kc = compress_blocks(k_cmp, cmp_pos[0], cmp_w1[0], cmp_w2[0])
    vc = compress_blocks(v_cmp, cmp_pos[1], cmp_w1[1], cmp_w2[1])
    n_cmp = kc.shape[2]
    cmp_end = jnp.arange(n_cmp) * CMP_STRIDE + CMP_BLOCK - 1
    valid_c = cmp_end[None, :] <= pos[:, None]
    bias_c = tbl[rel_bucket(pos[:, None] - cmp_end[None, :])].transpose(2, 3, 0, 1)
    logit_c = jnp.einsum("bgrsd,bgcd->bgrsc", q, kc).astype(f32) + bias_c
    p_c = jax.nn.softmax(jnp.where(valid_c, logit_c, NEG_INF), axis=-1) * valid_c
    o_cmp = jnp.einsum("bgrsc,bgcd->bgrsd", p_c.astype(q.dtype), vc)

    n_slc = S_ // SLC_BLOCK
    top_n = min(SLC_TOP_N, n_slc)
    slc_start = jnp.arange(n_slc) * SLC_BLOCK
    cmp_start = cmp_end - (CMP_BLOCK - 1)
    overlap = jnp.clip(jnp.minimum(cmp_start[:, None] + CMP_BLOCK, slc_start[None, :] + SLC_BLOCK)
                       - jnp.maximum(cmp_start[:, None], slc_start[None, :]), 0).astype(f32) / CMP_BLOCK
    imp = jnp.einsum("bgrsc,cj->bgsj", p_c, overlap)
    blk = jnp.arange(n_slc)[None, :]
    cur = (pos // SLC_BLOCK)[:, None]
    forced = (blk == 0) | (blk == cur) | (blk == cur - 1)
    score = jnp.where(forced, FORCED, jnp.where(blk <= cur, imp, -FORCED))
    _, sel = lax.top_k(score, top_n)

    kb = k_slc.reshape(B_, G, n_slc, SLC_BLOCK, hd)
    vb = v_slc.reshape(B_, G, n_slc, SLC_BLOCK, hd)
    nqs = S_ // SLC_Q_BLOCK
    q_blk = q.reshape(B_, G, R, nqs, SLC_Q_BLOCK, hd).transpose(3, 0, 1, 2, 4, 5)
    sel_blk = sel.reshape(B_, G, nqs, SLC_Q_BLOCK, top_n).transpose(2, 0, 1, 3, 4)
    bi = jnp.arange(B_)[:, None, None, None]
    gi = jnp.arange(G)[None, :, None, None]
    gi5 = jnp.arange(G)[None, :, None, None, None]
    tbl_g = tbl.transpose(1, 0, 2)

    def slc_block(args):
        qb, sb, start = args
        ks = kb[bi, gi, sb]
        vs = vb[bi, gi, sb]
        tq = start + jnp.arange(SLC_Q_BLOCK)
        tk = sb[..., None] * SLC_BLOCK + jnp.arange(SLC_BLOCK)
        dist = tq[:, None, None] - tk
        bias = tbl_g[gi5, rel_bucket(dist)].transpose(0, 1, 5, 2, 3, 4)
        logit = jnp.einsum("bgrqd,bgqnld->bgrqnl", qb, ks).astype(f32) + bias
        logit = jnp.where((dist >= 0)[:, :, None], logit, NEG_INF)
        p = jax.nn.softmax(logit.reshape(B_, G, R, SLC_Q_BLOCK, top_n * SLC_BLOCK), axis=-1)
        p = p.reshape(B_, G, R, SLC_Q_BLOCK, top_n, SLC_BLOCK)
        return jnp.einsum("bgrqnl,bgqnld->bgrqd", p.astype(qb.dtype), vs)

    o_slc = lax.map(slc_block, (q_blk, sel_blk, jnp.arange(nqs) * SLC_Q_BLOCK))
    o_slc = o_slc.transpose(1, 2, 3, 0, 4, 5).reshape(B_, G, R, S_, hd)

    nqb = S_ // Q_BLOCK
    nband = WINDOW // Q_BLOCK + 1

    def band(t):
        tp = jnp.pad(t, ((0, 0), (0, 0), ((nband - 1) * Q_BLOCK, 0), (0, 0)))
        tb = tp.reshape(B_, G, nqb + nband - 1, Q_BLOCK, hd)
        return jnp.concatenate([tb[:, :, j:j + nqb] for j in range(nband)], axis=3)

    kw, vw = band(k_win), band(v_win)
    qi = jnp.arange(Q_BLOCK)
    kj = jnp.arange(nband * Q_BLOCK)
    dist_w = (nband - 1) * Q_BLOCK + qi[:, None] - kj[None, :]
    key_pos = jnp.arange(nqb)[:, None] * Q_BLOCK - (nband - 1) * Q_BLOCK + kj[None, :]
    mask_w = ((dist_w >= 0) & (dist_w < WINDOW))[None] & (key_pos >= 0)[:, None, :]
    bias_w = tbl[rel_bucket(dist_w)].transpose(2, 3, 0, 1)[:, :, None]
    qw = q.reshape(B_, G, R, nqb, Q_BLOCK, hd)
    logit_w = jnp.einsum("bgrnqd,bgnkd->bgrnqk", qw, kw).astype(f32) + bias_w
    p_w = jax.nn.softmax(jnp.where(mask_w, logit_w, NEG_INF), axis=-1)
    o_win = jnp.einsum("bgrnqk,bgnkd->bgrnqd", p_w.astype(q.dtype), vw).reshape(B_, G, R, S_, hd)

    g = jax.nn.sigmoid(gate).reshape(B_, S_, 3, G, R).transpose(2, 0, 3, 4, 1)[..., None]
    o = g[0] * o_cmp + g[1] * o_slc + g[2] * o_win
    return o.transpose(0, 3, 1, 2, 4).reshape(B_, S_, NSA_WIDTH)

def gla_mixer(q, k, v, og, lr, wa2, ba, norm_g):
    B_, S_, _ = q.shape
    f32 = jnp.float32
    nc = S_ // GLA_CHUNK
    log_alpha = jax.nn.log_sigmoid((lr @ wa2 + ba).astype(f32)) / GLA_TAU

    def heads(t, d):
        return t.reshape(B_, nc, GLA_CHUNK, GLA_HEADS, d).transpose(1, 0, 3, 2, 4).astype(f32)

    qh = heads(q, GLA_DK) * (GLA_DK ** -0.5)
    kh = heads(k, GLA_DK)
    vh = heads(v, GLA_DV)
    b = jnp.cumsum(heads(log_alpha, GLA_DK), axis=3)
    q_t = qh * jnp.exp(b)
    k_t = kh * jnp.exp(-b)
    b_last = b[:, :, :, -1:]
    k_end = kh * jnp.exp(b_last - b)
    decay = jnp.exp(b_last[:, :, :, 0])
    causal = jnp.tril(jnp.ones((GLA_CHUNK, GLA_CHUNK), bool))
    att = jnp.where(causal, jnp.einsum("nbhcd,nbhsd->nbhcs", q_t, k_t), 0.0)
    o_intra = jnp.einsum("nbhcs,nbhse->nbhce", att, vh)

    def step(state, xs):
        q_c, ke_c, v_c, dec_c = xs
        o = jnp.einsum("bhcd,bhde->bhce", q_c, state)
        state = state * dec_c[..., None] + jnp.einsum("bhcd,bhce->bhde", ke_c, v_c)
        return state, o

    s0 = jnp.zeros((B_, GLA_HEADS, GLA_DK, GLA_DV), f32)
    _, o_inter = lax.scan(step, s0, (q_t, k_end, vh, decay))
    o = rms_norm(o_intra + o_inter, norm_g)
    o = o.transpose(1, 0, 3, 2, 4).reshape(B_, S_, GLA_VALUE_WIDTH)
    return o.astype(og.dtype) * jax.nn.silu(og)

def hybrid_layer(x, rel_table, norm_g, w_in, conv_w, conv_b, lru_w_gates, lru_b_gates, lru_lambda,
                 cmp_pos, cmp_w1, cmp_w2, gla_wa2, gla_ba, gla_norm, w_branch, w_out, w_ffn_in, w_ffn_out):
    B_, S_, D_ = x.shape
    h = rms_norm(x, norm_g[0])
    proj = h @ w_in
    cuts, acc = [], 0
    for size in IN_SIZES[:-1]:
        acc += size
        cuts.append(acc)
    (lru_x, lru_g, nsa_q, nsa_kv, nsa_gate, gla_q, gla_k, gla_v, gla_og, gla_lr,
     merge_logit) = jnp.split(proj, cuts, axis=-1)
    y_a = rglru_mixer(lru_x, lru_g, conv_w, conv_b, lru_w_gates, lru_b_gates, lru_lambda)
    y_b = nsa_mixer(nsa_q, nsa_kv, nsa_gate, rel_table, cmp_pos, cmp_w1, cmp_w2)
    y_c = gla_mixer(gla_q, gla_k, gla_v, gla_og, gla_lr, gla_wa2, gla_ba, gla_norm)
    gates = jax.nn.sigmoid(merge_logit.reshape(B_, S_, N_BRANCH, D_))
    merged = (gates[:, :, 0] * (y_a @ w_branch[0])
              + gates[:, :, 1] * (y_b @ w_branch[1])
              + gates[:, :, 2] * (y_c @ w_branch[2]))
    x = x + rms_norm(merged @ w_out, norm_g[1])
    h = rms_norm(x, norm_g[2])
    gt, up = jnp.split(h @ w_ffn_in, 2, axis=-1)
    x = x + rms_norm((jax.nn.silu(gt) * up) @ w_ffn_out, norm_g[3])
    return x

def first_inputs(seed: int = 0) -> dict:
    key = jax.random.key(seed)
    ks = jax.random.split(key, 20)
    f32 = jnp.float32

    def nrm(k, shape, scale):
        return jax.random.normal(k, shape, f32) * scale

    u = jax.random.uniform(ks[8], (DEPTH, LRU_WIDTH), f32, 0.9, 0.999)
    s = u ** (1.0 / LRU_C)
    return {
        "x": nrm(ks[0], (BATCH, SEQ, D_MODEL), 1.0),
        "rel_table": nrm(ks[1], (REL_BUCKETS, NSA_HEADS), 0.5),
        "norm_g": 1.0 + nrm(ks[2], (DEPTH, 4, D_MODEL), 0.05),
        "w_in": nrm(ks[3], (DEPTH, D_MODEL, IN_WIDTH), D_MODEL ** -0.5),
        "conv_w": nrm(ks[4], (DEPTH, CONV_WIDTH, LRU_WIDTH), CONV_WIDTH ** -0.5),
        "conv_b": nrm(ks[5], (DEPTH, LRU_WIDTH), 0.01),
        "lru_w_gates": nrm(ks[6], (DEPTH, 2, LRU_BLOCKS, LRU_BLOCK, LRU_BLOCK), LRU_BLOCK ** -0.5),
        "lru_b_gates": nrm(ks[7], (DEPTH, 2, LRU_WIDTH), 0.01),
        "lru_lambda": jnp.log(s) - jnp.log1p(-s),
        "cmp_pos": nrm(ks[9], (DEPTH, 2, CMP_BLOCK, NSA_HEAD_DIM), 0.1),
        "cmp_w1": nrm(ks[10], (DEPTH, 2, CMP_BLOCK * NSA_HEAD_DIM, CMP_HIDDEN), (CMP_BLOCK * NSA_HEAD_DIM) ** -0.5),
        "cmp_w2": nrm(ks[11], (DEPTH, 2, CMP_HIDDEN, NSA_HEAD_DIM), CMP_HIDDEN ** -0.5),
        "gla_wa2": nrm(ks[12], (DEPTH, GLA_GATE_RANK, GLA_KEY_WIDTH), GLA_GATE_RANK ** -0.5),
        "gla_ba": 1.0 + nrm(ks[13], (DEPTH, GLA_KEY_WIDTH), 0.5),
        "gla_norm": 1.0 + nrm(ks[14], (DEPTH, GLA_DV), 0.05),
        "w_branch": nrm(ks[15], (DEPTH, N_BRANCH, BRANCH_WIDTH, D_MODEL), BRANCH_WIDTH ** -0.5),
        "w_out": nrm(ks[16], (DEPTH, D_MODEL, D_MODEL), D_MODEL ** -0.5),
        "w_ffn_in": nrm(ks[17], (DEPTH, D_MODEL, 2 * D_FF), D_MODEL ** -0.5),
        "w_ffn_out": nrm(ks[18], (DEPTH, D_FF, D_MODEL), D_FF ** -0.5),
    }

def first_block(x, rel_table, norm_g, w_in, conv_w, conv_b, lru_w_gates, lru_b_gates, lru_lambda,
              cmp_pos, cmp_w1, cmp_w2, gla_wa2, gla_ba, gla_norm, w_branch, w_out, w_ffn_in, w_ffn_out):
    for l in range(DEPTH):
        x = hybrid_layer(x, rel_table, norm_g[l], w_in[l], conv_w[l], conv_b[l], lru_w_gates[l],
                         lru_b_gates[l], lru_lambda[l], cmp_pos[l], cmp_w1[l], cmp_w2[l],
                         gla_wa2[l], gla_ba[l], gla_norm[l], w_branch[l], w_out[l],
                         w_ffn_in[l], w_ffn_out[l])
    return x


DEPTH_2 = 2

N_MIXERS = 2

SSD_D_INNER = 2 * D_MODEL
SSD_HEAD_DIM = 64
SSD_N_HEADS = SSD_D_INNER // SSD_HEAD_DIM
SSD_N_GROUPS = 4
SSD_HEADS_PER_GROUP = SSD_N_HEADS // SSD_N_GROUPS
SSD_D_STATE = 128
SSD_D_CONV = 4
SSD_CHUNK = 128
SSD_CONV_DIM = SSD_D_INNER + 2 * SSD_N_GROUPS * SSD_D_STATE
SSD_D_IN_PROJ = SSD_D_INNER + SSD_CONV_DIM + SSD_N_HEADS

ATT_HEAD_DIM = 64
ATT_HEADS_PER_GROUP = 8
ATT_PATTERNS = ((128, 1), (512, 4), (2048, 16))
ATT_N_GROUPS = len(ATT_PATTERNS)
ATT_QKV_DIM = ATT_N_GROUPS * 3 * ATT_HEADS_PER_GROUP * ATT_HEAD_DIM
ATT_OUT_DIM = ATT_HEADS_PER_GROUP * ATT_HEAD_DIM
ROPE_THETA = 500000.0
ROPE_DIM = ATT_HEAD_DIM // 4

MOE_N_GROUPS = 4
MOE_EXPERTS_PER_GROUP = 8
MOE_N_EXPERTS = MOE_N_GROUPS * MOE_EXPERTS_PER_GROUP
MOE_TOP_K = 2
MOE_HIDDEN = 512
MOE_BLOCK = 128

DEEPNORM_ALPHA = (2 * DEPTH_2) ** 0.25
DEEPNORM_BETA = (8 * DEPTH_2) ** -0.25
LN_EPS = 1e-5
RMS_EPS = 1e-5
NEG_INF_2 = -1e30


def _layer_norm(x, g, b):
    xf = x.astype(jnp.float32)
    mu = jnp.mean(xf, -1, keepdims=True)
    var = jnp.mean(jnp.square(xf - mu), -1, keepdims=True)
    return ((xf - mu) * lax.rsqrt(var + LN_EPS) * g + b).astype(x.dtype)

def _rope_tables(positions):
    inv_freq = ROPE_THETA ** (-jnp.arange(0, ROPE_DIM, 2, dtype=jnp.float32) / ROPE_DIM)
    ang = positions.astype(jnp.float32)[..., None] * inv_freq
    return jnp.cos(ang)[:, :, None, :], jnp.sin(ang)[:, :, None, :]

def _apply_partial_rope(t, cos, sin):
    half = ROPE_DIM // 2
    t1, t2, rest = t[..., :half], t[..., half:ROPE_DIM], t[..., ROPE_DIM:]
    cos = cos.astype(t.dtype)
    sin = sin.astype(t.dtype)
    return jnp.concatenate([t1 * cos - t2 * sin, t2 * cos + t1 * sin, rest], -1)

def _causal_depthwise_conv(u, w, b):
    c = u.shape[-1]
    y = lax.conv_general_dilated(u, w.reshape(SSD_D_CONV, 1, c), window_strides=(1,),
                                 padding=((SSD_D_CONV - 1, 0),),
                                 dimension_numbers=('NWC', 'WIO', 'NWC'),
                                 feature_group_count=c)
    return y + b

def _ssd_chunked_scan(x, dt, a, b_in, c_in):
    bsz, s = x.shape[:2]
    nc = s // SSD_CHUNK
    Q, G, E, P, N = SSD_CHUNK, SSD_N_GROUPS, SSD_HEADS_PER_GROUP, SSD_HEAD_DIM, SSD_D_STATE
    xr = (x.astype(jnp.float32) * dt[..., None]).reshape(bsz, nc, Q, G, E, P)
    da = (dt * a).reshape(bsz, nc, Q, G, E).transpose(0, 1, 3, 4, 2)
    br = b_in.astype(jnp.float32).reshape(bsz, nc, Q, G, N)
    cr = c_in.astype(jnp.float32).reshape(bsz, nc, Q, G, N)
    da_cs = jnp.cumsum(da, -1)
    causal = jnp.tril(jnp.ones((Q, Q), bool))
    decay_in = jnp.exp(jnp.where(causal, da_cs[..., :, None] - da_cs[..., None, :], -jnp.inf))
    cb = jnp.einsum('bclgn,bcsgn->bcgls', cr, br)
    y_diag = jnp.einsum('bcgls,bcgels,bcsgep->bclgep', cb, decay_in, xr)
    decay_to_end = jnp.exp(da_cs[..., -1:] - da_cs)
    states = jnp.einsum('bclgn,bcgel,bclgep->bcgepn', br, decay_to_end, xr)
    chunk_decay = jnp.exp(da_cs[..., -1])

    def step(h, inp):
        s_c, dec_c = inp
        return h * dec_c[..., None, None] + s_c, h

    h0 = jnp.zeros((bsz, G, E, P, N), jnp.float32)
    _, prev = lax.scan(step, h0, (jnp.moveaxis(states, 1, 0), jnp.moveaxis(chunk_decay, 1, 0)))
    prev = jnp.moveaxis(prev, 0, 1)
    y_off = jnp.einsum('bclgn,bcgepn,bcgel->bclgep', cr, prev, jnp.exp(da_cs))
    return (y_diag + y_off).reshape(bsz, s, G * E, P)

def _ssd_mixer(x, w_in, conv_w, conv_b, dt_bias, a_log, d_skip, norm_w, w_out):
    bsz, s, _ = x.shape
    zxbcdt = x @ w_in
    z = zxbcdt[..., :SSD_D_INNER]
    xbc = zxbcdt[..., SSD_D_INNER:SSD_D_INNER + SSD_CONV_DIM]
    dt_raw = zxbcdt[..., SSD_D_INNER + SSD_CONV_DIM:]
    xbc = jax.nn.silu(_causal_depthwise_conv(xbc, conv_w, conv_b))
    gn = SSD_N_GROUPS * SSD_D_STATE
    xs = xbc[..., :SSD_D_INNER].reshape(bsz, s, SSD_N_HEADS, SSD_HEAD_DIM)
    b_in = xbc[..., SSD_D_INNER:SSD_D_INNER + gn].reshape(bsz, s, SSD_N_GROUPS, SSD_D_STATE)
    c_in = xbc[..., SSD_D_INNER + gn:].reshape(bsz, s, SSD_N_GROUPS, SSD_D_STATE)
    dt = jax.nn.softplus((dt_raw + dt_bias).astype(jnp.float32))
    a = -jnp.exp(a_log.astype(jnp.float32))
    y = _ssd_chunked_scan(xs, dt, a, b_in, c_in) + xs.astype(jnp.float32) * d_skip.astype(jnp.float32)[:, None]
    y = y.reshape(bsz, s, SSD_D_INNER) * jax.nn.silu(z.astype(jnp.float32))
    yg = y.reshape(bsz, s, SSD_N_GROUPS, -1)
    yg = yg * lax.rsqrt(jnp.mean(jnp.square(yg), -1, keepdims=True) + RMS_EPS)
    y = (yg.reshape(bsz, s, SSD_D_INNER) * norm_w).astype(x.dtype)
    return y @ w_out

def _dilated_window_attention(q, k, v, window, dilation):
    bsz, s, h, d = q.shape
    w = window // dilation
    n = s // dilation
    nb = -(-n // w)
    n_pad = nb * w - n

    def to_residues(t):
        return t.reshape(bsz, n, dilation, h, d).transpose(0, 2, 1, 3, 4)

    def key_blocks(t):
        t = jnp.pad(to_residues(t), ((0, 0), (0, 0), (w, n_pad), (0, 0), (0, 0)))
        t = t.reshape(bsz, dilation, nb + 1, w, h, d)
        return jnp.concatenate([t[:, :, :-1], t[:, :, 1:]], axis=3)

    q_r = jnp.pad(to_residues(q), ((0, 0), (0, 0), (0, n_pad), (0, 0), (0, 0)))
    q_r = q_r.reshape(bsz, dilation, nb, w, h, d).astype(jnp.float32)
    k_b = key_blocks(k).astype(jnp.float32)
    v_b = key_blocks(v).astype(jnp.float32)
    scores = jnp.einsum('brnqhd,brnkhd->brnhqk', q_r, k_b) * (ATT_HEAD_DIM ** -0.5)
    qi = jnp.arange(w)[:, None]
    ki = jnp.arange(2 * w)[None, :]
    blk = jnp.arange(nb)[:, None, None]
    valid = (ki >= qi) & (ki <= qi + w) & (blk * w + ki - w >= 0)
    scores = jnp.where(valid[None, None, :, None], scores, NEG_INF_2)
    m = jnp.max(scores, -1)
    p = jnp.exp(scores - m[..., None])
    l = jnp.sum(p, -1)
    m_t = m.transpose(0, 1, 2, 4, 3)
    l_t = l.transpose(0, 1, 2, 4, 3)
    o = jnp.einsum('brnhqk,brnkhd->brnqhd', p, v_b) / l_t[..., None]

    def from_residues(t):
        t = t.reshape(bsz, dilation, nb * w, *t.shape[4:])[:, :, :n]
        t = jnp.moveaxis(t, 1, 2)
        return t.reshape(bsz, s, *t.shape[3:])

    return from_residues(o), from_residues(m_t), from_residues(l_t)

def _dilated_attention_mixer(x, cos, sin, w_qkv, w_o):
    bsz, s, _ = x.shape
    qkv = (x @ w_qkv).reshape(bsz, s, ATT_N_GROUPS, 3, ATT_HEADS_PER_GROUP, ATT_HEAD_DIM)
    outs, maxes, dens = [], [], []
    for g, (window, dilation) in enumerate(ATT_PATTERNS):
        q = _apply_partial_rope(qkv[:, :, g, 0], cos, sin)
        k = _apply_partial_rope(qkv[:, :, g, 1], cos, sin)
        o, m, l = _dilated_window_attention(q, k, qkv[:, :, g, 2], window, dilation)
        outs.append(o)
        maxes.append(m)
        dens.append(l)
    o = jnp.stack(outs)
    m = jnp.stack(maxes)
    l = jnp.stack(dens)
    wgt = l * jnp.exp(m - jnp.max(m, 0, keepdims=True))
    merged = jnp.sum(wgt[..., None] * o, 0) / jnp.sum(wgt, 0)[..., None]
    return merged.reshape(bsz, s, ATT_OUT_DIM).astype(x.dtype) @ w_o

def _hierarchical_moe(x, w_rg, b_rg, w_re, b_re, w_gate, w_up, w_down):
    bsz, s, d = x.shape
    t = bsz * s
    xf = x.reshape(t, d)
    g_logits = (xf @ w_rg + b_rg).astype(jnp.float32)
    g_w, g_idx = lax.top_k(jax.nn.softmax(g_logits, axis=-1), 1)
    e_logits = (xf @ w_re + b_re).astype(jnp.float32).reshape(t, MOE_N_GROUPS, MOE_EXPERTS_PER_GROUP)
    e_logits = e_logits[jnp.arange(t), g_idx[:, 0]]
    e_w, e_idx = lax.top_k(jax.nn.softmax(e_logits, axis=-1), MOE_TOP_K)
    e_w = e_w / jnp.sum(e_w, -1, keepdims=True)
    gates = (g_w * e_w).reshape(-1)
    expert_id = (g_idx * MOE_EXPERTS_PER_GROUP + e_idx).reshape(-1).astype(jnp.int32)
    token_id = jnp.repeat(jnp.arange(t, dtype=jnp.int32), MOE_TOP_K)
    n_assign = t * MOE_TOP_K
    n_blocks = -(-n_assign // MOE_BLOCK) + MOE_N_EXPERTS
    n_rows = n_blocks * MOE_BLOCK
    order = jnp.argsort(expert_id)
    sorted_e = expert_id[order]
    counts = jnp.bincount(expert_id, length=MOE_N_EXPERTS)
    padded = (counts + MOE_BLOCK - 1) // MOE_BLOCK * MOE_BLOCK
    pad_end = jnp.cumsum(padded)
    pad_start = pad_end - padded
    cnt_start = jnp.cumsum(counts) - counts
    dest = pad_start[sorted_e] + jnp.arange(n_assign, dtype=jnp.int32) - cnt_start[sorted_e]
    row_tok = jnp.full((n_rows,), t, jnp.int32).at[dest].set(token_id[order])
    row_gate = jnp.zeros((n_rows,), x.dtype).at[dest].set(gates[order].astype(x.dtype))
    block_e = jnp.minimum(jnp.searchsorted(pad_end, jnp.arange(n_blocks) * MOE_BLOCK, side='right'),
                          MOE_N_EXPERTS - 1)
    x_rows = jnp.concatenate([xf, jnp.zeros((1, d), x.dtype)], 0)[row_tok]
    x_rows = x_rows.reshape(n_blocks, MOE_BLOCK, d)

    def expert_block(args):
        xb, e = args
        h = jax.nn.silu(xb @ w_gate[e]) * (xb @ w_up[e])
        return h @ w_down[e]

    y_rows = lax.map(expert_block, (x_rows, block_e)).reshape(n_rows, d)
    y = jax.ops.segment_sum(y_rows * row_gate[:, None], row_tok, num_segments=t + 1)[:t]
    return y.reshape(bsz, s, d)

def second_inputs(seed: int = 0) -> dict:
    key = jax.random.key(seed)
    ks = jax.random.split(key, 24)
    f32 = jnp.float32
    n_ssd = len(range(0, DEPTH_2, N_MIXERS))
    n_att = len(range(1, DEPTH_2, N_MIXERS))

    def nrm(k, shape, scale):
        return jax.random.normal(k, shape, f32) * scale

    x = jax.random.normal(ks[0], (BATCH, SEQ, D_MODEL), f32)
    positions = jnp.broadcast_to(jnp.arange(SEQ, dtype=jnp.int32), (BATCH, SEQ))
    dt0 = jnp.exp(jax.random.uniform(ks[4], (n_ssd, SSD_N_HEADS), f32) * (np.log(0.1) - np.log(0.001)) + np.log(0.001))
    return {
        'x': x,
        'positions': positions,
        'ssd_w_in': nrm(ks[1], (n_ssd, D_MODEL, SSD_D_IN_PROJ), D_MODEL ** -0.5),
        'ssd_conv_w': nrm(ks[2], (n_ssd, SSD_D_CONV, SSD_CONV_DIM), SSD_D_CONV ** -0.5),
        'ssd_conv_b': nrm(ks[3], (n_ssd, SSD_CONV_DIM), 0.02),
        'ssd_dt_bias': dt0 + jnp.log(-jnp.expm1(-dt0)),
        'ssd_a_log': jnp.log(jax.random.uniform(ks[5], (n_ssd, SSD_N_HEADS), f32, 1.0, 16.0)),
        'ssd_d': 1.0 + nrm(ks[6], (n_ssd, SSD_N_HEADS), 0.01),
        'ssd_norm_w': 1.0 + nrm(ks[7], (n_ssd, SSD_D_INNER), 0.02),
        'ssd_w_out': nrm(ks[8], (n_ssd, SSD_D_INNER, D_MODEL), SSD_D_INNER ** -0.5 * DEEPNORM_BETA),
        'attn_w_qkv': nrm(ks[9], (n_att, D_MODEL, ATT_QKV_DIM), D_MODEL ** -0.5),
        'attn_w_o': nrm(ks[10], (n_att, ATT_OUT_DIM, D_MODEL), ATT_OUT_DIM ** -0.5 * DEEPNORM_BETA),
        'ln_g': 1.0 + nrm(ks[11], (DEPTH_2, 2, D_MODEL), 0.02),
        'ln_b': nrm(ks[12], (DEPTH_2, 2, D_MODEL), 0.02),
        'moe_w_router_group': nrm(ks[13], (DEPTH_2, D_MODEL, MOE_N_GROUPS), D_MODEL ** -0.5),
        'moe_b_router_group': nrm(ks[14], (DEPTH_2, MOE_N_GROUPS), 0.01),
        'moe_w_router_expert': nrm(ks[15], (DEPTH_2, D_MODEL, MOE_N_EXPERTS), D_MODEL ** -0.5),
        'moe_b_router_expert': nrm(ks[16], (DEPTH_2, MOE_N_EXPERTS), 0.01),
        'moe_w_gate': nrm(ks[17], (DEPTH_2, MOE_N_EXPERTS, D_MODEL, MOE_HIDDEN), D_MODEL ** -0.5),
        'moe_w_up': nrm(ks[18], (DEPTH_2, MOE_N_EXPERTS, D_MODEL, MOE_HIDDEN), D_MODEL ** -0.5),
        'moe_w_down': nrm(ks[19], (DEPTH_2, MOE_N_EXPERTS, MOE_HIDDEN, D_MODEL), MOE_HIDDEN ** -0.5 * DEEPNORM_BETA),
    }

def second_block(x, positions, ssd_w_in, ssd_conv_w, ssd_conv_b, ssd_dt_bias, ssd_a_log, ssd_d,
              ssd_norm_w, ssd_w_out, attn_w_qkv, attn_w_o, ln_g, ln_b,
              moe_w_router_group, moe_b_router_group, moe_w_router_expert, moe_b_router_expert,
              moe_w_gate, moe_w_up, moe_w_down):
    cos, sin = _rope_tables(positions)
    for i in range(DEPTH_2):
        j = i // N_MIXERS
        if i % N_MIXERS == 0:
            mix = _ssd_mixer(x, ssd_w_in[j], ssd_conv_w[j], ssd_conv_b[j], ssd_dt_bias[j],
                             ssd_a_log[j], ssd_d[j], ssd_norm_w[j], ssd_w_out[j])
        else:
            mix = _dilated_attention_mixer(x, cos, sin, attn_w_qkv[j], attn_w_o[j])
        x = _layer_norm(DEEPNORM_ALPHA * x + mix, ln_g[i, 0], ln_b[i, 0])
        ffn = _hierarchical_moe(x, moe_w_router_group[i], moe_b_router_group[i],
                                moe_w_router_expert[i], moe_b_router_expert[i],
                                moe_w_gate[i], moe_w_up[i], moe_w_down[i])
        x = _layer_norm(DEEPNORM_ALPHA * x + ffn, ln_g[i, 1], ln_b[i, 1])
    return x


def setup_inputs(seed=0):
    out = dict(first_inputs(seed))
    for name, value in second_inputs(seed + 1).items():
        if name != "x":
            out[name + "_2"] = value
    return out


def reference(
    x, rel_table, norm_g, w_in, conv_w, conv_b, lru_w_gates, lru_b_gates, lru_lambda, cmp_pos,
    cmp_w1, cmp_w2, gla_wa2, gla_ba, gla_norm, w_branch, w_out, w_ffn_in, w_ffn_out,
    positions_2, ssd_w_in_2, ssd_conv_w_2, ssd_conv_b_2, ssd_dt_bias_2, ssd_a_log_2, ssd_d_2,
    ssd_norm_w_2, ssd_w_out_2, attn_w_qkv_2, attn_w_o_2, ln_g_2, ln_b_2, moe_w_router_group_2,
    moe_b_router_group_2, moe_w_router_expert_2, moe_b_router_expert_2, moe_w_gate_2,
    moe_w_up_2, moe_w_down_2,
):
    x = first_block(
        x, rel_table, norm_g, w_in, conv_w, conv_b, lru_w_gates, lru_b_gates, lru_lambda,
        cmp_pos, cmp_w1, cmp_w2, gla_wa2, gla_ba, gla_norm, w_branch, w_out, w_ffn_in,
        w_ffn_out,
    )
    return second_block(
        x, positions_2, ssd_w_in_2, ssd_conv_w_2, ssd_conv_b_2, ssd_dt_bias_2, ssd_a_log_2,
        ssd_d_2, ssd_norm_w_2, ssd_w_out_2, attn_w_qkv_2, attn_w_o_2, ln_g_2, ln_b_2,
        moe_w_router_group_2, moe_b_router_group_2, moe_w_router_expert_2,
        moe_b_router_expert_2, moe_w_gate_2, moe_w_up_2, moe_w_down_2,
    )


_drawn_inputs = setup_inputs


def setup_inputs(seed=0):
    import zlib

    import numpy as np

    out = dict(_drawn_inputs(seed))
    spreads = {}
    factors = {'lru_b_gates': 8.0,
     'ssd_conv_b_2': 8.0,
     'ssd_d_2': 8.0,
     'ssd_norm_w_2': 8.0,
     'moe_b_router_group_2': 8.0,
     'moe_b_router_expert_2': 7.078}
    for name, (base, spread) in spreads.items():
        noise = np.random.default_rng([zlib.crc32(name.encode()), seed]).standard_normal(out[name].shape)
        drawn = base * np.exp(spread * noise) if base else spread * noise
        out[name] = jnp.asarray(drawn.astype(out[name].dtype))
    for name, factor in factors.items():
        out[name] = (out[name] * factor).astype(out[name].dtype)
    return out
```

```python
from contextlib import ExitStack, contextmanager

import numpy as np
import concourse.bass as bass
from concourse import mybir
from concourse.bass import ds

F32 = mybir.dt.float32
I32 = mybir.dt.int32
U32 = mybir.dt.uint32
ALU = mybir.AluOpType
ACT = mybir.ActivationFunctionType
AX = mybir.AxisListType.X

P = 128
S = 512
TT = S // P
D = 1024
KD = D // P
EPS = 1e-6
NEG = -1e30

C_LRU_X, C_LRU_G, C_Q, C_KV = 0, 1024, 2048, 3072
C_GATE = C_KV + 1536
C_GLA_Q = C_GATE + 48
C_GLA_K = C_GLA_Q + 512
C_GLA_V = C_GLA_K + 512
C_GLA_OG = C_GLA_V + 1024
C_GLA_LR = C_GLA_OG + 1024
C_MERGE = C_GLA_LR + 16
D_FF = 2816
KF = D_FF // P

CW = 256


class Settle:

    def __init__(self, eng, sem, base=0):
        self.eng, self.sem, self.base, self.n = eng, sem, base, 0

    def __call__(self, ins):
        ins.then_inc(self.sem, 1)
        self.n += 1
        self.eng.wait_ge(self.sem, self.base + self.n)


RESTING = []


@contextmanager
def stage(nc, *names):
    sems = [nc.alloc_semaphore(f"{n}_{nc.next_id()}") for n in names]
    with nc.Block() as block:
        yield block, sems
    for sem in RESTING:
        nc.release_semaphore(sem)
    for sem in sems:
        nc.gpsimd.sem_clear(sem)
    RESTING[:] = sems


def constants(nc, K, A):
    K.ident = nc.alloc_sbuf_tensor("ident", [P, P], F32)
    K.vec = nc.alloc_sbuf_tensor("vec", [P, 2, P], F32)
    rows = nc.alloc_sbuf_tensor("vec_rows", [P, 2, P], F32)
    parts = [[("g0", A.norm_g[0, 0:1, :]), ("g2", A.norm_g[0, 2:3, :]), ("conv_w", A.conv_w[0]), ("conv_b", A.conv_b),
              ("lru_b", A.lru_b_gates[0]), ("lam", A.lru_lambda), ("gla_ba", A.gla_ba), ("gla_norm", A.gla_norm),
              ("ssd_norm", A.ssd_norm_w_2)],
             [("ssd_conv_w", A.ssd_conv_w_2[0]), ("ssd_conv_b", A.ssd_conv_b_2)]]
    K.col = {}
    with stage(nc, "loaded", "zeroed", "ident_set", "turned", "copied") as (block, (loaded, zeroed, ident_set, turned, copied)):
        n_loads = sum(len(x) for x in parts)

        @block.sync
        def _(sp):
            for half, group in enumerate(parts):
                at = 0
                for name, ap in group:
                    n = int(np.prod(ap.shape)) // P
                    K.col[name] = (half, at)
                    if half == 0 and at == 0:
                        sp.wait_ge(zeroed, 1)
                    sp.dma_start(rows[at:at + n, half, :], ap.rearrange("a (k p) -> (a k) p", p=P)).then_inc(loaded, 16)
                    at += n

        @block.gpsimd
        def _(pool):
            nc.gpsimd.memset(rows[:, :, :], 0.0).then_inc(zeroed, 1)
            nc.gpsimd.memset(K.ident[:, :], 0.0).then_inc(ident_set, 1)
            pool.wait_ge(ident_set, 1)
            nc.gpsimd.affine_select(out=K.ident[:, :], in_=K.ident[:, :], compare_op=ALU.not_equal, fill=1.0,
                                    base=0, pattern=[[-1, P]], channel_multiplier=1).then_inc(ident_set, 1)

        @block.tensor
        def _(pe):
            pe.wait_ge(ident_set, 2)
            pe.wait_ge(loaded, 16 * n_loads)
            for half in range(2):
                nc.tensor.transpose(K.bank[half][:, 0:P], rows[:, half, :], K.ident[:, :]).then_inc(turned, 1)

        @block.vector
        def _(dve):
            for half in range(2):
                dve.wait_ge(turned, half + 1)
                nc.vector.tensor_copy(K.vec[:, half, :], K.bank[half][:, 0:P]).then_inc(copied, 1)


def vcol(K, name, i=0, n=1):
    half, at = K.col[name]
    return K.vec[:, half, at + i:at + i + n]


def rms_scale(nc, K, src, dst, width=D):
    with ExitStack() as mem:
        junk = mem.enter_context(nc.sbuf_tensor(f"sq_{nc.next_id()}", [P, width], F32))
        stat = mem.enter_context(nc.sbuf_tensor(f"stat_{nc.next_id()}", [P, 3, TT], F32))
        with stage(nc, "squared", "meaned", "rooted", "inverted", "scaled") as (block, (squared, meaned, rooted, inverted, scaled)):
            @block.scalar
            def _(act):
                for t in range(TT):
                    if t:
                        act.wait_ge(squared, t)
                    nc.scalar.activation(junk[:, :], src[:, t, :], ACT.Square, accum_out=stat[:, 0, t:t + 1]).then_inc(squared, 1)
                act.wait_ge(meaned, 1)
                nc.scalar.activation(stat[:, 2, :], stat[:, 1, :], ACT.Sqrt).then_inc(rooted, 1)

            @block.vector
            def _(dve):
                dve.wait_ge(squared, TT)
                nc.vector.tensor_scalar(stat[:, 1, :], stat[:, 0, :], 1.0 / width, EPS, ALU.mult, ALU.add).then_inc(meaned, 1)
                dve.wait_ge(rooted, 1)
                nc.vector.reciprocal(stat[:, 0, :], stat[:, 2, :]).then_inc(inverted, 1)
                dve.wait_ge(inverted, 1)
                for t in range(TT):
                    nc.vector.tensor_scalar(dst[:, t, :], src[:, t, :], stat[:, 0, t:t + 1], None, ALU.mult).then_inc(scaled, 1)


def to_channels(nc, K, src, dst, n, scale=None, residues=False):
    with stage(nc, "turned", "copied") as (block, (turned, copied)):
        @block.tensor
        def _(pe):
            for k in range(n):
                if k >= 8:
                    pe.wait_ge(copied, k - 7)
                for t in range(TT):
                    last = nc.tensor.transpose(K.bank[k % 8][:, t * P:(t + 1) * P], src[:, t, k * P:(k + 1) * P], K.ident[:, :])
                last.then_inc(turned, 1)

        @block.scalar
        def _(act):
            for k in range(n):
                act.wait_ge(turned, k + 1)
                s = 1.0 if scale is None else scale(k)
                out, in_ = dst[:, k, 0:S], K.bank[k % 8][:, :]
                if residues:
                    out, in_ = out.rearrange("p (j t) -> p t j", t=TT), in_.rearrange("p (t j) -> p t j", t=TT)
                nc.scalar.activation(out, in_, ACT.Copy, scale=s).then_inc(copied, 1)


def project_channels(nc, K, w, kt, rhs, chunks, column, evacuate):
    tiles = CW // P
    with nc.sbuf_tensor(f"ring_{nc.next_id()}", [P, 2, kt, CW], F32) as ring, stage(nc, "w_loaded0", "w_loaded1", "products", "bank_free") as (block, (w0, w1, products, bank_free)):
        w_loaded = [w0, w1]

        @block.sync
        def _(sp):
            for s in range(2):
                sp.dma_start(ring[:, s], w[:, :, ds(column(s), CW)]).then_inc(w_loaded[s], 16)
            if chunks > 2:
                with sp.Fori(1, chunks // 2) as i:
                    for s in range(2):
                        sp.wait_ge(products, (i * 2 + s - 1) * tiles)
                        sp.dma_start(ring[:, s], w[:, :, ds(column(i * 2 + s), CW)]).then_inc(w_loaded[s], 16)

        @block.tensor
        def _(pe):
            with pe.Fori(0, chunks // 2) as i:
                for s in range(2):
                    pe.wait_ge(w_loaded[s], i * 16 + 16)
                    for m in range(tiles):
                        b = s * tiles + m
                        pe.wait_ge(bank_free, i * 2 * tiles + b + 1)
                        for k in range(kt):
                            last = nc.tensor.matmul(K.bank[b][:, :], ring[:, s, k, m * P:(m + 1) * P], rhs[:, k, :],
                                                    start=(k == 0), stop=(k == kt - 1))
                        last.then_inc(products, 1)

        @block.scalar
        def _(act):
            act.sem_inc(bank_free, 2 * tiles)
            with act.Fori(0, chunks // 2) as i:
                for b in range(2 * tiles):
                    act.wait_ge(products, i * 2 * tiles + b + 1)
                    evacuate(K.bank[b][:, :], i * 2 * tiles + b).then_inc(bank_free, 1)


def project_tokens(nc, K, w, kt, lhs, chunks, column, evacuate, rows=lambda t: slice(t * P, (t + 1) * P)):
    with nc.sbuf_tensor(f"ring_{nc.next_id()}", [P, 2, kt, CW], F32) as ring, stage(nc, "w_loaded0", "w_loaded1", "products", "bank_free") as (block, (w0, w1, products, bank_free)):
        w_loaded = [w0, w1]

        @block.sync
        def _(sp):
            for s in range(2):
                sp.dma_start(ring[:, s], w[:, :, ds(column(s), CW)]).then_inc(w_loaded[s], 16)
            if chunks > 2:
                with sp.Fori(1, chunks // 2) as i:
                    for s in range(2):
                        sp.wait_ge(products, (i * 2 + s - 1) * TT)
                        sp.dma_start(ring[:, s], w[:, :, ds(column(i * 2 + s), CW)]).then_inc(w_loaded[s], 16)

        @block.tensor
        def _(pe):
            with pe.Fori(0, chunks // 2) as i:
                for s in range(2):
                    pe.wait_ge(w_loaded[s], i * 16 + 16)
                    for t in range(TT):
                        b = s * TT + t
                        pe.wait_ge(bank_free, i * 2 * TT + b + 1)
                        for k in range(kt):
                            last = nc.tensor.matmul(K.bank[b][:, 0:CW], lhs[:, k, rows(t)], ring[:, s, k, :],
                                                    start=(k == 0), stop=(k == kt - 1))
                        last.then_inc(products, 1)

        @block.vector
        def _(dve):
            dve.sem_inc(bank_free, 2 * TT)
            with dve.Fori(0, chunks // 2) as i:
                for s in range(2):
                    for t in range(TT):
                        dve.wait_ge(products, i * 2 * TT + s * TT + t + 1)
                        evacuate(K.bank[s * TT + t][:, 0:CW], t, i * 2 + s).then_inc(bank_free, 1)


def lru(nc, K, A, y):
    with ExitStack() as mem:
        sb = lambda n, s: mem.enter_context(nc.sbuf_tensor(n, s, F32))
        PAD = 3
        xa = sb("lru_xa", [P, KD, S + PAD])
        xc, r, gi, u = (sb(f"lru_{n}", [P, KD, S]) for n in ("xc", "r", "i", "u"))
        wg = sb("lru_wg", [P, 2 * KD, P])
        sp8 = sb("lru_sp8", [P, 4, KD])
        w = A.w_in[0].rearrange("(k p) m -> p k m", p=P)
        project_channels(nc, K, w, KD, K.hT, 4, lambda c: c * CW + C_LRU_X,
                         lambda bank, m: nc.scalar.activation(xa[:, ds(m, 1), PAD:], bank, ACT.Copy))
        project_channels(nc, K, w, KD, K.hT, 4, lambda c: c * CW + C_LRU_G,
                         lambda bank, m: nc.scalar.activation(y[:, ds(m, 1), :], bank, ACT.Gelu_apprx_tanh))
        with stage(nc, "wg_loaded", "convolved", "products", "gated", "exped", "vec_step", "act_step", "rated", "halved", "rooted") as (
                block, (wg_loaded, convolved, products, gated, exped, vec_step, act_step, rated, halved, rooted)):
            @block.sync
            def _(sp):
                sp.dma_start(wg[:, :, :], A.lru_w_gates[0].rearrange("k n c e -> c (k n) e")).then_inc(wg_loaded, 16)

            @block.tensor
            def _(pe):
                pe.wait_ge(wg_loaded, 16)
                for j in range(2 * KD):
                    pe.wait_ge(convolved, j % KD + 1)
                    if j >= 8:
                        pe.wait_ge(gated, j - 7)
                    nc.tensor.matmul(K.bank[j % 8][:, :], wg[:, j, :], xc[:, j % KD, :], start=True, stop=True).then_inc(products, 1)

            @block.scalar
            def _(act):
                done = Settle(act, act_step)
                done(nc.scalar.activation(sp8[:, 0, :], vcol(K, "lam", 0, KD), ACT.Abs))
                done(nc.scalar.activation(sp8[:, 0, :], sp8[:, 0, :], ACT.Exp, scale=-1.0))
                done(nc.scalar.activation(sp8[:, 0, :], sp8[:, 0, :], ACT.Ln, bias=1.0))
                nc.scalar.activation(sp8[:, 1, :], vcol(K, "lam", 0, KD), ACT.Relu, scale=-1.0).then_inc(exped, 1)
                for j in range(2 * KD):
                    act.wait_ge(products, j + 1)
                    dst = r if j < KD else gi
                    nc.scalar.activation(dst[:, j % KD, :], K.bank[j % 8][:, :], ACT.Sigmoid, bias=vcol(K, "lru_b", j)).then_inc(gated, 1)
                act.wait_ge(rated, 1)
                done(nc.scalar.activation(u[:, :, :], r[:, :, :], ACT.Tanh))
                nc.scalar.activation(r[:, :, :], r[:, :, :], ACT.Exp, scale=-1.0).then_inc(exped, 1)
                act.wait_ge(halved, 1)
                nc.scalar.activation(u[:, :, :], u[:, :, :], ACT.Sqrt).then_inc(rooted, 1)

            @block.vector
            def _(dve):
                done = Settle(dve, vec_step)
                done(nc.vector.memset(xa[:, :, 0:PAD], 0.0))
                for n in range(KD):
                    done(nc.vector.tensor_scalar(xc[:, n, :], xa[:, n, 0:S], vcol(K, "conv_w", n), vcol(K, "conv_b", n), ALU.mult, ALU.add))
                    for j in range(1, 4):
                        ins = nc.vector.scalar_tensor_tensor(out=xc[:, n, :], in0=xa[:, n, j:j + S], scalar=vcol(K, "conv_w", j * KD + n),
                                                             in1=xc[:, n, :], op0=ALU.mult, op1=ALU.add)
                        if j < 3:
                            done(ins)
                    ins.then_inc(convolved, 1)
                dve.wait_ge(exped, 1)
                dve.wait_ge(act_step, 3)
                done(nc.vector.tensor_tensor(sp8[:, 2, :], sp8[:, 0, :], sp8[:, 1, :], ALU.add))
                done(nc.vector.tensor_scalar(sp8[:, 3, :], sp8[:, 2, :], 8.0, None, ALU.mult))
                dve.wait_ge(gated, KD)
                for n in range(KD):
                    done(nc.vector.tensor_scalar(r[:, n, :], r[:, n, :], sp8[:, 3, n:n + 1], None, ALU.mult))
                dve.sem_inc(rated, 1)
                dve.wait_ge(gated, 2 * KD)
                dve.wait_ge(convolved, KD)
                done(nc.vector.tensor_tensor(gi[:, :, :], gi[:, :, :], xc[:, :, :], ALU.mult))
                dve.wait_ge(exped, 2)
                done(nc.vector.tensor_scalar(xc[:, :, :], u[:, :, :], 1.0, None, ALU.add))
                done(nc.vector.reciprocal(xc[:, :, :], xc[:, :, :]))
                nc.vector.scalar_tensor_tensor(out=u[:, :, :], in0=u[:, :, :], scalar=2.0, in1=xc[:, :, :],
                                               op0=ALU.mult, op1=ALU.mult).then_inc(halved, 1)
                dve.wait_ge(rooted, 1)
                done(nc.vector.tensor_tensor(u[:, :, :], u[:, :, :], gi[:, :, :], ALU.mult))
                for n in range(KD):
                    done(nc.vector.tensor_tensor_scan(xc[:, n, :], r[:, n, :], u[:, n, :], 0.0, ALU.mult, ALU.add))
                done(nc.vector.tensor_tensor(y[:, :, :], y[:, :, :], xc[:, :, :], ALU.mult))


class Names:
    pass


def rel_bias_constants():
    n = np.arange(S)
    large = 16 + (np.log(np.maximum(n, 16).astype(np.float32) / np.float32(16)) / np.float32(np.log(128 / 16))
                  * np.float32(16)).astype(np.int32)
    bucket = np.where(n < 16, n, np.minimum(large, 31))
    oh = np.zeros((33, GW), np.float32)
    oh[bucket[S - 1 - np.arange(S)], np.arange(S)] = 1.0
    oh[32, S:] = NEG
    return oh


GW = 640
N_CMP = 31
HD = 64


def rel_bias(nc, K, A):
    K.bias_rows = nc.dram_tensor("bias_rows", (16, GW), F32, kind="Internal").ap()
    oh_dram = nc.inline_tensor(rel_bias_constants(), name="bucket_onehot").ap()
    with ExitStack() as mem:
        sb = lambda n, s: mem.enter_context(nc.sbuf_tensor(n, s, F32))
        oh, table, rows = sb("bucket_oh", [33, GW]), sb("rel_table33", [33, 16]), sb("bias_sb", [16, GW])
        with stage(nc, "loaded", "set", "products", "copied", "stored") as (block, (loaded, is_set, products, copied, stored)):
            @block.vector
            def _(dve):
                nc.vector.memset(table[:, :], 1.0).then_inc(is_set, 1)

            @block.sync
            def _(sp):
                sp.dma_start(oh[:, :], oh_dram).then_inc(loaded, 16)
                sp.wait_ge(is_set, 1)
                sp.dma_start(table[0:32, :], A.rel_table).then_inc(loaded, 16)
                sp.wait_ge(copied, 2)
                sp.dma_start(K.bias_rows, rows[:, :]).then_inc(stored, 16)
                sp.wait_ge(stored, 16)

            @block.tensor
            def _(pe):
                pe.wait_ge(loaded, 32)
                for b, (lo, hi) in enumerate(((0, S), (S, GW))):
                    nc.tensor.matmul(K.bank[b][0:16, 0:hi - lo], table[:, :], oh[:, lo:hi], start=True, stop=True).then_inc(products, 1)

            @block.scalar
            def _(act):
                for b, (lo, hi) in enumerate(((0, S), (S, GW))):
                    act.wait_ge(products, b + 1)
                    nc.scalar.activation(rows[:, lo:hi], K.bank[b][0:16, 0:hi - lo], ACT.Copy).then_inc(copied, 1)


def compressed(nc, K, A, kind, src, sb, kcT, vc):
    with ExitStack() as mem:
        tmp = lambda n, s: mem.enter_context(nc.sbuf_tensor(f"cmp{kind}_{n}", s, F32))
        w1 = tmp("w1", [P, 32, 256])
        w2 = tmp("w2", [P, 2, HD])
        pos_rows, pos = tmp("pos_rows", [32, P]), tmp("pos", [P, 32])
        withpos = tmp("withpos", [P, 2, 2, S])
        hid = tmp("hid", [P, 2, 2, 2, N_CMP])
        with stage(nc, "loaded", "turned", "vec_step", "added", "products", "acted", "outputs", "stored") as (
                block, (loaded, turned, vec_step, added, products, acted, outputs, stored)):
            @block.sync
            def _(sp):
                for a in range(2):
                    sp.dma_start(pos_rows[:, a * HD:(a + 1) * HD], A.cmp_pos[0, kind]).then_inc(loaded, 16)
                for a in range(2):
                    sp.dma_start(w1[a * HD:(a + 1) * HD, :, :], A.cmp_w1[0, kind].rearrange("(j d) m -> d j m", d=HD)).then_inc(loaded, 16)
                sp.dma_start(w2[:, :, :], A.cmp_w2[0, kind].rearrange("(h p) d -> p h d", p=P)).then_inc(loaded, 16)

            @block.tensor
            def _(pe):
                pe.wait_ge(loaded, 80)
                nc.tensor.transpose(K.bank[0][:, 0:32], pos_rows[:, :], K.ident[0:32, 0:32]).then_inc(turned, 1)
                pe.wait_ge(added, 4)
                for h in range(2):
                    for a in range(2):
                        rows = slice(a * HD, (a + 1) * HD)
                        for j in range(32):
                            last = nc.tensor.matmul(K.bank[1 + 2 * h + a][:, 0:2 * N_CMP].rearrange("p (g c) -> p g c", g=2),
                                                    w1[rows, j, h * P:(h + 1) * P],
                                                    withpos[rows, j // 16, :, j:j + 16 * (N_CMP - 1) + 1:16],
                                                    start=(j == 0), stop=(j == 31))
                        last.then_inc(products, 1)
                pe.wait_ge(acted, 4)
                for a in range(2):
                    if kind == 0:
                        for h in range(2):
                            last = nc.tensor.matmul(K.bank[5 + a][a * HD:(a + 1) * HD, 0:2 * N_CMP], w2[:, h, :],
                                                    hid[:, h, a, :, :].rearrange("p g c -> p (g c)"), start=(h == 0), stop=(h == 1))
                    else:
                        for g in range(2):
                            for h in range(2):
                                last = nc.tensor.matmul(K.bank[5 + a][0:N_CMP, g * HD:(g + 1) * HD], hid[:, h, a, g, :],
                                                        w2[:, h, :], start=(h == 0), stop=(h == 1))
                    last.then_inc(outputs, 1)

            @block.vector
            def _(dve):
                done = Settle(dve, vec_step)
                dve.wait_ge(turned, 1)
                done(nc.vector.tensor_copy(pos[:, :], K.bank[0][:, 0:32]))
                for half in range(2):
                    for g in range(2):
                        nc.vector.tensor_tensor(withpos[:, half, g, :].rearrange("p (c j) -> p c j", j=16),
                                                src[:, g, :].rearrange("p (c j) -> p c j", j=16),
                                                pos[:, half * 16:(half + 1) * 16].unsqueeze(1).broadcast_to([P, 32, 16]),
                                                ALU.add).then_inc(added, 1)

            @block.scalar
            def _(act):
                for h in range(2):
                    for a in range(2):
                        act.wait_ge(products, 2 * h + a + 1)
                        nc.scalar.activation(hid[:, h, a, :, :].rearrange("p g c -> p (g c)"), K.bank[1 + 2 * h + a][:, 0:2 * N_CMP],
                                             ACT.Gelu_apprx_tanh).then_inc(acted, 1)
                for a in range(2):
                    act.wait_ge(outputs, a + 1)
                    if kind == 0:
                        nc.scalar.activation(kcT[a * HD:(a + 1) * HD, :, :].rearrange("p g c -> p (g c)"),
                                             K.bank[5 + a][a * HD:(a + 1) * HD, 0:2 * N_CMP], ACT.Copy).then_inc(stored, 1)
                    else:
                        nc.scalar.activation(vc[:, a, :, :].rearrange("c g d -> c (g d)"), K.bank[5 + a][0:N_CMP, 0:2 * HD],
                                             ACT.Copy).then_inc(stored, 1)


def nsa(nc, K, A, y):
    w = A.w_in[0].rearrange("(k p) m -> p k m", p=P)
    rel_bias(nc, K, A)
    with ExitStack() as mem:
        sb = lambda n, s: mem.enter_context(nc.sbuf_tensor(n, s, F32))
        qT = sb("nsa_q", [P, 8, S])
        kT = sb("nsa_k", [P, 4, S])
        v = sb("nsa_v", [P, TT, 2 * CW])
        gate = sb("nsa_gate", [P, TT, 48])
        kcT = sb("nsa_kc", [P, 2, N_CMP])
        vc = sb("nsa_vc", [N_CMP, 2, 2, HD])
        with ExitStack() as inner:
            cmpT = inner.enter_context(nc.sbuf_tensor("nsa_cmp", [P, 4, S], F32))
            project_channels(nc, K, w, KD, K.hT, 2, lambda c: c * CW + C_KV,
                             lambda bank, m: nc.scalar.activation(cmpT[:, ds(m, 1), :], bank, ACT.Copy))
            for kind in range(2):
                compressed(nc, K, A, kind, cmpT[:, 2 * kind:2 * kind + 2, :], sb, kcT, vc)
        project_channels(nc, K, w, KD, K.hT, 2, lambda c: c * 2 * CW + C_KV + 512,
                         lambda bank, m: nc.scalar.activation(kT[:, ds(m, 1), :], bank, ACT.Copy))
        project_tokens(nc, K, w, KD, K.hT, 2, lambda c: c * 2 * CW + C_KV + 768,
                       lambda bank, t, c: nc.vector.tensor_copy(v[:, t, ds(c * CW, CW)], bank))
        nsa_queries(nc, K, w, qT, gate)
        for gp in range(2):
            nsa_attend(nc, K, gp, qT, kT, v, gate, kcT, vc, y)


def backwards(ap):
    (step, n), axes = ap.ap[-1], list(ap.ap[:-1])
    return bass.AP(ap.tensor, ap.offset + step * (n - 1), [*axes, [-step, n]])


def nsa_queries(nc, K, w, qT, gate):
    with ExitStack() as mem:
        wg = mem.enter_context(nc.sbuf_tensor("gate_w", [P, KD, 48], F32))
        ring = mem.enter_context(nc.sbuf_tensor("q_w", [P, KD, 512], F32))
        gateT = mem.enter_context(nc.sbuf_tensor("gateT", [48, S], F32))
        half = KD // 2
        with stage(nc, "g_loaded", "q_loaded", "products", "bank_free") as (block, (g_loaded, q_loaded, products, bank_free)):
            @block.sync
            def _(sp):
                sp.dma_start(wg[:, :, :], w[:, :, C_GATE:C_GATE + 48]).then_inc(g_loaded, 16)
                for gp in range(2):
                    if gp:
                        sp.wait_ge(products, 4)
                    for k in range(KD):
                        for a in range(2):
                            first = C_Q + gp * 512 + a * CW
                            sp.dma_start(ring[:, k, :].rearrange("p (r a d) -> p r a d", a=2, r=4)[:, :, a, :],
                                         w[:, k, first:first + CW].rearrange("p (r d) -> p r d", r=4)).then_inc(q_loaded, 16)

            @block.tensor
            def _(pe):
                for gp in range(2):
                    pe.wait_ge(q_loaded, 16 * 2 * KD * (gp + 1))
                    for r in range(4):
                        b = gp * 4 + r
                        for k in range(KD):
                            last = nc.tensor.matmul(K.bank[b][:, :], ring[:, k, r * P:(r + 1) * P], K.hT[:, k, :], start=(k == 0), stop=(k == KD - 1))
                        last.then_inc(products, 1)
                pe.wait_ge(g_loaded, 16)
                pe.wait_ge(bank_free, 1)
                for k in range(KD):
                    last = nc.tensor.matmul(K.bank[0][0:48, :], wg[:, k, :], K.hT[:, k, :], start=(k == 0), stop=(k == KD - 1))
                last.then_inc(products, 1)
                pe.wait_ge(bank_free, 9)
                for t in range(TT):
                    last = nc.tensor.transpose(K.bank[1][:, t * 48:(t + 1) * 48], gateT[:, t * P:(t + 1) * P], K.ident[0:48, 0:48])
                last.then_inc(products, 1)

            @block.scalar
            def _(act):
                for b in range(8):
                    act.wait_ge(products, b + 1)
                    nc.scalar.activation(qT[:, b, :], K.bank[b][:, :], ACT.Copy, scale=HD ** -0.5).then_inc(bank_free, 1)
                act.wait_ge(products, 9)
                nc.scalar.activation(backwards(gateT[:, :].rearrange("p (t n) -> p t n", t=TT)),
                                     K.bank[0][0:48, :].rearrange("p (t n) -> p t n", t=TT), ACT.Sigmoid).then_inc(bank_free, 1)
                act.wait_ge(products, 10)
                nc.scalar.activation(gate[:, :, :].rearrange("p t c -> p (t c)"), K.bank[1][:, 0:TT * 48], ACT.Copy).then_inc(bank_free, 1)


def nsa_attend(nc, K, gp, qT, kT, v, gate, kcT, vc, y):
    UNITS = [(a, i) for a in range(2) for i in range(TT)]
    U = len(UNITS)
    with ExitStack() as mem:
        sb = lambda n, s: mem.enter_context(nc.sbuf_tensor(f"at{gp}_{n}", s, F32))
        bias = sb("bias", [P, 8, S])
        wbias = sb("wbias", [P, 8, 3 * P])
        pair = sb("pair", [P, 2, S + 3 * P])
        far = sb("far", [P, P])
        seen = sb("seen", [P, 1])
        q = sb("q", [P, S])
        logit = sb("logit", [P, 2, 2 * S])
        prob = sb("prob", [P, 2, 2 * S])
        probT = sb("probT", [P, 2, 2 * S])
        stat = sb("stat", [P, 2, 4, 3])
        CB = 896
        with stage(nc, "loaded", "masked", "prepared", "staged", "scored", "biased", "exped", "weighted", "turned", "copied",
                   "valued", "kept", "vec_step", "paired", "opened") as (
                block, (loaded, masked, prepared, staged, scored, biased, exped, weighted, turned, copied, valued, kept, vec_step,
                        paired, opened)):
            def shape(i):
                n = (i + 1) * P
                return n, min(n, 3 * P), 7 + 8 * i

            @block.sync
            def _(sp):
                src = bass.AP(K.bias_rows.tensor, gp * 8 * GW, [[1, P], [GW, 8], [1, S]])
                sp.dma_start(bias[:, :, :], src).then_inc(loaded, 16)

            @block.gpsimd
            def _(pool):
                nc.gpsimd.memset(far[:, :], 0.0).then_inc(masked, 1)
                nc.gpsimd.memset(seen[:, :], 1.0).then_inc(masked, 1)
                pool.wait_ge(masked, 2)
                nc.gpsimd.affine_select(out=far[:, :], in_=far[:, :], compare_op=ALU.is_gt, fill=NEG, base=1 - P,
                                        pattern=[[1, P]], channel_multiplier=1).then_inc(masked, 1)
                nc.gpsimd.affine_select(out=seen[:, :], in_=seen[:, :], compare_op=ALU.is_ge, fill=0.0,
                                        base=(P - 1) - (2 * 16 - 1), pattern=[[0, 1]], channel_multiplier=-1).then_inc(masked, 1)
                pool.wait_ge(prepared, 2)
                with pool.Fori(0, 4) as it:
                    for a in range(2):
                        pool.wait_ge(biased, it * U + TT * (a + 1))
                        nc.gpsimd.tensor_copy(pair[:, a, 0:S], bias[:, ds(it + a * 4, 1), :].rearrange("p o n -> p (o n)"))
                        nc.gpsimd.tensor_copy(pair[:, a, S:], wbias[:, ds(it + a * 4, 1), :].rearrange("p o n -> p (o n)")).then_inc(paired, 1)

            @block.tensor
            def _(pe):
                pe.wait_ge(prepared, 2)
                with pe.Fori(0, 4) as it:
                    pe.wait_ge(staged, it + 1)
                    for step in range(U + 2):
                        if step < U:
                            u = step
                            a, i = UNITS[u]
                            n, nw, ncmp = shape(i)
                            rows = slice(a * HD, (a + 1) * HD)
                            b0, b1 = K.bank[2 * (u % 2)], K.bank[2 * (u % 2) + 1]
                            if u >= 2:
                                pe.wait_ge(biased, (it + 1) * U + u - 1)
                            qs = q[rows, i * P:(i + 1) * P]
                            nc.tensor.matmul(b0[:, 0:n], qs, kT[rows, gp, 0:n], start=True, stop=True)
                            nc.tensor.matmul(b1[:, 0:nw], qs, kT[rows, 2 + gp, n - nw:n], start=True, stop=True)
                            nc.tensor.matmul(b1[:, CB - S:CB - S + ncmp], qs, kcT[rows, gp, 0:ncmp], start=True, stop=True).then_inc(scored, 1)
                        if 1 <= step <= U:
                            u = step - 1
                            a, i = UNITS[u]
                            n, nw, ncmp = shape(i)
                            pr = prob[:, u % 2, :]
                            pe.wait_ge(weighted, it * U + u + 1)
                            if u >= 1:
                                pe.wait_ge(copied, it * U + u)
                            for j in range(n // P):
                                nc.tensor.transpose(K.bank[4][:, j * P:(j + 1) * P], pr[:, j * P:(j + 1) * P], K.ident[:, :])
                            for j in range(nw // P):
                                nc.tensor.transpose(K.bank[5][:, j * P:(j + 1) * P], pr[:, S + j * P:S + (j + 1) * P], K.ident[:, :])
                            nc.tensor.transpose(K.bank[5][0:ncmp, 3 * P:S], pr[:, CB:CB + ncmp], K.ident[:, :]).then_inc(turned, 1)
                        if step >= 2:
                            u = step - 2
                            a, i = UNITS[u]
                            n, nw, ncmp = shape(i)
                            rows = slice(a * HD, (a + 1) * HD)
                            g = 2 * gp + a
                            pt = probT[:, u % 2, :]
                            pe.wait_ge(copied, it * U + u + 1)
                            if u == 0:
                                pe.wait_ge(kept, it + 1)
                            o = K.bank[6][rows, i * P:(i + 1) * P]
                            for j in range(n // P):
                                nc.tensor.matmul(o, v[:, j, g * HD:(g + 1) * HD], pt[:, j * P:(j + 1) * P], start=(j == 0), stop=False)
                            for j in range(nw // P):
                                nc.tensor.matmul(o, v[:, (n - nw) // P + j, CW + g * HD:CW + (g + 1) * HD],
                                                 pt[:, S + j * P:S + (j + 1) * P], start=False, stop=False)
                            nc.tensor.matmul(o, vc[0:ncmp, a, gp, :], pt[0:ncmp, S + 3 * P:2 * S], start=False, stop=True).then_inc(valued, 1)

            @block.vector
            def _(dve):
                dve.wait_ge(loaded, 16)
                dve.wait_ge(masked, 4)
                nc.vector.tensor_copy(wbias[:, :, :], bias[:, :, P:S]).then_inc(prepared, 1)
                dve.wait_ge(prepared, 1)
                nc.vector.tensor_tensor(wbias[:, :, 0:P], bias[:, :, P:2 * P], far[:, :].unsqueeze(1).broadcast_to([P, 8, P]), ALU.add).then_inc(prepared, 1)
                dve.wait_ge(prepared, 2)
                dve.sem_inc(biased, U)
                PER = U * 4 + 1
                with dve.Fori(0, 4) as it:
                    done = Settle(dve, vec_step, it * PER)
                    for step in range(U + 1):
                        if step < U:
                            u = step
                            a, i = UNITS[u]
                            n, nw, ncmp = shape(i)
                            b0, b1 = K.bank[2 * (u % 2)], K.bank[2 * (u % 2) + 1]
                            lg, st = logit[:, u % 2, :], stat[:, u % 2]
                            dve.wait_ge(scored, it * U + u + 1)
                            if i == 0:
                                dve.wait_ge(paired, it * 2 + a + 1)
                            dve.sem_inc(opened, 1)
                            cc = 415 - P * i
                            for k, (dst, src, bb) in enumerate((
                                    (lg[:, 0:n], b0[:, 0:n], pair[:, a, S - n:S]),
                                    (lg[:, S:S + nw], b1[:, 0:nw], pair[:, a, S + 3 * P - nw:S + 3 * P]),
                                    (lg[:, CB:CB + ncmp], b1[:, CB - S:CB - S + ncmp], pair[:, a, cc:cc + 16 * (ncmp - 1) + 1:16]))):
                                ins = nc.vector.tensor_tensor_reduce(out=dst, in0=src, in1=bb, scale=1.0, scalar=-3e38,
                                                                     op0=ALU.add, op1=ALU.max, accum_out=st[:, 0, k:k + 1])
                            done(ins)
                            nc.vector.tensor_scalar(st[:, 1, :], st[:, 0, :], -1.0, None, ALU.mult).then_inc(biased, 1)
                        if step >= 1:
                            u = step - 1
                            a, i = UNITS[u]
                            n, nw, ncmp = shape(i)
                            pr, st = prob[:, u % 2, :], stat[:, u % 2]
                            dve.wait_ge(exped, it * U + u + 1)
                            done(nc.vector.reciprocal(st[:, 2, :], st[:, 2, :]))
                            gcol = gate[:, i, :].rearrange("p (b h) -> p b h", b=3)[:, :, ds(it + (2 * gp + a) * 4, 1)]
                            done(nc.vector.tensor_tensor(st[:, 3, :], st[:, 2, :], gcol.rearrange("p b o -> p (b o)"), ALU.mult))
                            if i == 0:
                                nc.vector.tensor_tensor(st[:, 3, 0:1], st[:, 3, 0:1], seen[:, :], ALU.mult).then_inc(vec_step, 1)
                            else:
                                dve.sem_inc(vec_step, 1)
                            done.n += 1
                            dve.wait_ge(vec_step, done.base + done.n)
                            nc.vector.tensor_scalar(pr[:, 0:n], pr[:, 0:n], st[:, 3, 1:2], None, ALU.mult)
                            nc.vector.tensor_scalar(pr[:, S:S + nw], pr[:, S:S + nw], st[:, 3, 2:3], None, ALU.mult)
                            nc.vector.tensor_scalar(pr[:, CB:CB + ncmp], pr[:, CB:CB + ncmp], st[:, 3, 0:1], None, ALU.mult).then_inc(weighted, 1)
                    dve.sem_inc(vec_step, 1)
                    done.n += 1
                    assert done.n == PER

            @block.scalar
            def _(act):
                act.sem_inc(kept, 1)
                with act.Fori(0, 4) as it:
                    nc.scalar.activation(backwards(q[:, :].rearrange("p (t n) -> p t n", t=TT)),
                                         qT[:, ds(it + gp * 4, 1), :].rearrange("p o (t n) -> p (o t) n", t=TT), ACT.Copy).then_inc(staged, 1)
                    for step in range(U + 1):
                        if step < U:
                            u = step
                            a, i = UNITS[u]
                            n, nw, ncmp = shape(i)
                            lg, pr, st = logit[:, u % 2, :], prob[:, u % 2, :], stat[:, u % 2]
                            act.wait_ge(biased, (it + 1) * U + u + 1)
                            if u >= 2:
                                act.wait_ge(turned, it * U + u - 1)
                            nc.scalar.activation(pr[:, 0:n], lg[:, 0:n], ACT.Exp, bias=st[:, 1, 0:1], accum_out=st[:, 2, 1:2])
                            nc.scalar.activation(pr[:, S:S + nw], lg[:, S:S + nw], ACT.Exp, bias=st[:, 1, 1:2], accum_out=st[:, 2, 2:3])
                            nc.scalar.activation(pr[:, CB:CB + ncmp], lg[:, CB:CB + ncmp], ACT.Exp, bias=st[:, 1, 2:3],
                                                 accum_out=st[:, 2, 0:1]).then_inc(exped, 1)
                        if step >= 1:
                            u = step - 1
                            a, i = UNITS[u]
                            n, nw, ncmp = shape(i)
                            pt = probT[:, u % 2, :]
                            act.wait_ge(turned, it * U + u + 1)
                            if u >= 2:
                                act.wait_ge(valued, it * U + u - 1)
                            nc.scalar.activation(pt[:, 0:n], K.bank[4][:, 0:n], ACT.Copy)
                            nc.scalar.activation(pt[:, S:S + nw], K.bank[5][:, 0:nw], ACT.Copy)
                            nc.scalar.activation(pt[0:ncmp, S + 3 * P:2 * S], K.bank[5][0:ncmp, 3 * P:S], ACT.Copy).then_inc(copied, 1)
                    act.wait_ge(valued, it * U + U)
                    nc.scalar.activation(y[:, ds(it + gp * 4, 1), :].rearrange("p o (t n) -> p (o t) n", t=TT),
                                         backwards(K.bank[6][:, :].rearrange("p (t n) -> p t n", t=TT)), ACT.Copy).then_inc(kept, 1)


GH, GC = 4, 32
DV = 256
NC = S // GC
PER_TILE = P // GC


def chunk_mask():
    i = np.arange(P)
    return ((i[:, None] // GC == i[None, :] // GC) & (i[:, None] <= i[None, :])).astype(np.float32)


def gla(nc, K, A, y):
    w = A.w_in[0].rearrange("(k p) m -> p k m", p=P)
    mask_dram = nc.inline_tensor(chunk_mask(), name="gla_chunk_mask").ap()
    with ExitStack() as mem:
        sb = lambda n, s: mem.enter_context(nc.sbuf_tensor(f"gla_{n}", s, F32))
        vog = sb("vog", [P, TT, 2 * D])
        qt, kt = sb("qt", [P, GH, S]), sb("kt", [P, GH, S])
        ke = sb("ke", [P, GH, S])
        decay = sb("decay", [P, GH, NC])
        gla_keys(nc, K, A, w, qt, kt, ke, decay)
        project_tokens(nc, K, w, KD, K.hT, 8, lambda c: c * CW + C_GLA_V,
                       lambda bank, t, c: nc.vector.tensor_copy(vog[:, t, ds(c * CW, CW)], bank))
        mask = sb("mask", [P, P])
        attm = sb("attm", [P, 2, GH, P])
        keT = sb("keT", [P, 2, GH, P])
        state = sb("state", [P, 2, GH, DV])
        o = sb("o", [P, TT, D])
        ss = sb("ss", [P, 2, TT, GH])
        junk = sb("junk", [P, DV])
        with stage(nc, "loaded", "zeroed", "attended", "masked", "turned", "copied", "outer", "updated", "inter", "squared",
                   "kept", "gated", "vec_step", "rooted") as (
                block, (loaded, zeroed, attended, masked, turned, copied, outer, updated, inter, squared, kept, gated, vec_step, rooted)):
            @block.sync
            def _(sp):
                sp.dma_start(mask[:, :], mask_dram).then_inc(loaded, 16)

            @block.tensor
            def _(pe):
                for t in range(TT):
                    toks = slice(t * P, (t + 1) * P)
                    if t:
                        pe.wait_ge(masked, t)
                    for h in range(GH):
                        last = nc.tensor.matmul(K.bank[0][:, h * P:(h + 1) * P], kt[:, h, toks], qt[:, h, toks], start=True, stop=True)
                    last.then_inc(attended, 1)
                    if t:
                        pe.wait_ge(copied, t)
                    for h in range(GH):
                        last = nc.tensor.transpose(K.bank[1][:, h * P:(h + 1) * P], ke[:, h, toks], K.ident[:, :])
                    last.then_inc(turned, 1)
                    pe.wait_ge(masked, t + 1)
                    if t:
                        pe.wait_ge(kept, t)
                    for h in range(GH):
                        nc.tensor.matmul(K.bank[2 + h // 2][:, (h % 2) * DV:(h % 2 + 1) * DV], attm[:, t % 2, h, :],
                                         vog[:, t, h * DV:(h + 1) * DV], start=(h % 2 == 0), stop=False, skip_group_check=True)
                    pe.wait_ge(copied, t + 1)
                    for j in range(PER_TILE):
                        n = t * PER_TILE + j
                        rows = slice(j * GC, (j + 1) * GC)
                        if n:
                            pe.wait_ge(updated, n)
                        for h in range(GH):
                            last = nc.tensor.matmul(K.bank[4 + h // 2][:, (h % 2) * DV:(h % 2 + 1) * DV], keT[rows, t % 2, h, :],
                                                    vog[rows, t, h * DV:(h + 1) * DV], start=True, stop=True)
                        last.then_inc(outer, 1)
                        if n:
                            for h in range(GH):
                                last = nc.tensor.matmul(K.bank[2 + h // 2][rows, (h % 2) * DV:(h % 2 + 1) * DV],
                                                        qt[:, h, n * GC:(n + 1) * GC], state[:, n % 2, h, :],
                                                        start=False, stop=(j == PER_TILE - 1), skip_group_check=True)
                            last.then_inc(inter, 1)

            @block.vector
            def _(dve):
                done = Settle(dve, vec_step)
                dve.wait_ge(loaded, 16)
                nc.vector.memset(state[:, 0], 0.0).then_inc(zeroed, 1)
                dve.wait_ge(zeroed, 1)
                for t in range(TT):
                    dve.wait_ge(attended, t + 1)
                    nc.vector.tensor_tensor(attm[:, t % 2], K.bank[0][:, :].rearrange("p (h c) -> p h c", h=GH),
                                            mask[:, :].unsqueeze(1).broadcast_to([P, GH, P]), ALU.mult).then_inc(masked, 1)
                    for j in range(PER_TILE):
                        n = t * PER_TILE + j
                        dve.wait_ge(outer, n + 1)
                        if n:
                            dve.wait_ge(updated, n)
                        if n >= 2:
                            dve.wait_ge(inter, n - 1)
                        for h in range(GH):
                            last = nc.vector.scalar_tensor_tensor(out=state[:, (n + 1) % 2, h, :], in0=state[:, n % 2, h, :],
                                                                  scalar=decay[:, h, n:n + 1],
                                                                  in1=K.bank[4 + h // 2][:, (h % 2) * DV:(h % 2 + 1) * DV],
                                                                  op0=ALU.mult, op1=ALU.add)
                        last.then_inc(updated, 1)
                    dve.wait_ge(inter, t * PER_TILE + PER_TILE - 1)
                    for b in range(2):
                        last = nc.vector.tensor_copy(o[:, t, b * 2 * DV:(b + 1) * 2 * DV], K.bank[2 + b][:, :])
                    last.then_inc(kept, 1)
                dve.wait_ge(squared, TT * GH)
                done(nc.vector.tensor_scalar(ss[:, 1], ss[:, 0], 1.0 / DV, EPS, ALU.mult, ALU.add))
                dve.wait_ge(rooted, 1)
                done(nc.vector.reciprocal(ss[:, 1], ss[:, 0]))
                dve.wait_ge(gated, 1)
                dve.wait_ge(kept, TT)
                for t in range(TT):
                    for h in range(GH):
                        cols = slice(h * DV, (h + 1) * DV)
                        nc.vector.scalar_tensor_tensor(out=o[:, t, cols], in0=o[:, t, cols], scalar=ss[:, 1, t, h:h + 1],
                                                       in1=vog[:, t, h * DV + D:h * DV + D + DV], op0=ALU.mult, op1=ALU.mult)

            @block.scalar
            def _(act):
                nc.scalar.activation(vog[:, :, D:2 * D], vog[:, :, D:2 * D], ACT.Silu).then_inc(gated, 1)
                for t in range(TT):
                    act.wait_ge(turned, t + 1)
                    nc.scalar.activation(keT[:, t % 2].rearrange("p h d -> p (h d)"), K.bank[1][:, :], ACT.Copy).then_inc(copied, 1)
                    act.wait_ge(kept, t + 1)
                    for h in range(GH):
                        if t + h:
                            act.wait_ge(squared, t * GH + h)
                        nc.scalar.activation(junk[:, :], o[:, t, h * DV:(h + 1) * DV], ACT.Square,
                                             accum_out=ss[:, 0, t, h:h + 1]).then_inc(squared, 1)
                act.wait_ge(vec_step, 1)
                nc.scalar.activation(ss[:, 0], ss[:, 1], ACT.Sqrt).then_inc(rooted, 1)
        to_channels(nc, K, o, y, KD, lambda k: vcol(K, "gla_norm", k % 2))


def gla_keys(nc, K, A, w, qt, kt, ke, decay):
    with ExitStack() as mem:
        sb = lambda n, s: mem.enter_context(nc.sbuf_tensor(f"glak_{n}", s, F32))
        qk = sb("qk", [P, 2 * GH, S])
        project_channels(nc, K, w, KD, K.hT, 4, lambda c: c * CW + C_GLA_Q,
                         lambda bank, m: nc.scalar.activation(qk[:, ds(m, 1), :], bank, ACT.Copy))
        wlr, lr, wa2 = sb("wlr", [P, KD, 16]), sb("lr", [16, S]), sb("wa2", [16, GH * P])
        b, e, la, keep = (sb(n, [P, GH, S]) for n in ("b", "e", "la", "keep"))
        with stage(nc, "loaded", "set", "lr_ready", "lr_kept", "products", "act_step", "logged", "vec_step", "summed", "exped", "used") as (
                block, (loaded, is_set, lr_ready, lr_kept, products, act_step, logged, vec_step, summed, exped, used)):
            @block.sync
            def _(sp):
                sp.dma_start(wlr[:, :, :], w[:, :, C_GLA_LR:C_GLA_LR + 16]).then_inc(loaded, 16)
                sp.dma_start(wa2[:, :], A.gla_wa2[0]).then_inc(loaded, 16)

            @block.gpsimd
            def _(pool):
                nc.gpsimd.memset(keep[:, 0, :], 1.0).then_inc(is_set, 1)
                pool.wait_ge(is_set, 1)
                nc.gpsimd.memset(keep[:, 0, 0:S:GC], 0.0).then_inc(is_set, 1)

            @block.tensor
            def _(pe):
                pe.wait_ge(loaded, 32)
                for k in range(KD):
                    last = nc.tensor.matmul(K.bank[4][0:16, :], wlr[:, k, :], K.hT[:, k, :], start=(k == 0), stop=(k == KD - 1))
                last.then_inc(lr_ready, 1)
                pe.wait_ge(lr_kept, 1)
                for h in range(GH):
                    nc.tensor.matmul(K.bank[h][:, :], wa2[:, h * P:(h + 1) * P], lr[:, :], start=True, stop=True).then_inc(products, 1)

            @block.scalar
            def _(act):
                done = Settle(act, act_step)
                act.wait_ge(lr_ready, 1)
                nc.scalar.activation(lr[:, :], K.bank[4][0:16, :], ACT.Copy).then_inc(lr_kept, 1)
                for h in range(GH):
                    act.wait_ge(products, h + 1)
                    done(nc.scalar.activation(e[:, h, :], K.bank[h][:, :], ACT.Abs, bias=vcol(K, "gla_ba", h)))
                done(nc.scalar.activation(e[:, :, :], e[:, :, :], ACT.Exp, scale=-1.0))
                nc.scalar.activation(e[:, :, :], e[:, :, :], ACT.Ln, bias=1.0).then_inc(logged, 1)
                act.wait_ge(summed, 1)
                nc.scalar.activation(decay[:, :, :], b[:, :, GC - 1:S:GC], ACT.Exp, scale=1 / 16.0).then_inc(exped, 1)
                nc.scalar.activation(e[:, :, :], b[:, :, :], ACT.Exp, scale=1 / 16.0).then_inc(exped, 1)
                act.wait_ge(used, 1)
                nc.scalar.activation(e[:, :, :], b[:, :, :], ACT.Exp, scale=-1 / 16.0).then_inc(exped, 1)
                act.wait_ge(used, 2)
                nc.scalar.activation(e[:, :, :], la[:, :, :], ACT.Exp, scale=1 / 16.0).then_inc(exped, 1)

            @block.vector
            def _(dve):
                done = Settle(dve, vec_step)
                for h in range(GH):
                    dve.wait_ge(act_step, h + 1)
                    done(nc.vector.tensor_scalar(la[:, h, :], K.bank[h][:, :], vcol(K, "gla_ba", h), 0.0, ALU.add, ALU.min))
                dve.wait_ge(logged, 1)
                done(nc.vector.tensor_tensor(la[:, :, :], la[:, :, :], e[:, :, :], ALU.subtract))
                dve.wait_ge(is_set, 2)
                for h in range(GH):
                    done(nc.vector.tensor_tensor_scan(b[:, h, :], keep[:, 0, :], la[:, h, :], 0.0, ALU.mult, ALU.add))
                chunks = lambda x: x[:, :, :].rearrange("p h (n c) -> p (h n) c", c=GC)
                nc.vector.tensor_tensor(chunks(la), chunks(b)[:, :, GC - 1:GC].broadcast_to([P, GH * NC, GC]), chunks(b), ALU.subtract).then_inc(summed, 1)
                dve.wait_ge(exped, 2)
                nc.vector.scalar_tensor_tensor(out=qt[:, :, :], in0=qk[:, 0:GH, :], scalar=float(P) ** -0.5, in1=e[:, :, :],
                                               op0=ALU.mult, op1=ALU.mult).then_inc(used, 1)
                dve.wait_ge(exped, 3)
                nc.vector.tensor_tensor(kt[:, :, :], qk[:, GH:, :], e[:, :, :], ALU.mult).then_inc(used, 1)
                dve.wait_ge(exped, 4)
                nc.vector.tensor_tensor(ke[:, :, :], qk[:, GH:, :], e[:, :, :], ALU.mult).then_inc(used, 1)


def gated(nc, K, tiles, load, n_loads, rhs_gate, rhs_value, func, combine, n_combine):
    with ExitStack() as mem:
        ring = mem.enter_context(nc.sbuf_tensor(f"ring_{nc.next_id()}", [P, 2, 2, KD, P], F32))
        act_out = mem.enter_context(nc.sbuf_tensor(f"gate_{nc.next_id()}", [P, 2, S], F32))
        with stage(nc, "w_loaded0", "w_loaded1", "products", "acted", "combined", "vec_step") as (
                block, (w0, w1, products, acted, combined, vec_step)):
            w_loaded = [w0, w1]

            @block.sync
            def _(sp):
                for s in range(2):
                    load(sp, ring[:, s], s, w_loaded[s])
                with sp.Fori(1, tiles // 2) as i:
                    for s in range(2):
                        sp.wait_ge(products, (i * 2 + s - 1) * 2)
                        load(sp, ring[:, s], i * 2 + s, w_loaded[s])

            @block.tensor
            def _(pe):
                pe.sem_inc(combined, 2)
                with pe.Fori(0, tiles // 2) as i:
                    for s in range(2):
                        pe.wait_ge(w_loaded[s], (i + 1) * (16 * n_loads))
                        pe.wait_ge(combined, i * 2 + s + 1)
                        for side, rhs in enumerate((rhs_gate, rhs_value)):
                            for k in range(KD):
                                last = nc.tensor.matmul(K.bank[2 * s + side][:, :], ring[:, s, side, k, :], rhs[:, k, :],
                                                        start=(k == 0), stop=(k == KD - 1))
                            last.then_inc(products, 1)

            @block.scalar
            def _(act):
                with act.Fori(0, tiles // 2) as i:
                    for s in range(2):
                        act.wait_ge(products, (i * 2 + s) * 2 + 1)
                        act.wait_ge(combined, i * 2 + s + 1)
                        nc.scalar.activation(act_out[:, s, :], K.bank[2 * s][:, :], func).then_inc(acted, 1)

            @block.vector
            def _(dve):
                with dve.Fori(0, tiles // 2) as i:
                    done = Settle(dve, vec_step, i * (2 * n_combine))
                    for s in range(2):
                        dve.wait_ge(acted, i * 2 + s + 1)
                        dve.wait_ge(products, (i * 2 + s) * 2 + 2)
                        combine(done, i * 2 + s, act_out[:, s, :], K.bank[2 * s + 1][:, :])
                        dve.sem_inc(combined, 1)
                    assert done.n == 2 * n_combine


def broadcast_row(ap):
    return bass.AP(ap.tensor, ap.offset, [[0, P], [1, int(np.prod(ap.shape))]])


def residual_norm(nc, K, o, g_row):
    rms_scale(nc, K, o, o)
    with ExitStack() as mem:
        g = mem.enter_context(nc.sbuf_tensor(f"g_{nc.next_id()}", [P, D], F32))
        with stage(nc, "loaded", "scaled", "added") as (block, (loaded, scaled, added)):
            @block.sync
            def _(sp):
                sp.dma_start(g[:, :], broadcast_row(g_row)).then_inc(loaded, 16)

            @block.vector
            def _(dve):
                dve.wait_ge(loaded, 16)
                for t in range(TT):
                    nc.vector.tensor_tensor(o[:, t, :], o[:, t, :], g[:, :], ALU.mult).then_inc(scaled, 1)
                for t in range(TT):
                    dve.wait_ge(scaled, t + 1)
                    nc.vector.tensor_tensor(K.x[:, t, :], K.x[:, t, :], o[:, t, :], ALU.add).then_inc(added, 1)


def merge(nc, K, A, y, merged):
    w_gate = A.w_in[0].rearrange("(k p) m -> p k m", p=P)
    with nc.sbuf_tensor("merge_term", [P, S], F32) as term:
        for b in range(3):
            def load(sp, weights, m, sem):
                sp.dma_start(weights[:, 0], w_gate[:, :, ds(m * P + (C_MERGE + b * D), P)]).then_inc(sem, 16)
                if b != 1:
                    sp.dma_start(weights[:, 1], A.w_branch[0, b].rearrange("(k p) m -> p k m", p=P)[:, :, ds(m * P, P)]).then_inc(sem, 16)
                    return
                src = A.w_branch[0, b].rearrange("(gp a r d) m -> gp a d r m", gp=2, a=2, r=4)
                for gp in range(2):
                    for a in range(2):
                        sp.dma_start(weights[a * HD:(a + 1) * HD, 1, gp * 4:gp * 4 + 4, :], src[gp, a][:, :, ds(m * P, P)]).then_inc(sem, 16)

            def combine(done, m, gate, value):
                if b == 0:
                    done(nc.vector.tensor_tensor(merged[:, ds(m, 1), :].rearrange("p o n -> p (o n)"), gate, value, ALU.mult))
                    return
                row = merged[:, ds(m, 1), :].rearrange("p o n -> p (o n)")
                done(nc.vector.tensor_tensor(term[:, :], gate, value, ALU.mult))
                done(nc.vector.tensor_tensor(row, row, term[:, :], ALU.add))

            gated(nc, K, KD, load, 5 if b == 1 else 2, K.hT, y[b], ACT.Sigmoid, combine, 1 if b == 0 else 2)


def ffn(nc, K, A, o):
    w = A.w_ffn_in[0].rearrange("(k p) m -> p k m", p=P)
    with nc.sbuf_tensor("ffn_hidden", [P, KF, S], F32) as hidden:
        def load(sp, weights, m, sem):
            for side in range(2):
                sp.dma_start(weights[:, side], w[:, :, ds(m * P + side * D_FF, P)]).then_inc(sem, 16)

        gated(nc, K, KF, load, 2, K.hT, K.hT, ACT.Silu,
              lambda done, m, gate, value: done(nc.vector.tensor_tensor(hidden[:, ds(m, 1), :].rearrange("p o n -> p (o n)"), gate, value, ALU.mult)), 1)
        project_tokens(nc, K, A.w_ffn_out[0].rearrange("(k p) m -> p k m", p=P), KF, hidden, 4, lambda c: c * CW,
                       lambda bank, t, c: nc.vector.tensor_copy(o[:, t, ds(c * CW, CW)], bank))


ALPHA = 4 ** 0.25
LN_EPS = 1e-5
SI = 2048
SG, SE, SP, SN = 4, 8, 64, 128
SH = SG * SE


def layer_norm(nc, K, mix, g_row, b_row):
    with ExitStack() as mem:
        sb = lambda n, s: mem.enter_context(nc.sbuf_tensor(f"ln_{n}_{nc.next_id()}", s, F32))
        g, b = sb("g", [P, D]), sb("b", [P, D])
        parts, stat = sb("parts", [P, TT, 2, 6]), sb("stat", [P, TT, 2])
        std, rstd = sb("std", [P, TT]), sb("rstd", [P, TT])
        with stage(nc, "loaded", "vec_step", "varied", "rooted") as (block, (loaded, vec_step, varied, rooted)):
            @block.sync
            def _(sp):
                sp.dma_start(g[:, :], broadcast_row(g_row)).then_inc(loaded, 16)
                sp.dma_start(b[:, :], broadcast_row(b_row)).then_inc(loaded, 16)

            @block.scalar
            def _(act):
                act.wait_ge(varied, 1)
                nc.scalar.activation(std[:, :], rstd[:, :], ACT.Sqrt).then_inc(rooted, 1)

            @block.vector
            def _(dve):
                done = Settle(dve, vec_step)
                for t in range(TT):
                    last = nc.vector.scalar_tensor_tensor(out=mix[:, t, :], in0=K.x[:, t, :], scalar=ALPHA, in1=mix[:, t, :],
                                                          op0=ALU.mult, op1=ALU.add)
                done(last)
                for t in range(TT):
                    for h in range(2):
                        last = nc.vector.bn_stats(parts[:, t, h, :], mix[:, t, h * 512:(h + 1) * 512])
                done(last)
                for t in range(TT):
                    last = nc.vector.bn_aggr(stat[:, t, :], parts[:, t, :, :].rearrange("p h s -> p (h s)"))
                done(last)
                nc.vector.tensor_scalar(rstd[:, :], stat[:, :, 1], LN_EPS, None, ALU.add).then_inc(varied, 1)
                dve.wait_ge(rooted, 1)
                done(nc.vector.reciprocal(rstd[:, :], std[:, :]))
                for t in range(TT):
                    last = nc.vector.tensor_scalar(mix[:, t, :], mix[:, t, :], stat[:, t, 0:1], rstd[:, t:t + 1], ALU.subtract, ALU.mult)
                done(last)
                dve.wait_ge(loaded, 32)
                for t in range(TT):
                    last = nc.vector.tensor_tensor(mix[:, t, :], mix[:, t, :], g[:, :], ALU.mult)
                done(last)
                for t in range(TT):
                    last = nc.vector.tensor_tensor(K.x[:, t, :], mix[:, t, :], b[:, :], ALU.add)
                done(last)


def ssd_steps(nc, K, A, w, rows):
    csT = K.csT
    with ExitStack() as mem:
        sb = lambda n, s: mem.enter_context(nc.sbuf_tensor(f"dt_{n}", s, F32))
        wdt, vec = sb("w", [P, KD, SH]), sb("vec", [SH, 4])
        e, dt, ecs, keep = (sb(n, [SH, S]) for n in ("e", "dt", "ecs", "keep"))
        with stage(nc, "loaded", "product", "act_step", "vec_step", "turned", "copied", "stepped", "summed", "exped") as (
                block, (loaded, product, act_step, vec_step, turned, copied, stepped, summed, exped)):
            @block.sync
            def _(sp):
                sp.dma_start(wdt[:, :, :], w[:, :, SI + 3072:SI + 3072 + SH]).then_inc(loaded, 16)
                sp.dma_start(vec[:, 0:1], A.ssd_dt_bias_2.rearrange("a h -> h a")).then_inc(loaded, 16)
                sp.dma_start(vec[:, 1:2], A.ssd_a_log_2.rearrange("a h -> h a")).then_inc(loaded, 16)

            @block.tensor
            def _(pe):
                pe.wait_ge(loaded, 48)
                for k in range(KD):
                    last = nc.tensor.matmul(K.bank[0][0:SH, :], wdt[:, k, :], K.hT[:, k, :], start=(k == 0), stop=(k == KD - 1))
                last.then_inc(product, 1)
                pe.wait_ge(stepped, 1)
                for n, src in enumerate((csT, dt, e, ecs)):
                    for t in range(TT):
                        c = (n * TT + t) * SH
                        last = nc.tensor.transpose(K.bank[1][:, c:c + SH], src[:, t * P:(t + 1) * P], K.ident[0:SH, 0:SH])
                last.then_inc(turned, 1)

            @block.scalar
            def _(act):
                done = Settle(act, act_step)
                act.wait_ge(product, 1)
                done(nc.scalar.activation(e[:, :], K.bank[0][0:SH, :], ACT.Abs, bias=vec[:, 0:1]))
                done(nc.scalar.activation(e[:, :], e[:, :], ACT.Exp, scale=-1.0))
                done(nc.scalar.activation(e[:, :], e[:, :], ACT.Ln, bias=1.0))
                done(nc.scalar.activation(vec[:, 2:3], vec[:, 1:2], ACT.Exp))
                act.wait_ge(summed, 1)
                nc.scalar.activation(ecs[:, :], csT[:, :], ACT.Exp).then_inc(exped, 1)
                nc.scalar.activation(e[:, :], e[:, :], ACT.Exp).then_inc(exped, 1)
                act.wait_ge(turned, 1)
                nc.scalar.activation(rows[:, :, :, :].rearrange("p n t h -> p (n t h)"), K.bank[1][:, :], ACT.Copy).then_inc(copied, 1)

            @block.vector
            def _(dve):
                done = Settle(dve, vec_step)
                done(nc.vector.memset(keep[:, :], 1.0))
                done(nc.vector.memset(keep[:, 0:S:P], 0.0))
                dve.wait_ge(act_step, 4)
                done(nc.vector.tensor_scalar(dt[:, :], K.bank[0][0:SH, :], vec[:, 0:1], 0.0, ALU.add, ALU.max))
                done(nc.vector.tensor_tensor(dt[:, :], dt[:, :], e[:, :], ALU.add))
                done(nc.vector.tensor_scalar(ecs[:, :], dt[:, :], vec[:, 2:3], -1.0, ALU.mult, ALU.mult))
                done(nc.vector.tensor_tensor_scan(csT[:, :], keep[:, :], ecs[:, :], 0.0, ALU.mult, ALU.add))
                chunks = lambda x: x[:, :].rearrange("h (n c) -> h n c", c=P)
                nc.vector.tensor_tensor(chunks(e), chunks(csT)[:, :, P - 1:P].broadcast_to([SH, TT, P]), chunks(csT), ALU.subtract).then_inc(summed, 1)
                dve.wait_ge(exped, 2)
                nc.vector.tensor_tensor(e[:, :], e[:, :], dt[:, :], ALU.mult).then_inc(stepped, 1)


def ssd_conv(nc, K, xbc, pad):
    n_tiles = xbc.shape[1]
    with nc.sbuf_tensor("conv_acc", [P, 2, S], F32) as acc:
        with stage(nc, "zeroed", "vec_step", "convolved", "acted") as (block, (zeroed, vec_step, convolved, acted)):
            @block.vector
            def _(dve):
                done = Settle(dve, vec_step)
                done(nc.vector.memset(xbc[:, :, 0:pad], 0.0))
                for n in range(n_tiles):
                    a = acc[:, n % 2, :]
                    if n >= 2:
                        dve.wait_ge(acted, n - 1)
                    done(nc.vector.tensor_scalar(a, xbc[:, n, 0:S], vcol(K, "ssd_conv_w", n), vcol(K, "ssd_conv_b", n), ALU.mult, ALU.add))
                    for j in range(1, pad + 1):
                        ins = nc.vector.scalar_tensor_tensor(out=a, in0=xbc[:, n, j:j + S], scalar=vcol(K, "ssd_conv_w", j * n_tiles + n),
                                                             in1=a, op0=ALU.mult, op1=ALU.add)
                        if j < pad:
                            done(ins)
                    ins.then_inc(convolved, 1)

            @block.scalar
            def _(act):
                for n in range(n_tiles):
                    act.wait_ge(convolved, n + 1)
                    nc.scalar.activation(xbc[:, n, pad:pad + S], acc[:, n % 2, :], ACT.Silu).then_inc(acted, 1)


def to_tokens(nc, K, src, col, dst, n):
    with stage(nc, "turned", "copied") as (block, (turned, copied)):
        @block.tensor
        def _(pe):
            for k in range(n):
                if k >= 8:
                    pe.wait_ge(copied, k - 7)
                for t in range(TT):
                    last = nc.tensor.transpose(K.bank[k % 8][:, t * P:(t + 1) * P], src(k)[:, t * P:(t + 1) * P], K.ident[:, :])
                last.then_inc(turned, 1)

        @block.scalar
        def _(act):
            for k in range(n):
                act.wait_ge(turned, k + 1)
                nc.scalar.activation(dst[:, :, (col + k) * P:(col + k + 1) * P], K.bank[k % 8][:, :].rearrange("p (t c) -> p t c", t=TT),
                                     ACT.Copy).then_inc(copied, 1)


def ssd(nc, K, A, o):
    PAD = 3
    w = A.ssd_w_in_2[0].rearrange("(k p) m -> p k m", p=P)
    with ExitStack() as mem:
        sb = lambda n, s: mem.enter_context(nc.sbuf_tensor(f"ssd_{n}", s, F32))
        z = sb("z", [P, TT, SI])
        with ExitStack() as inner:
            sb2 = lambda n, s: inner.enter_context(nc.sbuf_tensor(f"ssd_{n}", s, F32))
            xbc = sb2("xbc", [P, 24, S + PAD])
            rows = sb2("rows", [P, 4, TT, SH])
            K.csT = sb2("csT", [SH, S])
            with nc.sbuf_tensor("ssd_xT", [P, KD, S], F32) as xT:
                K.hT = xT
                to_channels(nc, K, K.x, xT, KD)
                project_channels(nc, K, w, KD, xT, 12, lambda c: c * CW + SI,
                                 lambda bank, m: nc.scalar.activation(xbc[:, ds(m, 1), PAD:], bank, ACT.Copy))
                project_tokens(nc, K, w, KD, xT, 8, lambda c: c * CW,
                               lambda bank, t, c: nc.vector.tensor_copy(z[:, t, ds(c * CW, CW)], bank))
                ssd_steps(nc, K, A, w, rows)
            ssd_conv(nc, K, xbc, PAD)
            xtok = sb2("xtok", [P, TT, SI + SG * SN])
            to_tokens(nc, K, lambda k: xbc[:, k, PAD:], 0, xtok, 20)
            ssd_scan(nc, K, A, xbc[:, :, PAD:], xtok, z, rows)
        with nc.sbuf_tensor("ssd_yT", [P, SI // P, S], F32) as yT:
            to_channels(nc, K, z, yT, SI // P, lambda k: vcol(K, "ssd_norm", k))
            project_tokens(nc, K, A.ssd_w_out_2[0].rearrange("(k p) m -> p k m", p=P), SI // P, yT, 4, lambda c: c * CW,
                           lambda bank, t, c: nc.vector.tensor_copy(o[:, t, ds(c * CW, CW)], bank))


def ssd_scan(nc, K, A, xbc, xtok, z, rows):
    UNITS = [(t, g) for t in range(TT) for g in range(SG)]
    GWID = SE * SP
    with ExitStack() as mem:
        sb = lambda n, s: mem.enter_context(nc.sbuf_tensor(f"scan_{n}", s, F32))
        cmask, nmask = sb("cmask", [P, P]), sb("nmask", [P, P])
        dskip = sb("dskip", [P, SH])
        cb = sb("cb", [P, 2, P])
        dec = sb("dec", [P, 2, SE, P])
        last_dec = sb("last", [P, 2, SE])
        xr, xe = sb("xr", [P, 2, GWID]), sb("xe", [P, 2, GWID])
        state = sb("state", [P, SG, GWID])
        off, skip = sb("off", [P, 2, GWID]), sb("skip", [P, 2, GWID])
        ss = sb("ss", [P, 2, TT, SG])
        junk = sb("junk", [P, GWID])
        heads = lambda x: x.rearrange("p (e q) -> p e q", e=SE)
        with stage(nc, "loaded", "masked", "spread", "shifted", "exped", "mixed", "scaled", "produced", "moved", "finished",
                   "vec_step", "pool_step", "gated", "squared", "rooted") as (
                block, (loaded, masked, spread, shifted, exped, mixed, scaled, produced, moved, finished, vec_step, pool_step, gated, squared, rooted)):
            @block.sync
            def _(sp):
                sp.dma_start(dskip[:, :], broadcast_row(A.ssd_d_2[0])).then_inc(loaded, 16)

            @block.gpsimd
            def _(pool):
                nc.gpsimd.memset(cmask[:, :], 1.0).then_inc(masked, 1)
                nc.gpsimd.memset(nmask[:, :], 0.0).then_inc(masked, 1)
                pool.wait_ge(masked, 2)
                nc.gpsimd.affine_select(out=cmask[:, :], in_=cmask[:, :], compare_op=ALU.is_ge, fill=0.0, base=0,
                                        pattern=[[1, P]], channel_multiplier=-1).then_inc(masked, 1)
                nc.gpsimd.affine_select(out=nmask[:, :], in_=nmask[:, :], compare_op=ALU.is_ge, fill=NEG, base=0,
                                        pattern=[[1, P]], channel_multiplier=-1).then_inc(masked, 1)
                for u, (t, g) in enumerate(UNITS):
                    if u >= 2:
                        pool.wait_ge(finished, u - 1)
                    xs = heads(xtok[:, t, g * GWID:(g + 1) * GWID])
                    hs = slice(g * SE, (g + 1) * SE)
                    per_head = lambda r: r.unsqueeze(2).broadcast_to([P, SE, SP])
                    nc.gpsimd.tensor_tensor(heads(xr[:, u % 2, :]), xs, per_head(rows[:, 1, t, hs]), ALU.mult)
                    nc.gpsimd.tensor_tensor(heads(xe[:, u % 2, :]), xs, per_head(rows[:, 2, t, hs]), ALU.mult)
                    if u == 0:
                        pool.wait_ge(loaded, 16)
                    nc.gpsimd.tensor_tensor(heads(skip[:, u % 2, :]), xs, per_head(dskip[:, hs]), ALU.mult).then_inc(scaled, 1)

            @block.tensor
            def _(pe):
                for step in range(len(UNITS) + 1):
                    if step < len(UNITS):
                        u = step
                        t, g = UNITS[u]
                        toks = slice(t * P, (t + 1) * P)
                        if u >= 1:
                            pe.wait_ge(shifted, u)
                            pe.wait_ge(exped, u)
                        for e in range(SE):
                            h = g * SE + e
                            nc.tensor.matmul(K.bank[e // 4][:, (e % 4) * P:(e % 4 + 1) * P], K.ident[0:SH, h:h + 1].broadcast_to([SH, P]),
                                             K.csT[:, toks], start=True, stop=True)
                        nc.tensor.matmul(K.bank[2][:, 0:P], xbc[:, 16 + g, toks], xbc[:, 20 + g, toks], start=True, stop=True).then_inc(spread, 1)
                    if step >= 1:
                        u = step - 1
                        t, g = UNITS[u]
                        toks = slice(t * P, (t + 1) * P)
                        pe.wait_ge(mixed, u + 1)
                        pe.wait_ge(scaled, u + 1)
                        if u >= 1:
                            pe.wait_ge(moved, u)
                        if t:
                            nc.tensor.matmul(K.bank[4][:, :], xbc[:, 20 + g, toks], state[:, g, :], start=True, stop=True)
                        nc.tensor.matmul(K.bank[5][:, :], xtok[:, t, SI + g * SN:SI + (g + 1) * SN], xe[:, u % 2, :], start=True, stop=True)
                        for e in range(SE):
                            last = nc.tensor.matmul(K.bank[3][:, e * SP:(e + 1) * SP], dec[:, u % 2, e, :], xr[:, u % 2, e * SP:(e + 1) * SP],
                                                    start=True, stop=True)
                        last.then_inc(produced, 1)

            @block.scalar
            def _(act):
                nc.scalar.activation(z[:, :, :], z[:, :, :], ACT.Silu).then_inc(gated, 1)
                for u in range(len(UNITS)):
                    act.wait_ge(shifted, u + 1)
                    nc.scalar.activation(last_dec[:, u % 2, 0:4], K.bank[0][:, P - 1:S:P], ACT.Exp)
                    nc.scalar.activation(last_dec[:, u % 2, 4:8], K.bank[1][:, P - 1:S:P], ACT.Exp)
                    nc.scalar.activation(dec[:, u % 2], dec[:, u % 2], ACT.Exp).then_inc(exped, 1)
                for u, (t, g) in enumerate(UNITS):
                    act.wait_ge(finished, u + 1)
                    if u:
                        act.wait_ge(squared, u)
                    nc.scalar.activation(junk[:, :], z[:, t, g * GWID:(g + 1) * GWID], ACT.Square, accum_out=ss[:, 0, t, g:g + 1]).then_inc(squared, 1)
                act.wait_ge(rooted, 1)
                nc.scalar.activation(ss[:, 0], ss[:, 1], ACT.Sqrt).then_inc(rooted, 1)

            @block.vector
            def _(dve):
                done = Settle(dve, vec_step)
                dve.wait_ge(masked, 4)
                dve.wait_ge(gated, 1)
                for step in range(len(UNITS) + 1):
                    if step < len(UNITS):
                        u = step
                        t, g = UNITS[u]
                        dve.wait_ge(spread, u + 1)
                        if u >= 2:
                            dve.wait_ge(produced, u - 1)
                        for b in range(2):
                            last = nc.vector.tensor_tensor(dec[:, u % 2, b * 4:(b + 1) * 4, :], K.bank[b][:, :].rearrange("p (e l) -> p e l", e=4),
                                                           nmask[:, :].unsqueeze(1).broadcast_to([P, 4, P]), ALU.add)
                        done(nc.vector.tensor_tensor(cb[:, u % 2, :], K.bank[2][:, 0:P], cmask[:, :], ALU.mult))
                        nc.vector.tensor_tensor(dec[:, u % 2], dec[:, u % 2],
                                                rows[:, 0, t, g * SE:(g + 1) * SE].unsqueeze(2).broadcast_to([P, SE, P]), ALU.subtract).then_inc(shifted, 1)
                        dve.wait_ge(exped, u + 1)
                        nc.vector.tensor_tensor(dec[:, u % 2], dec[:, u % 2], cb[:, u % 2, :].unsqueeze(1).broadcast_to([P, SE, P]), ALU.mult).then_inc(mixed, 1)
                    if step >= 1:
                        u = step - 1
                        t, g = UNITS[u]
                        cols = slice(g * GWID, (g + 1) * GWID)
                        dve.wait_ge(produced, u + 1)
                        sk = skip[:, u % 2, :]
                        if t:
                            nc.vector.tensor_tensor(heads(off[:, u % 2, :]), heads(K.bank[4][:, :]),
                                                    rows[:, 3, t, g * SE:(g + 1) * SE].unsqueeze(2).broadcast_to([P, SE, SP]), ALU.mult)
                            done(nc.vector.tensor_tensor(heads(state[:, g, :]), heads(state[:, g, :]),
                                                         last_dec[:, u % 2, :].unsqueeze(2).broadcast_to([P, SE, SP]), ALU.mult))
                            done(nc.vector.tensor_tensor(sk, sk, off[:, u % 2, :], ALU.add))
                            nc.vector.tensor_tensor(state[:, g, :], state[:, g, :], K.bank[5][:, :], ALU.add)
                        else:
                            nc.vector.tensor_copy(state[:, g, :], K.bank[5][:, :])
                        ins = nc.vector.tensor_tensor(sk, sk, K.bank[3][:, :], ALU.add)
                        ins.then_inc(moved, 1)
                        dve.wait_ge(moved, u + 1)
                        nc.vector.tensor_tensor(z[:, t, cols], z[:, t, cols], sk, ALU.mult).then_inc(finished, 1)
                dve.wait_ge(squared, len(UNITS))
                nc.vector.tensor_scalar(ss[:, 1], ss[:, 0], 1.0 / GWID, LN_EPS, ALU.mult, ALU.add).then_inc(rooted, 1)
                dve.wait_ge(rooted, 2)
                done(nc.vector.reciprocal(ss[:, 1], ss[:, 0]))
                for t, g in UNITS:
                    cols = slice(g * GWID, (g + 1) * GWID)
                    nc.vector.tensor_scalar(z[:, t, cols], z[:, t, cols], ss[:, 1, t, g:g + 1], None, ALU.mult)


EG, EE, NE = 4, 8, 32
HID = 512
KH = HID // P
NB = -(-((2 * S + NE * (P - 1)) // P) // 2) * 2
FAR_INDEX = 100.0


def moe(nc, K, A, layer, o):
    with ExitStack() as mem:
        sb = lambda n, s, dt=F32: mem.enter_context(nc.sbuf_tensor(f"moe{layer}_{n}", s, dt))
        weight = sb("weight", [P, 2, TT])
        dest = sb("dest", [P, 2, TT], U32)
        expert = sb("expert", [1, NB], I32)
        idx = sb("idx", [P, NB + 2], U32)
        K.scattered = nc.alloc_semaphore(f"scattered{layer}")
        K.x_gathered = [nc.alloc_semaphore(f"x_gathered{layer}_{s}") for s in range(2)]
        K.picked = [nc.alloc_semaphore(f"picked{layer}_{n}") for n in range(2 * TT)]
        moe_route(nc, K, A, layer, weight, dest, expert, idx)
        moe_experts(nc, K, A, layer, expert, idx)
        moe_combine(nc, K, layer, weight, dest, o)


def moe_route(nc, K, A, layer, weight, dest, expert, idx):
    K.x_rows = nc.dram_tensor(f"x_rows{layer}", (S, D), F32, kind="Internal").ap()
    K.y_rows = nc.dram_tensor(f"y_rows{layer}", (NB * P, D), F32, kind="Internal").ap()
    tokens_of = nc.dram_tensor(f"tokens_of_rows{layer}", ((NB + 2) * P, 1), F32, kind="Internal").ap()
    with ExitStack() as mem:
        sb = lambda n, s, dt=F32: mem.enter_context(nc.sbuf_tensor(f"rt{layer}_{n}", s, dt))
        xT = sb("xT", [P, KD, S])
        to_channels(nc, K, K.x, xT, KD)
        NL = EG + NE
        wr, br = sb("w", [P, KD, NL]), sb("b", [P, NL])
        lg = sb("logit", [P, TT, NL])
        before, ones = sb("before", [P, P]), sb("ones", [P, P])
        iota_e, iota_b, iota_t = sb("iota_e", [P, NE]), sb("iota_b", [P, NB]), sb("iota_t", [P, TT])
        zero = sb("zero", [NB + 2, P])
        g4, e4 = sb("g4", [P, TT, 3, EG]), sb("e4", [P, TT, EG])
        el, cand = sb("el", [P, TT, NE]), sb("cand", [P, TT, NE])
        oh = sb("oh", [P, 3, TT, NE])
        st = sb("st", [P, 12, TT])
        rank = sb("rank", [P, TT, NE])
        cnt, nblk, bend, tmp32 = (sb(n, [P, NE]) for n in ("cnt", "nblk", "bend", "tmp32"))
        cmpb, fexp = sb("cmpb", [1, NB, NE]), sb("fexp", [1, NB])
        destf = sb("destf", [P, 2, TT])
        tok_rows = sb("tok_rows", [NB + 2, P])
        MX, EX, SM, GI, GW1, M1, I1, M2, I2, DN, T1, T2 = range(12)
        col = lambda i: st[:, i, :]
        wide = lambda i, n: st[:, i, :].unsqueeze(2).broadcast_to([P, TT, n])
        with stage(nc, "loaded", "made", "logits", "vec_step", "asked", "exped", "counted", "zeroed", "x_stored",
                   "reloaded", "turned", "placed") as (
                block, (loaded, made, logits, vec_step, asked, exped, counted, zeroed, x_stored, reloaded, turned, placed)):
            scattered = K.scattered

            @block.sync
            def _(sp):
                sp.dma_start(wr[:, :, 0:EG], A.moe_w_router_group_2[layer].rearrange("(k p) m -> p k m", p=P)).then_inc(loaded, 16)
                sp.dma_start(wr[:, :, EG:NL], A.moe_w_router_expert_2[layer].rearrange("(k p) m -> p k m", p=P)).then_inc(loaded, 16)
                sp.dma_start(br[:, 0:EG], broadcast_row(A.moe_b_router_group_2[layer])).then_inc(loaded, 16)
                sp.dma_start(br[:, EG:NL], broadcast_row(A.moe_b_router_expert_2[layer])).then_inc(loaded, 16)
                sp.dma_start(K.x_rows.rearrange("(t p) d -> p t d", p=P), K.x[:, :, :]).then_inc(x_stored, 16)
                sp.wait_ge(made, 8)
                sp.dma_start(tokens_of.rearrange("(b p) a -> b (p a)", p=P), zero[:, :]).then_inc(zeroed, 16)
                sp.wait_ge(scattered, 16 * 2 * TT)
                sp.dma_start(tok_rows[:, :], tokens_of.rearrange("(b p) a -> b (p a)", p=P)).then_inc(reloaded, 16)
                sp.wait_ge(x_stored, 16)

            @block.gpsimd
            def _(pool):
                nc.gpsimd.memset(before[:, :], 1.0).then_inc(made, 1)
                nc.gpsimd.memset(ones[:, :], 1.0).then_inc(made, 1)
                pool.wait_ge(made, 2)
                nc.gpsimd.affine_select(out=before[:, :], in_=before[:, :], compare_op=ALU.is_gt, fill=0.0, base=0,
                                        pattern=[[1, P]], channel_multiplier=-1).then_inc(made, 1)
                nc.gpsimd.iota(iota_e[:, :], pattern=[[1, NE]], base=0, channel_multiplier=0, allow_small_or_imprecise_dtypes=True).then_inc(made, 1)
                nc.gpsimd.iota(iota_b[:, :], pattern=[[1, NB]], base=0, channel_multiplier=0, allow_small_or_imprecise_dtypes=True).then_inc(made, 1)
                nc.gpsimd.iota(iota_t[:, :], pattern=[[P, TT]], base=0, channel_multiplier=1, allow_small_or_imprecise_dtypes=True).then_inc(made, 1)
                nc.gpsimd.memset(zero[:, :], 0.0).then_inc(made, 1)
                pool.wait_ge(made, 7)
                nc.gpsimd.engine_nop().then_inc(made, 1)
                pool.wait_ge(placed, 1)
                pool.wait_ge(zeroed, 16)
                for k in range(2):
                    for t in range(TT):
                        nc.gpsimd.indirect_dma_start(out=tokens_of, out_offset=bass.IndirectOffsetOnAxis(ap=dest[:, k, t:t + 1], axis=0),
                                                     in_=iota_t[:, t:t + 1], in_offset=None).then_inc(scattered, 16)

            @block.tensor
            def _(pe):
                pe.wait_ge(loaded, 64)
                for t in range(TT):
                    for k in range(KD):
                        last = nc.tensor.matmul(K.bank[0][:, t * NL:(t + 1) * NL], xT[:, k, t * P:(t + 1) * P], wr[:, k, :],
                                                start=(k == 0), stop=(k == KD - 1))
                last.then_inc(logits, 1)
                pe.wait_ge(made, 8)
                pe.wait_ge(asked, 2)
                for t in range(TT):
                    for b in range(t + 1):
                        nc.tensor.matmul(K.bank[1][:, t * NE:(t + 1) * NE], (before if b == t else ones)[:, :], oh[:, 2, b, :],
                                         start=(b == 0), stop=(b == t))
                for b in range(TT):
                    last = nc.tensor.matmul(K.bank[1][:, TT * NE:(TT + 1) * NE], ones[:, :], oh[:, 2, b, :], start=(b == 0), stop=(b == TT - 1))
                last.then_inc(counted, 1)
                pe.wait_ge(reloaded, 16)
                nc.tensor.transpose(K.bank[2][:, 0:NB + 2], tok_rows[:, :], K.ident[0:NB + 2, 0:NB + 2]).then_inc(turned, 1)

            @block.scalar
            def _(act):
                act.wait_ge(asked, 1)
                nc.scalar.activation(g4[:, :, 1, :], g4[:, :, 0, :], ACT.Exp).then_inc(exped, 1)
                act.wait_ge(asked, 2)
                nc.scalar.activation(col(EX), col(T1), ACT.Exp).then_inc(exped, 1)

            @block.vector
            def _(dve):
                done = Settle(dve, vec_step)

                def first_equal(values, best, iota, n, scratch, index, out):
                    shape = [P, TT, n]
                    done(nc.vector.tensor_tensor(scratch, values, wide(best, n), ALU.is_equal))
                    done(nc.vector.tensor_scalar(scratch, scratch, -FAR_INDEX, FAR_INDEX, ALU.mult, ALU.add))
                    done(nc.vector.tensor_tensor(scratch, scratch, iota[:, 0:n].unsqueeze(1).broadcast_to(shape), ALU.add))
                    done(nc.vector.tensor_reduce(col(index), scratch, AX, ALU.min))
                    done(nc.vector.tensor_tensor(out, wide(index, n), iota[:, 0:n].unsqueeze(1).broadcast_to(shape), ALU.is_equal))

                dve.wait_ge(logits, 1)
                dve.wait_ge(made, 8)
                done(nc.vector.tensor_tensor(lg[:, :, :], K.bank[0][:, 0:TT * NL].rearrange("p (t n) -> p t n", t=TT),
                                             br[:, :].unsqueeze(1).broadcast_to([P, TT, NL]), ALU.add))
                gl = lg[:, :, 0:EG]
                done(nc.vector.tensor_reduce(col(MX), gl, AX, ALU.max))
                nc.vector.tensor_tensor(g4[:, :, 0, :], gl, wide(MX, EG), ALU.subtract).then_inc(asked, 1)
                first_equal(gl, MX, iota_e, EG, g4[:, :, 2, :], GI, e4[:, :, :])
                dve.wait_ge(exped, 1)
                done(nc.vector.tensor_reduce(col(SM), g4[:, :, 1, :], AX, ALU.add))
                done(nc.vector.reciprocal(col(GW1), col(SM)))
                done(nc.vector.tensor_scalar(e4[:, :, :], e4[:, :, :], -NEG, NEG, ALU.mult, ALU.add))
                done(nc.vector.tensor_tensor(el[:, :, :].rearrange("p t (g e) -> p t g e", g=EG),
                                             lg[:, :, EG:].rearrange("p t (g e) -> p t g e", g=EG),
                                             e4[:, :, :].unsqueeze(3).broadcast_to([P, TT, EG, EE]), ALU.add))
                done(nc.vector.tensor_reduce(col(M1), el[:, :, :], AX, ALU.max))
                first_equal(el[:, :, :], M1, iota_e, NE, cand[:, :, :], I1, oh[:, 0])
                done(nc.vector.scalar_tensor_tensor(out=el[:, :, :], in0=oh[:, 0], scalar=4 * NEG, in1=el[:, :, :], op0=ALU.mult, op1=ALU.add))
                done(nc.vector.tensor_reduce(col(M2), el[:, :, :], AX, ALU.max))
                first_equal(el[:, :, :], M2, iota_e, NE, cand[:, :, :], I2, oh[:, 1])
                done(nc.vector.tensor_tensor(col(T1), col(M2), col(M1), ALU.subtract))
                nc.vector.tensor_tensor(oh[:, 2], oh[:, 0], oh[:, 1], ALU.add).then_inc(asked, 1)
                dve.wait_ge(exped, 2)
                done(nc.vector.tensor_scalar(col(DN), col(EX), 1.0, None, ALU.add))
                done(nc.vector.reciprocal(col(T2), col(DN)))
                done(nc.vector.tensor_tensor(weight[:, 0, :], col(T2), col(GW1), ALU.mult))
                done(nc.vector.tensor_tensor(weight[:, 1, :], weight[:, 0, :], col(EX), ALU.mult))
                dve.wait_ge(counted, 1)
                done(nc.vector.tensor_copy(cnt[:, :], K.bank[1][:, TT * NE:(TT + 1) * NE]))
                done(nc.vector.tensor_scalar(nblk[:, :], cnt[:, :], 0.0, None, ALU.is_gt))
                for j in range(1, S // P):
                    done(nc.vector.scalar_tensor_tensor(out=nblk[:, :], in0=cnt[:, :], scalar=float(j * P), in1=nblk[:, :], op0=ALU.is_gt, op1=ALU.add))
                done(nc.vector.tensor_tensor_scan(bend[:, :], ones[:, 0:NE], nblk[:, :], 0.0, ALU.mult, ALU.add))
                done(nc.vector.tensor_tensor(tmp32[:, :], bend[:, :], nblk[:, :], ALU.subtract))
                done(nc.vector.tensor_scalar(tmp32[:, :], tmp32[:, :], float(P), None, ALU.mult))
                done(nc.vector.tensor_tensor(rank[:, :, :], K.bank[1][:, 0:TT * NE].rearrange("p (t e) -> p t e", t=TT),
                                             tmp32[:, :].unsqueeze(1).broadcast_to([P, TT, NE]), ALU.add))
                for k in range(2):
                    done(nc.vector.tensor_tensor(cand[:, :, :], rank[:, :, :], oh[:, k], ALU.mult))
                    done(nc.vector.tensor_reduce(destf[:, k, :], cand[:, :, :], AX, ALU.add))
                nc.vector.tensor_copy(dest[:, :, :], destf[:, :, :]).then_inc(placed, 1)
                done(nc.vector.tensor_tensor(cmpb[:, :, :], iota_b[0:1, :].unsqueeze(2).broadcast_to([1, NB, NE]),
                                             bend[0:1, :].unsqueeze(1).broadcast_to([1, NB, NE]), ALU.is_ge))
                done(nc.vector.tensor_reduce(fexp[:, :], cmpb[:, :, :], AX, ALU.add))
                done(nc.vector.tensor_scalar(expert[:, :], fexp[:, :], float(NE - 1), None, ALU.min))
                dve.wait_ge(turned, 1)
                done(nc.vector.tensor_copy(idx[:, :], K.bank[2][:, 0:NB + 2]))


def moe_experts(nc, K, A, layer, expert, idx):
    wg_d = A.moe_w_gate_2[layer].rearrange("e (k p) m -> e p k m", p=P)
    wu_d = A.moe_w_up_2[layer].rearrange("e (k p) m -> e p k m", p=P)
    wd_d = A.moe_w_down_2[layer].rearrange("e (k p) m -> e p k m", p=P)
    with ExitStack() as mem:
        sb = lambda n, s, dt=F32: mem.enter_context(nc.sbuf_tensor(f"ex{layer}_{n}", s, dt))
        wg, wu, wd = sb("wg", [P, 2, KD, HID]), sb("wu", [P, 2, KD, HID]), sb("wd", [P, 2, KH, D])
        col = sb("col", [P, 2], U32)
        x = sb("x", [P, 2, D])
        xT = sb("xT", [P, 2, D])
        gate, h, hT = sb("gate", [P, 2, HID]), sb("h", [P, 2, HID]), sb("hT", [P, 2, HID])
        y = sb("y", [P, 2, D])
        TX, GB, UB, HB, DB = K.bank[0:2], K.bank[2], K.bank[3], K.bank[4], K.bank[5:7]
        with stage(nc, "g_loaded0", "g_loaded1", "u_loaded0", "u_loaded1", "d_loaded0", "d_loaded1",
                   "named", "asked", "x_turned", "x_kept", "gate_ready", "up_ready", "gate_done", "h_ready", "h_turned", "h_kept", "down_ready", "y_kept",
                   "y_stored0", "y_stored1") as (
                block, (g0, g1, u0, u1, d0, d1, named, asked, x_turned, x_kept, gate_ready, up_ready, gate_done, h_ready, h_turned,
                        h_kept, down_ready, y_kept, y0, y1)):
            g_loaded, u_loaded, d_loaded, x_loaded, y_stored = (g0, g1), (u0, u1), (d0, d1), K.x_gathered, (y0, y1)

            @block.sync
            def _(sp):
                with sp.Fori(0, NB // 2) as i:
                    for s in range(2):
                        e = sp.value_load(expert[0:1, ds(i * 2 + s, 1)], min_val=0, max_val=NE - 1)
                        sp.wait_ge(gate_ready, i * 2 + s + 1)
                        sp.dma_start(wg[:, s], wg_d[ds(e, 1)].rearrange("e p k m -> p (e k) m")).then_inc(g_loaded[s], 16)
                        sp.wait_ge(up_ready, i * 2 + s + 1)
                        sp.dma_start(wu[:, s], wu_d[ds(e, 1)].rearrange("e p k m -> p (e k) m")).then_inc(u_loaded[s], 16)
                        sp.wait_ge(down_ready, i * 2 + s + 1)
                        sp.dma_start(wd[:, s], wd_d[ds(e, 1)].rearrange("e p k m -> p (e k) m")).then_inc(d_loaded[s], 16)

            @block.gpsimd
            def _(pool):
                def gather(s, b, first):
                    nc.gpsimd.tensor_copy(col[:, s:s + 1], idx[:, ds(b, 1)]).then_inc(named, 1)
                    pool.wait_ge(named, b + 1)
                    pool.sem_inc(asked, 1)
                    nc.gpsimd.indirect_dma_start(out=x[:, s, :], out_offset=None, in_=K.x_rows,
                                                 in_offset=bass.IndirectOffsetOnAxis(ap=col[:, s:s + 1], axis=0)).then_inc(x_loaded[s], 16)

                gather(0, 0, True)
                with pool.Fori(0, NB // 2) as i:
                    for s in range(2):
                        b = i * 2 + s
                        pool.wait_ge(x_turned, b + 1)
                        gather(1 - s, b + 1, False)

            @block.tensor
            def _(pe):
                def turn_x(s, i_next, b):
                    pe.wait_ge(x_loaded[s], i_next)
                    for k in range(KD):
                        last = nc.tensor.transpose(TX[k // 4][:, (k % 4) * P:(k % 4 + 1) * P], x[:, s, k * P:(k + 1) * P], K.ident[:, :])
                    last.then_inc(x_turned, 1)

                pe.sem_inc(gate_ready, 2)
                pe.sem_inc(up_ready, 2)
                pe.sem_inc(down_ready, 2)
                pe.sem_inc(x_turned, 1)
                turn_x(0, 16, 0)
                with pe.Fori(0, NB // 2) as i:
                    for s in range(2):
                        b = i * 2 + s
                        pe.wait_ge(x_kept, b + 1)
                        pe.wait_ge(g_loaded[s], i * 16 + 16)
                        pe.wait_ge(gate_done, b + 1)
                        for k in range(KD):
                            last = nc.tensor.matmul(GB[:, :], xT[:, s, k * P:(k + 1) * P], wg[:, s, k, :], start=(k == 0), stop=(k == KD - 1))
                        last.then_inc(gate_ready, 1)
                        pe.wait_ge(u_loaded[s], i * 16 + 16)
                        pe.wait_ge(h_ready, b + 1)
                        for k in range(KD):
                            last = nc.tensor.matmul(UB[:, :], xT[:, s, k * P:(k + 1) * P], wu[:, s, k, :], start=(k == 0), stop=(k == KD - 1))
                        last.then_inc(up_ready, 1)
                        turn_x(1 - s, i * 16 + 16 * (s + 1), b + 1)
                        pe.wait_ge(h_ready, b + 2)
                        for k in range(KH):
                            last = nc.tensor.transpose(HB[:, k * P:(k + 1) * P], h[:, s, k * P:(k + 1) * P], K.ident[:, :])
                        last.then_inc(h_turned, 1)
                        pe.wait_ge(h_kept, b + 1)
                        pe.wait_ge(d_loaded[s], i * 16 + 16)
                        pe.wait_ge(y_kept, b + 1)
                        for half in range(2):
                            for k in range(KH):
                                last = nc.tensor.matmul(DB[half][:, :], hT[:, s, k * P:(k + 1) * P], wd[:, s, k, half * 512:(half + 1) * 512],
                                                        start=(k == 0), stop=(k == KH - 1))
                        last.then_inc(down_ready, 1)

            @block.scalar
            def _(act):
                def keep_x(s, b):
                    act.wait_ge(x_turned, b + 2)
                    nc.scalar.activation(xT[:, s, 0:512], TX[0][:, :], ACT.Copy)
                    nc.scalar.activation(xT[:, s, 512:D], TX[1][:, :], ACT.Copy).then_inc(x_kept, 1)

                act.sem_inc(gate_done, 1)
                for s in range(2):
                    act.sem_inc(y_stored[s], 16)
                keep_x(0, 0)
                with act.Fori(0, NB // 2) as i:
                    for s in range(2):
                        b = i * 2 + s
                        act.wait_ge(gate_ready, b + 3)
                        nc.scalar.activation(gate[:, s, :], GB[:, :], ACT.Silu).then_inc(gate_done, 1)
                        keep_x(1 - s, b + 1)
                        act.wait_ge(y_kept, b + 2)
                        act.dma_start(K.y_rows[ds(b * P, P), :], y[:, s, :]).then_inc(y_stored[s], 16)
                for s in range(2):
                    act.wait_ge(y_stored[s], 16 * (NB // 2 + 1))

            @block.vector
            def _(dve):
                dve.sem_inc(h_ready, 1)
                dve.sem_inc(y_kept, 1)
                with dve.Fori(0, NB // 2) as i:
                    for s in range(2):
                        b = i * 2 + s
                        dve.wait_ge(gate_done, b + 2)
                        dve.wait_ge(up_ready, b + 3)
                        nc.vector.tensor_tensor(h[:, s, :], gate[:, s, :], UB[:, :], ALU.mult).then_inc(h_ready, 1)
                        dve.wait_ge(h_turned, b + 1)
                        nc.vector.tensor_copy(hT[:, s, :], HB[:, :]).then_inc(h_kept, 1)
                        dve.wait_ge(down_ready, b + 3)
                        dve.wait_ge(y_stored[s], i * 16 + 16)
                        nc.vector.tensor_copy(y[:, s, 0:512], DB[0][:, :])
                        nc.vector.tensor_copy(y[:, s, 512:D], DB[1][:, :]).then_inc(y_kept, 1)


def moe_combine(nc, K, layer, weight, dest, o):
    with nc.sbuf_tensor(f"picked{layer}", [P, 2, TT, D], F32) as picked:
        with stage(nc, "weighed", "summed") as (block, (weighed, summed)):
            @block.gpsimd
            def _(pool):
                for t in range(TT):
                    for k in range(2):
                        nc.gpsimd.indirect_dma_start(out=picked[:, k, t, :], out_offset=None, in_=K.y_rows,
                                                     in_offset=bass.IndirectOffsetOnAxis(ap=dest[:, k, t:t + 1], axis=0)).then_inc(K.picked[2 * t + k], 16)

            @block.vector
            def _(dve):
                for t in range(TT):
                    dve.wait_ge(K.picked[2 * t], 16)
                    nc.vector.tensor_scalar(o[:, t, :], picked[:, 0, t, :], weight[:, 0, t:t + 1], None, ALU.mult).then_inc(weighed, 1)
                    dve.wait_ge(K.picked[2 * t + 1], 16)
                    dve.wait_ge(weighed, t + 1)
                    nc.vector.scalar_tensor_tensor(out=o[:, t, :], in0=picked[:, 1, t, :], scalar=weight[:, 1, t:t + 1], in1=o[:, t, :],
                                                   op0=ALU.mult, op1=ALU.add).then_inc(summed, 1)


AH = 8
AR = 4
ROPE = 16


def attention_constants():
    half = ROPE // 2
    inv = (500000.0 ** (-np.arange(0, ROPE, 2, dtype=np.float32) / ROPE)).astype(np.float32)
    rot, freq = np.zeros((P, P), np.float32), np.zeros((P, 1), np.float32)
    for base in (0, HD):
        for i in range(half):
            rot[base + half + i, base + i] = -1.0
            rot[base + i, base + half + i] = 1.0
            freq[base + i] = freq[base + half + i] = inv[i]
    j = np.arange(P)
    dist = (4 * j[:, None, None] + np.arange(AR)[None, :, None]) - np.arange(S)[None, None, :]
    near = np.where((dist >= 0) & (dist <= 128), 0.0, NEG)
    causal = np.where(j[:, None] >= j[None, :], 0.0, NEG)
    sparse = np.where((j[:, None] >= j[None, :]) & ((j[:, None] - j[None, :]) % 4 == 0), 0.0, NEG)
    masks = np.concatenate([near.reshape(P, AR * S), causal, sparse], 1)
    return np.concatenate([rot, freq, masks], 1).astype(np.float32)


def rope_tables(nc, A, const, cos, sin):
    TWO_PI = 2 * np.pi
    C1 = 6.28125
    C2 = float(np.float32(TWO_PI - C1))
    C3 = float(TWO_PI - C1 - C2)
    MAGIC = 1.5 * 2.0 ** 23
    PI = float(np.nextafter(np.float32(np.pi), np.float32(0)))
    with ExitStack() as mem:
        posi = mem.enter_context(nc.sbuf_tensor("pos_i", [P, S], I32))
        ang, n, r = (mem.enter_context(nc.sbuf_tensor(f"rope_{x}", [P, S], F32)) for x in ("ang", "n", "r"))
        with stage(nc, "loaded", "vec_step", "reduced", "taken") as (block, (loaded, vec_step, reduced, taken)):
            @block.sync
            def _(sp):
                sp.dma_start(posi[:, :], broadcast_row(A.positions_2)).then_inc(loaded, 16)

            @block.vector
            def _(dve):
                done = Settle(dve, vec_step)
                dve.wait_ge(loaded, 16)
                done(nc.vector.tensor_copy(ang[:, :], posi[:, :]))
                done(nc.vector.tensor_scalar(ang[:, :], ang[:, :], const[:, P:P + 1], None, ALU.mult))
                for k, (turn, shift) in enumerate(((0.0, 0.0), (0.25, np.pi / 2))):
                    done(nc.vector.tensor_scalar(n[:, :], ang[:, :], float(1 / TWO_PI), turn, ALU.mult, ALU.add))
                    done(nc.vector.tensor_scalar(n[:, :], n[:, :], MAGIC, MAGIC, ALU.add, ALU.subtract))
                    if k:
                        dve.wait_ge(taken, k)
                    done(nc.vector.scalar_tensor_tensor(out=r[:, :], in0=n[:, :], scalar=-C1, in1=ang[:, :], op0=ALU.mult, op1=ALU.add))
                    done(nc.vector.scalar_tensor_tensor(out=r[:, :], in0=n[:, :], scalar=-C2, in1=r[:, :], op0=ALU.mult, op1=ALU.add))
                    done(nc.vector.scalar_tensor_tensor(out=r[:, :], in0=n[:, :], scalar=-C3, in1=r[:, :], op0=ALU.mult, op1=ALU.add))
                    done(nc.vector.tensor_scalar(r[:, :], r[:, :], float(shift), PI, ALU.add, ALU.min))
                    nc.vector.tensor_scalar(r[:, :], r[:, :], -PI, None, ALU.max).then_inc(reduced, 1)
                    dve.wait_ge(reduced, k + 1)

            @block.scalar
            def _(act):
                for k, out in enumerate((sin, cos)):
                    act.wait_ge(reduced, k + 1)
                    nc.scalar.activation(out[:, :], r[:, :], ACT.Sin).then_inc(taken, 1)


def attention(nc, K, A, o):
    w = A.attn_w_qkv_2[0].rearrange("(k p) m -> p k m", p=P)
    HW = AH * HD
    const_dram = nc.inline_tensor(attention_constants(), name="attention_constants").ap()
    with ExitStack() as mem:
        sb = lambda n, s: mem.enter_context(nc.sbuf_tensor(f"dil_{n}", s, F32))
        ores = sb("ores", [P, AR, HW])
        with ExitStack() as inner:
            sb2 = lambda n, s: inner.enter_context(nc.sbuf_tensor(f"dil_{n}", s, F32))
            const = sb2("const", [P, P + 1 + AR * S + 2 * P])
            cos, sin = sb2("cos", [P, S]), sb2("sin", [P, S])
            qk = sb2("qk", [P, 3, 8, S])
            v = sb2("v", [P, 3, TT, HW])
            with stage(nc, "loaded") as (block, (loaded,)):
                @block.sync
                def _(sp):
                    sp.dma_start(const[:, :], const_dram).then_inc(loaded, 16)
                    sp.wait_ge(loaded, 16)
            rope_tables(nc, A, const, cos, sin)
            with nc.sbuf_tensor("dil_xT", [P, KD, S], F32) as xT:
                to_channels(nc, K, K.x, xT, KD)
                for g in range(3):
                    for part in range(2):
                        project_channels(nc, K, w, KD, xT, 2, lambda c: c * CW + (g * 3 + part) * HW,
                                         lambda bank, m: nc.scalar.activation(qk[:, g, ds(m + 4 * part, 1), :], bank, ACT.Copy,
                                                                              scale=1.0 if part else HD ** -0.5))
                    rows = (lambda t: slice(t * P, (t + 1) * P)) if g == 0 else (lambda r: slice(r, S, AR))
                    project_tokens(nc, K, w, KD, xT, 2, lambda c: c * CW + (g * 3 + 2) * HW,
                                   lambda bank, t, c: nc.vector.tensor_copy(v[:, g, t, ds(c * CW, CW)], bank), rows)
            attend_residues(nc, K, const, cos, sin, qk, v, ores)
        oT = sb("oT", [P, HW // P, S])
        to_channels(nc, K, ores, oT, HW // P, residues=True)
        project_tokens(nc, K, A.attn_w_o_2[0].rearrange("(k p) m -> p k m", p=P), HW // P, oT, 4, lambda c: c * CW,
                       lambda bank, t, c: nc.vector.tensor_copy(o[:, t, ds(c * CW, CW)], bank))


def attend_residues(nc, K, const, cos, sin, qk, v, ores):
    UNITS = [(a, r) for a in range(2) for r in range(AR)]
    U = len(UNITS)
    W = S + 2 * P
    rot = const[:, 0:P]
    near = const[:, P + 1:P + 1 + AR * S].rearrange("p (r n) -> p r n", r=AR)
    sparse = const[:, P + 1 + AR * S:]
    with ExitStack() as mem:
        sb = lambda n, s: mem.enter_context(nc.sbuf_tensor(f"ar_{n}", s, F32))
        src = sb("src", [P, 6, S])
        turned_part = sb("turned", [P, 2, S])
        ready = sb("ready", [P, 6, S])
        logit, prob, probT = sb("logit", [P, 2, W]), sb("prob", [P, 2, W]), sb("probT", [P, 2, W])
        st = sb("st", [P, 2, 4])
        recips = sb("recips", [P, U])
        ROT = 12
        PER = ROT + 2 * U
        with stage(nc, "taken", "rotated", "vec_step", "prepared", "scored", "biased", "exped", "turned", "copied", "valued", "kept", "masked",
                   "opened") as (
                block, (taken, rotated, vec_step, prepared, scored, biased, exped, turned, copied, valued, kept, masked, opened)):

            @block.tensor
            def _(pe):
                with pe.Fori(0, AH // 2) as it:
                    for n in range(6):
                        pe.wait_ge(taken, it * 6 + n + 1)
                        if n >= 2:
                            pe.wait_ge(rotated, it * 6 + n - 1)
                        nc.tensor.matmul(K.bank[n % 2][:, :], rot, src[:, n, :], start=True, stop=True).then_inc(masked, 1)
                    pe.wait_ge(prepared, it + 1)
                    for step in range(U + 2):
                        if step < U:
                            u = step
                            a, r = UNITS[u]
                            rows = slice(a * HD, (a + 1) * HD)
                            b0, b1 = K.bank[2 * (u % 2)], K.bank[2 * (u % 2) + 1]
                            if u >= 2:
                                pe.wait_ge(biased, it * U + u - 1)
                            toks = slice(r * P, (r + 1) * P)
                            nc.tensor.matmul(b0[:, :], ready[rows, 0, toks], ready[rows, 3, :], start=True, stop=True)
                            nc.tensor.matmul(b1[:, 0:P], ready[rows, 1, toks], ready[rows, 4, toks], start=True, stop=True)
                            nc.tensor.matmul(b1[:, P:2 * P], ready[rows, 2, toks], ready[rows, 5, toks], start=True, stop=True).then_inc(scored, 1)
                        if 1 <= step <= U:
                            u = step - 1
                            pe.wait_ge(exped, it * U + u + 1)
                            if u >= 1:
                                pe.wait_ge(copied, it * U + u)
                            for j in range(W // P):
                                last = nc.tensor.transpose(K.bank[4 + j // 4][:, (j % 4) * P:(j % 4 + 1) * P], prob[:, u % 2, j * P:(j + 1) * P], K.ident[:, :])
                            last.then_inc(turned, 1)
                        if step >= 2:
                            u = step - 2
                            a, r = UNITS[u]
                            pe.wait_ge(copied, it * U + u + 1)
                            pe.wait_ge(kept, it * U + u + 1)
                            cols = ds(it * (2 * HD) + a * HD, HD)
                            for j in range(W // P):
                                g, t = (0, j) if j < TT else (j - TT + 1, r)
                                last = nc.tensor.matmul(K.bank[6][:, 0:HD], probT[:, u % 2, j * P:(j + 1) * P], v[:, g, t, cols],
                                                        start=(j == 0), stop=(j == W // P - 1))
                            last.then_inc(valued, 1)

            @block.scalar
            def _(act):
                with act.Fori(0, AH // 2) as it:
                    for n in range(6):
                        nc.scalar.activation(src[:, n, :], qk[:, n % 3, ds(it + 4 * (n // 3), 1), :].rearrange("p o n -> p (o n)"), ACT.Copy).then_inc(taken, 1)
                    for step in range(U + 1):
                        if step < U:
                            u = step
                            act.wait_ge(biased, it * U + u + 1)
                            if u >= 2:
                                act.wait_ge(turned, it * U + u - 1)
                            nc.scalar.activation(prob[:, u % 2, :], logit[:, u % 2, :], ACT.Exp, bias=st[:, u % 2, 2:3],
                                                 accum_out=st[:, u % 2, 3:4]).then_inc(exped, 1)
                        if step >= 1:
                            u = step - 1
                            act.wait_ge(turned, it * U + u + 1)
                            if u >= 2:
                                act.wait_ge(valued, it * U + u - 1)
                            nc.scalar.activation(probT[:, u % 2, 0:S], K.bank[4][:, :], ACT.Copy)
                            nc.scalar.activation(probT[:, u % 2, S:W], K.bank[5][:, 0:W - S], ACT.Copy).then_inc(copied, 1)
                    act.wait_ge(kept, it * U + U + 1)

            @block.vector
            def _(dve):
                dve.sem_inc(kept, 1)
                with dve.Fori(0, AH // 2) as it:
                    done = Settle(dve, vec_step, it * PER)
                    for n in range(6):
                        dve.wait_ge(masked, it * 6 + n + 1)
                        part = turned_part[:, n % 2, :]
                        done(nc.vector.tensor_tensor(part, K.bank[n % 2][:, :], sin[:, :], ALU.mult))
                        dve.sem_inc(rotated, 1)
                        done(nc.vector.tensor_tensor(src[:, n, :], src[:, n, :], cos[:, :], ALU.mult))
                        if n == 3:
                            ins = nc.vector.tensor_tensor(ready[:, n, :], src[:, n, :], part, ALU.add)
                        else:
                            split = lambda x: x.rearrange("p (j r) -> p r j", r=AR)
                            ins = nc.vector.tensor_tensor(ready[:, n, :].rearrange("p (r j) -> p r j", r=AR), split(src[:, n, :]), split(part), ALU.add)
                    ins.then_inc(prepared, 1)
                    for step in range(U + 3):
                        if step < U:
                            u = step
                            a, r = UNITS[u]
                            s = st[:, u % 2]
                            dve.wait_ge(scored, it * U + u + 1)
                            if u >= 2:
                                dve.wait_ge(exped, it * U + u - 1)
                            dve.sem_inc(opened, 1)
                            nc.vector.tensor_tensor_reduce(out=logit[:, u % 2, 0:S], in0=K.bank[2 * (u % 2)][:, :], in1=near[:, r, :], scale=1.0,
                                                           scalar=-3e38, op0=ALU.add, op1=ALU.max, accum_out=s[:, 0:1])
                            done(nc.vector.tensor_tensor_reduce(out=logit[:, u % 2, S:W], in0=K.bank[2 * (u % 2) + 1][:, 0:2 * P], in1=sparse, scale=1.0,
                                                                scalar=-3e38, op0=ALU.add, op1=ALU.max, accum_out=s[:, 1:2]))
                            nc.vector.tensor_reduce(s[:, 2:3], s[:, 0:2], AX, ALU.max, negate=True).then_inc(biased, 1)
                        if 1 <= step <= U:
                            u = step - 1
                            a, r = UNITS[u]
                            dve.wait_ge(exped, it * U + u + 1)
                            done(nc.vector.reciprocal(recips[:, u:u + 1], st[:, u % 2, 3:4]))
                        if step >= 3:
                            u = step - 3
                            a, r = UNITS[u]
                            dve.wait_ge(valued, it * U + u + 1)
                            nc.vector.tensor_scalar(ores[:, r, ds(it * (2 * HD) + a * HD, HD)], K.bank[6][:, 0:HD], recips[:, u:u + 1], None,
                                                    ALU.mult).then_inc(kept, 1)
                    assert done.n == PER


def second_block(nc, K, A):
    with nc.sbuf_tensor("mix", [P, TT, D], F32) as o:
        ssd(nc, K, A, o)
        if K.stop == 11:
            return
        layer_norm(nc, K, o, A.ln_g_2[0, 0], A.ln_b_2[0, 0])
        if K.stop == 12:
            return
        moe(nc, K, A, 0, o)
        if K.stop == 13:
            return
        layer_norm(nc, K, o, A.ln_g_2[0, 1], A.ln_b_2[0, 1])
        if K.stop == 14:
            return
        attention(nc, K, A, o)
        layer_norm(nc, K, o, A.ln_g_2[1, 0], A.ln_b_2[1, 0])
        if K.stop == 15:
            return
        moe(nc, K, A, 1, o)
        layer_norm(nc, K, o, A.ln_g_2[1, 1], A.ln_b_2[1, 1])




def program(nc, A, out, stop=None):
    RESTING.clear()
    K = Names()
    K.stop = stop
    K.bank = [nc.alloc_psum_tensor(f"bank{i}", [P, S], F32) for i in range(8)]
    K.x = nc.alloc_sbuf_tensor("x_tok", [P, TT, D], F32)
    constants(nc, K, A)
    with stage(nc, "x_loaded") as (block, (x_loaded,)):
        @block.sync
        def _(sp):
            sp.dma_start(K.x[:, :, :], A.x[0].rearrange("(t p) d -> p t d", p=P)).then_inc(x_loaded, 16)
            sp.wait_ge(x_loaded, 16)
    if stop is None or stop <= 10:
        first_block(nc, K, A)
    if stop is None or stop > 10:
        second_block(nc, K, A)
    if stop is None:
        with stage(nc, "x_stored") as (block, (x_stored,)):
            @block.sync
            def _(sp):
                sp.dma_start(out[0].rearrange("(t p) d -> p t d", p=P), K.x[:, :, :]).then_inc(x_stored, 16)
                sp.wait_ge(x_stored, 16)


def first_block(nc, K, A):
    with ExitStack() as mem:
        sb = lambda n, s: mem.enter_context(nc.sbuf_tensor(n, s, F32))
        K.hT = sb("hT", [P, KD, S])
        y = [sb(f"y{b}", [P, KD, S]) for b in range(2)]
        with ExitStack() as inner:
            h = inner.enter_context(nc.sbuf_tensor("h_tok", [P, TT, D], F32))
            rms_scale(nc, K, K.x, h)
            to_channels(nc, K, h, K.hT, KD, lambda k: vcol(K, "g0", k))
        lru(nc, K, A, y[0])
        if K.stop == 1:
            return
        nsa(nc, K, A, y[1])
        if K.stop == 2:
            return
        y.append(sb("y2", [P, KD, S]))
        gla(nc, K, A, y[2])
        if K.stop == 3:
            return
        merged = sb("merged", [P, KD, S])
        merge(nc, K, A, y, merged)
        if K.stop == 4:
            return
        o = sb("mixed", [P, TT, D])
        project_tokens(nc, K, A.w_out[0].rearrange("(k p) m -> p k m", p=P), KD, merged, 4, lambda c: c * CW,
                       lambda bank, t, c: nc.vector.tensor_copy(o[:, t, ds(c * CW, CW)], bank))
        residual_norm(nc, K, o, A.norm_g[0, 1])
        if K.stop == 5:
            return
    with ExitStack() as mem:
        sb = lambda n, s: mem.enter_context(nc.sbuf_tensor(n, s, F32))
        K.hT = sb("h2T", [P, KD, S])
        o = sb("ffn_o", [P, TT, D])
        rms_scale(nc, K, K.x, o)
        to_channels(nc, K, o, K.hT, KD, lambda k: vcol(K, "g2", k))
        ffn(nc, K, A, o)
        residual_norm(nc, K, o, A.norm_g[0, 3])


_INS = ["x", "rel_table", "norm_g", "w_in", "conv_w", "conv_b", "lru_w_gates", "lru_b_gates", "lru_lambda", "cmp_pos", "cmp_w1",
        "cmp_w2", "gla_wa2", "gla_ba", "gla_norm", "w_branch", "w_out", "w_ffn_in", "w_ffn_out", "positions_2", "ssd_w_in_2",
        "ssd_conv_w_2", "ssd_conv_b_2", "ssd_dt_bias_2", "ssd_a_log_2", "ssd_d_2", "ssd_norm_w_2", "ssd_w_out_2", "attn_w_qkv_2",
        "attn_w_o_2", "ln_g_2", "ln_b_2", "moe_w_router_group_2", "moe_b_router_group_2", "moe_w_router_expert_2",
        "moe_b_router_expert_2", "moe_w_gate_2", "moe_w_up_2", "moe_w_down_2"]


def kernel(**inputs):
    import concourse.bacc as bacc
    from concourse.bass_utils import run_bass_kernel_spmd

    nc = bacc.Bacc("TRN2", target_bir_lowering=False, num_devices=1)
    arrays, A = {}, Names()
    for name in _INS:
        a = np.ascontiguousarray(inputs[name])
        arrays[f"in_{name}"] = a
        A.__dict__[name] = nc.dram_tensor(f"in_{name}", a.shape, mybir.dt.from_np(a.dtype), kind="ExternalInput").ap()
    out = nc.dram_tensor("out", (1, S, D), F32, kind="ExternalOutput").ap()
    program(nc, A, out)
    result = run_bass_kernel_spmd(nc, [arrays], core_ids=[0])
    return result.results[0]["out"]
```

```python
from contextlib import ExitStack, contextmanager

import numpy as np
import concourse.bass as bass
from concourse import mybir
from concourse.bass import ds

F32 = mybir.dt.float32
F32R = mybir.dt.float32r
I32 = mybir.dt.int32
U32 = mybir.dt.uint32
ALU = mybir.AluOpType
ACT = mybir.ActivationFunctionType
AX = mybir.AxisListType.X

P = 128
S = 512
TT = S // P
D = 1024
KD = D // P
EPS = 1e-6
NEG = -1e30

C_LRU_X, C_LRU_G, C_Q, C_KV = 0, 1024, 2048, 3072
C_GATE = C_KV + 1536
C_GLA_Q = C_GATE + 48
C_GLA_K = C_GLA_Q + 512
C_GLA_V = C_GLA_K + 512
C_GLA_OG = C_GLA_V + 1024
C_GLA_LR = C_GLA_OG + 1024
C_MERGE = C_GLA_LR + 16
D_FF = 2816
KF = D_FF // P

CW = 256


class Settle:

    def __init__(self, eng, sem, base=0):
        self.eng, self.sem, self.base, self.n = eng, sem, base, 0

    def __call__(self, ins):
        ins.then_inc(self.sem, 1)
        self.n += 1
        self.eng.wait_ge(self.sem, self.base + self.n)


RESTING = []


@contextmanager
def stage(nc, *names):
    sems = [nc.alloc_semaphore(f"{n}_{nc.next_id()}") for n in names]
    with nc.Block() as block:
        yield block, sems
    for sem in RESTING:
        nc.release_semaphore(sem)
    for sem in sems:
        nc.gpsimd.sem_clear(sem)
    RESTING[:] = sems


def constants(nc, K, A):
    K.ident = nc.alloc_sbuf_tensor("ident", [P, P], F32)
    K.vec = nc.alloc_sbuf_tensor("vec", [P, 2, P], F32)
    rows = nc.alloc_sbuf_tensor("vec_rows", [P, 2, P], F32)
    parts = [[("g0", A.norm_g[0, 0:1, :]), ("g2", A.norm_g[0, 2:3, :]), ("conv_w", A.conv_w[0]), ("conv_b", A.conv_b),
              ("lru_b", A.lru_b_gates[0]), ("lam", A.lru_lambda), ("gla_ba", A.gla_ba), ("gla_norm", A.gla_norm),
              ("ssd_norm", A.ssd_norm_w_2)],
             [("ssd_conv_w", A.ssd_conv_w_2[0]), ("ssd_conv_b", A.ssd_conv_b_2)]]
    K.col = {}
    with stage(nc, "loaded", "zeroed", "ident_set", "turned", "copied") as (block, (loaded, zeroed, ident_set, turned, copied)):
        n_loads = sum(len(x) for x in parts)

        @block.sync
        def _(sp):
            for half, group in enumerate(parts):
                at = 0
                for name, ap in group:
                    n = int(np.prod(ap.shape)) // P
                    K.col[name] = (half, at)
                    if half == 0 and at == 0:
                        sp.wait_ge(zeroed, 1)
                    sp.dma_start(rows[at:at + n, half, :], ap.rearrange("a (k p) -> (a k) p", p=P)).then_inc(loaded, 16)
                    at += n

        @block.gpsimd
        def _(pool):
            nc.gpsimd.memset(rows[:, :, :], 0.0).then_inc(zeroed, 1)
            nc.gpsimd.memset(K.ident[:, :], 0.0).then_inc(ident_set, 1)
            pool.wait_ge(ident_set, 1)
            nc.gpsimd.affine_select(out=K.ident[:, :], in_=K.ident[:, :], compare_op=ALU.not_equal, fill=1.0,
                                    base=0, pattern=[[-1, P]], channel_multiplier=1).then_inc(ident_set, 1)

        @block.tensor
        def _(pe):
            pe.wait_ge(ident_set, 2)
            pe.wait_ge(loaded, 16 * n_loads)
            for half in range(2):
                nc.tensor.transpose(K.bank[half][:, 0:P], rows[:, half, :], K.ident[:, :]).then_inc(turned, 1)

        @block.vector
        def _(dve):
            for half in range(2):
                dve.wait_ge(turned, half + 1)
                nc.vector.tensor_copy(K.vec[:, half, :], K.bank[half][:, 0:P]).then_inc(copied, 1)


def vcol(K, name, i=0, n=1):
    half, at = K.col[name]
    return K.vec[:, half, at + i:at + i + n]


def rms_scale(nc, K, src, dst, width=D):
    with ExitStack() as mem:
        junk = mem.enter_context(nc.sbuf_tensor(f"sq_{nc.next_id()}", [P, width], F32))
        stat = mem.enter_context(nc.sbuf_tensor(f"stat_{nc.next_id()}", [P, 3, TT], F32))
        with stage(nc, "squared", "meaned", "rooted", "inverted", "scaled") as (block, (squared, meaned, rooted, inverted, scaled)):
            @block.scalar
            def _(act):
                for t in range(TT):
                    if t:
                        act.wait_ge(squared, t)
                    nc.scalar.activation(junk[:, :], src[:, t, :], ACT.Square, accum_out=stat[:, 0, t:t + 1]).then_inc(squared, 1)
                act.wait_ge(meaned, 1)
                nc.scalar.activation(stat[:, 2, :], stat[:, 1, :], ACT.Sqrt).then_inc(rooted, 1)

            @block.vector
            def _(dve):
                dve.wait_ge(squared, TT)
                nc.vector.tensor_scalar(stat[:, 1, :], stat[:, 0, :], 1.0 / width, EPS, ALU.mult, ALU.add).then_inc(meaned, 1)
                dve.wait_ge(rooted, 1)
                nc.vector.reciprocal(stat[:, 0, :], stat[:, 2, :]).then_inc(inverted, 1)
                dve.wait_ge(inverted, 1)
                for t in range(TT):
                    nc.vector.tensor_scalar(dst[:, t, :], src[:, t, :], stat[:, 0, t:t + 1], None, ALU.mult).then_inc(scaled, 1)


def to_channels(nc, K, src, dst, n, scale=None, residues=False):
    pair = isinstance(dst, Pair)
    by_token = lambda x: x.rearrange("p (j t) -> p t j", t=TT) if residues else x
    by_tile = lambda x: x.rearrange("p (t j) -> p t j", t=TT) if residues else x
    with stage(nc, "turned", "rounded", "copied") as (block, (turned, rounded, copied)):
        @block.tensor
        def _(pe):
            for k in range(n):
                if k >= 8:
                    pe.wait_ge(copied, k - 7)
                for t in range(TT):
                    last = nc.tensor.transpose(K.bank[k % 8][:, t * P:(t + 1) * P], src[:, t, k * P:(k + 1) * P], K.ident[:, :])
                last.then_inc(turned, 1)

        @block.scalar
        def _(act):
            for k in range(n):
                act.wait_ge(turned, k + 1)
                s = 1.0 if scale is None else scale(k)
                out = (dst.hi if pair else dst)[:, k, 0:S]
                nc.scalar.activation(by_token(out), by_tile(K.bank[k % 8][:, :]), ACT.Copy, scale=s).then_inc(rounded if pair else copied, 1)

        @block.vector
        def _(dve):
            for k in range(n if pair else 0):
                dve.wait_ge(rounded, k + 1)
                s = 1.0 if scale is None else scale(k)
                nc.vector.scalar_tensor_tensor(out=by_token(dst.lo[:, k, 0:S]), in0=by_tile(K.bank[k % 8][:, :]), scalar=s,
                                               in1=by_token(dst.hi[:, k, 0:S].bitcast(F32)), op0=ALU.mult, op1=ALU.subtract).then_inc(copied, 1)


class Pair:

    def __init__(self, mem, nc, name, shape):
        self.hi, self.lo = (mem.enter_context(nc.sbuf_tensor(f"{name}_{part}", shape, F32R)) for part in ("hi", "lo"))


TERMS = (("hi", "hi"), ("hi", "lo"), ("lo", "hi"))


def product(nc, out, a, b, kt, first=0, total=None):
    total = kt if total is None else total
    for k in range(first, first + kt):
        for n, (pa, pb) in enumerate(TERMS):
            last = nc.tensor.matmul(out, a(pa, k), b(pb, k), start=(k == 0 and n == 0), stop=(k == total - 1 and n == len(TERMS) - 1))
    return last


def narrow_product(nc, out, w, x):
    for k in range(KD):
        for n, part in enumerate((x.hi, x.lo)):
            last = nc.tensor.matmul(out, w[:, k, :], part[:, k, :].bitcast(F32), start=(k == 0 and n == 0), stop=(k == KD - 1 and n == 1))
    return last


def part_of(pair, part):
    return pair.hi if part == "hi" else pair.lo


def split(nc, pair, src, n, name):
    with stage(nc, "rounded", "split") as (block, (rounded, is_split)):
        @block.scalar
        def _(act):
            for k in range(n):
                nc.scalar.activation(pair.hi[:, k, :], src[:, k, :], ACT.Copy).then_inc(rounded, 1)

        @block.vector
        def _(dve):
            for k in range(n):
                dve.wait_ge(rounded, k + 1)
                nc.vector.tensor_tensor(pair.lo[:, k, :], src[:, k, :], pair.hi[:, k, :].bitcast(F32), ALU.subtract).then_inc(is_split, 1)


def split_weights(nc, dve, raw, hi, lo, rounded, count):
    nc.vector.tensor_copy(hi, raw).then_inc(rounded, 1)
    dve.wait_ge(rounded, count)
    return nc.vector.tensor_tensor(lo, raw, hi.bitcast(F32), ALU.subtract)


class Job:

    def __init__(self, tiles, load, multiply, evacuate, loads=1):
        self.tiles, self.load, self.multiply, self.evacuate, self.loads = tiles, load, multiply, evacuate, loads


def columns(w, column):
    return lambda sp, raw, i, sem: sp.dma_start(raw, w[:, :, ds(column(i), CW)]).then_inc(sem, 16)


def channels_job(nc, x, kt, load, evacuate, loads=1):
    def multiply(bank, weights, m):
        return product(nc, bank[:, :], lambda part, k: weights(part)[:, k, m * P:(m + 1) * P], lambda part, k: part_of(x, part)[:, k, :], kt)

    return Job(CW // P, load, multiply, lambda bank, m, i: evacuate(bank[:, :], m, i), loads)


def tokens_job(nc, x, kt, load, evacuate, rows=lambda t: slice(t * P, (t + 1) * P)):
    def multiply(bank, weights, t):
        return product(nc, bank[:, 0:CW], lambda part, k: part_of(x, part)[:, k, rows(t)], lambda part, k: weights(part)[:, k, :], kt)

    return Job(TT, load, multiply, lambda bank, t, i: evacuate(bank[:, 0:CW], t, i))


class Beside:

    names = ()

    def scalar_before(self, act, c):
        pass

    def scalar_after(self, act, c):
        pass

    def vector(self, dve, c):
        pass


def project(nc, K, kt, jobs, passes=1, lead=(), beside=Beside()):
    n = len(jobs)
    tiles = [job.tiles for job in jobs]
    assert n % 2 == 0 and len({job.loads for job in jobs}) == 1 and (not lead or [job.tiles for job in lead] == tiles)
    loads, total = jobs[0].loads, sum(tiles)
    credit = tiles[-1] + 1
    first = 1 if lead else 0

    def sweep(eng, run):
        for c, job in enumerate(lead):
            run(c, job, 0)
        if passes == 1:
            for c, job in enumerate(jobs):
                run(c, job, first)
            return
        with eng.Fori(first, first + passes) as i:
            for c, job in enumerate(jobs):
                run(c, job, i)

    def settled(c, i):
        return i * total + (credit + sum(tiles[:c]) - tiles[c - 1])

    with ExitStack() as mem:
        raw = mem.enter_context(nc.sbuf_tensor(f"raw_{nc.next_id()}", [P, 2, kt, CW], F32))
        cut = Pair(mem, nc, f"cut_{nc.next_id()}", [P, 2, kt, CW])
        with stage(nc, "w_loaded0", "w_loaded1", "w_rounded", "w_split", "products", "read_out", *beside.names) as (
                block, (w0, w1, w_rounded, w_split, products, read_out, *beside.sems)):
            w_loaded = [w0, w1]

            @block.sync
            def _(sp):
                def run(c, job, i):
                    sp.wait_ge(w_split, i * n + c + 1)
                    job.load(sp, raw[:, c % 2], i, w_loaded[c % 2])

                sweep(sp, run)

            @block.vector
            def _(dve):
                def run(c, job, i):
                    dve.wait_ge(w_loaded[c % 2], i * (n // 2 * 16 * loads) + 16 * loads * (c // 2 + 1))
                    dve.wait_ge(products, settled(c, i))
                    split_weights(nc, dve, raw[:, c % 2], cut.hi[:, c % 2], cut.lo[:, c % 2], w_rounded, i * n + c + 1).then_inc(w_split, 1)
                    beside.vector(dve, c)

                dve.sem_inc(w_split, 2)
                sweep(dve, run)

            @block.tensor
            def _(pe):
                def run(c, job, i):
                    pe.wait_ge(w_split, i * n + c + 3)
                    pe.wait_ge(read_out, settled(c, i))
                    for m in range(job.tiles):
                        job.multiply(K.bank[c % 2 * TT + m], lambda part: part_of(cut, part)[:, c % 2], m).then_inc(products, 1)

                pe.sem_inc(products, credit)
                sweep(pe, run)

            @block.scalar
            def _(act):
                def run(c, job, i):
                    beside.scalar_before(act, c)
                    for m in range(job.tiles):
                        act.wait_ge(products, i * total + (credit + sum(tiles[:c]) + m + 1))
                        job.evacuate(K.bank[c % 2 * TT + m], m, i).then_inc(read_out, 1)
                    beside.scalar_after(act, c)

                act.sem_inc(read_out, credit)
                sweep(act, run)


def project_model(nc, K, w, kt, x, o):
    SLOTS = 3
    with ExitStack() as mem:
        raw = mem.enter_context(nc.sbuf_tensor(f"raw_{nc.next_id()}", [P, SLOTS, D], F32))
        cut = Pair(mem, nc, f"cut_{nc.next_id()}", [P, SLOTS, D])
        with stage(nc, *[f"w_loaded{s}" for s in range(SLOTS)], "w_rounded", "w_split", "products", "done", "kept") as (block, sems):
            w_loaded, (w_rounded, w_split, products, done, kept) = sems[:SLOTS], sems[SLOTS:]

            @block.sync
            def _(sp):
                for k in range(kt):
                    if k >= SLOTS:
                        sp.wait_ge(w_split, k - SLOTS + 1)
                    sp.dma_start(raw[:, k % SLOTS, :], w[k * P:(k + 1) * P, :]).then_inc(w_loaded[k % SLOTS], 16)

            @block.vector
            def _(dve):
                for k in range(kt):
                    s = k % SLOTS
                    dve.wait_ge(w_loaded[s], 16 * (k // SLOTS + 1))
                    if k >= SLOTS:
                        dve.wait_ge(products, k - SLOTS + 1)
                    split_weights(nc, dve, raw[:, s, :], cut.hi[:, s, :], cut.lo[:, s, :], w_rounded, k + 1).then_inc(w_split, 1)

            @block.tensor
            def _(pe):
                for k in range(kt):
                    pe.wait_ge(w_split, k + 1)
                    for t in range(TT):
                        for half in range(2):
                            last = product(nc, K.bank[2 * t + half][:, :], lambda part, k: part_of(x, part)[:, k, t * P:(t + 1) * P],
                                           lambda part, k: part_of(cut, part)[:, k % SLOTS, half * 512:(half + 1) * 512], 1, k, kt)
                            if k == kt - 1 and half == 0:
                                last.then_inc(done, 1)
                        if k == kt - 1:
                            last.then_inc(done, 1)
                    if k < kt - 1:
                        last.then_inc(products, 1)

            @block.scalar
            def _(act):
                for b in range(8):
                    act.wait_ge(done, b + 1)
                    nc.scalar.activation(o[:, b // 2, (b % 2) * 512:(b % 2 + 1) * 512], K.bank[b][:, :], ACT.Copy).then_inc(kept, 1)


def lru(nc, K, A, y):
    with ExitStack() as mem:
        sb = lambda n, s: mem.enter_context(nc.sbuf_tensor(n, s, F32))
        PAD = 3
        xa = sb("lru_xa", [P, KD, S + PAD])
        w = A.w_in[0].rearrange("(k p) m -> p k m", p=P)
        project(nc, K, KD, [
            channels_job(nc, K.hT, KD, columns(w, lambda i: i * CW + C_LRU_X),
                         lambda bank, m, i: nc.scalar.activation(xa[:, ds(i * 2 + m, 1), PAD:], bank, ACT.Copy)),
            channels_job(nc, K.hT, KD, columns(w, lambda i: i * CW + C_LRU_G),
                         lambda bank, m, i: nc.scalar.activation(y[:, ds(i * 2 + m, 1), :], bank, ACT.Gelu_apprx_tanh))], passes=4)
        xc, r, gi, u = (sb(f"lru_{n}", [P, KD, S]) for n in ("xc", "r", "i", "u"))
        part = sb("lru_part", [P, 2, S])
        wg = sb("lru_wg", [P, 2 * KD, P])
        sp8 = sb("lru_sp8", [P, 5, KD])
        with stage(nc, "wg_loaded", "zeroed", "opened", "tapped", "convolved", "products", "gated", "exped", "vec_step", "act_step", "rated",
                   "tanhed", "decayed", "squared", "raised", "rooted", "driven", "scaled", "scanned") as (
                block, (wg_loaded, zeroed, opened, tapped, convolved, products, gated, exped, vec_step, act_step, rated,
                        tanhed, decayed, squared, raised, rooted, driven, scaled, scanned)):
            @block.sync
            def _(sp):
                sp.dma_start(wg[:, :, :], A.lru_w_gates[0].rearrange("k n c e -> c (k n) e")).then_inc(wg_loaded, 16)

            @block.tensor
            def _(pe):
                pe.wait_ge(wg_loaded, 16)
                for j in range(2 * KD):
                    pe.wait_ge(convolved, j % KD + 1)
                    if j >= 8:
                        pe.wait_ge(gated, j - 7)
                    nc.tensor.matmul(K.bank[j % 8][:, :], wg[:, j, :], xc[:, j % KD, :], start=True, stop=True).then_inc(products, 1)

            @block.scalar
            def _(act):
                done = Settle(act, act_step)
                done(nc.scalar.activation(sp8[:, 0, :], vcol(K, "lam", 0, KD), ACT.Abs))
                done(nc.scalar.activation(sp8[:, 0, :], sp8[:, 0, :], ACT.Exp, scale=-1.0))
                done(nc.scalar.activation(sp8[:, 0, :], sp8[:, 0, :], ACT.Ln, bias=1.0))
                nc.scalar.activation(sp8[:, 1, :], vcol(K, "lam", 0, KD), ACT.Relu, scale=-1.0).then_inc(exped, 1)
                act.wait_ge(zeroed, 1)
                for n in range(KD):
                    nc.scalar.activation(xc[:, n, :], xa[:, n, 0:S], ACT.Identity, scale=vcol(K, "conv_w", n), bias=vcol(K, "conv_b", n)).then_inc(opened, 1)
                for j in range(2 * KD):
                    act.wait_ge(products, j + 1)
                    dst = r if j < KD else gi
                    nc.scalar.activation(dst[:, j % KD, :], K.bank[j % 8][:, :], ACT.Sigmoid, bias=vcol(K, "lru_b", j)).then_inc(gated, 1)
                act.wait_ge(rated, 1)
                act.wait_ge(gated, KD)
                for n in range(KD):
                    nc.scalar.activation(u[:, n, :], r[:, n, :], ACT.Tanh, scale=sp8[:, 3, n:n + 1]).then_inc(tanhed, 1)
                act.wait_ge(tanhed, KD)
                for n in range(KD):
                    nc.scalar.activation(r[:, n, :], r[:, n, :], ACT.Exp, scale=sp8[:, 4, n:n + 1]).then_inc(decayed, 1)
                for n in range(KD):
                    act.wait_ge(raised, n + 1)
                    nc.scalar.activation(u[:, n, :], u[:, n, :], ACT.Sqrt).then_inc(rooted, 1)

            @block.gpsimd
            def _(pool):
                for n in range(KD):
                    pool.wait_ge(gated, KD + n + 1)
                    nc.gpsimd.tensor_tensor(gi[:, n, :], gi[:, n, :], xc[:, n, :], ALU.mult).then_inc(driven, 1)
                for n in range(KD):
                    pool.wait_ge(decayed, n + 1)
                    if n >= 2:
                        pool.wait_ge(raised, n - 1)
                    nc.gpsimd.tensor_tensor(part[:, n % 2, :], r[:, n, :], r[:, n, :], ALU.mult).then_inc(squared, 1)
                for n in range(KD):
                    pool.wait_ge(scanned, n + 1)
                    nc.gpsimd.tensor_tensor(y[:, n, :], y[:, n, :], xc[:, n, :], ALU.mult)

            @block.vector
            def _(dve):
                done = Settle(dve, vec_step)
                nc.vector.memset(xa[:, :, 0:PAD], 0.0).then_inc(zeroed, 1)
                dve.wait_ge(exped, 1)
                dve.wait_ge(act_step, 3)
                done(nc.vector.tensor_tensor(sp8[:, 2, :], sp8[:, 0, :], sp8[:, 1, :], ALU.add))
                nc.vector.tensor_scalar(sp8[:, 3, :], sp8[:, 2, :], 8.0, None, ALU.mult).then_inc(vec_step, 1)
                done(nc.vector.tensor_scalar(sp8[:, 4, :], sp8[:, 2, :], -8.0, None, ALU.mult))
                done.n += 1
                dve.wait_ge(vec_step, done.n)
                dve.sem_inc(rated, 1)
                for n0 in range(0, KD, 2):
                    for j in range(1, 4):
                        for n in (n0, n0 + 1):
                            if j == 1:
                                dve.wait_ge(opened, n + 1)
                            else:
                                dve.wait_ge(tapped, (n0 // 2) * 4 + (j - 2) * 2 + n - n0 + 1)
                            nc.vector.scalar_tensor_tensor(out=xc[:, n, :], in0=xa[:, n, j:j + S], scalar=vcol(K, "conv_w", j * KD + n),
                                                           in1=xc[:, n, :], op0=ALU.mult, op1=ALU.add).then_inc(tapped if j < 3 else convolved, 1)
                for n in range(KD):
                    dve.wait_ge(squared, n + 1)
                    nc.vector.scalar_tensor_tensor(out=u[:, n, :], in0=part[:, n % 2, :], scalar=1.0, in1=u[:, n, :],
                                                   op0=ALU.add, op1=ALU.mult).then_inc(raised, 1)
                dve.wait_ge(driven, KD)
                for n in range(KD):
                    dve.wait_ge(rooted, n + 1)
                    nc.vector.tensor_tensor(u[:, n, :], u[:, n, :], gi[:, n, :], ALU.mult).then_inc(scaled, 1)
                    dve.wait_ge(scaled, n + 1)
                    nc.vector.tensor_tensor_scan(xc[:, n, :], r[:, n, :], u[:, n, :], 0.0, ALU.mult, ALU.add).then_inc(scanned, 1)


class Names:
    pass


def rel_bias_constants():
    n = np.arange(S)
    large = 16 + (np.log(np.maximum(n, 16).astype(np.float32) / np.float32(16)) / np.float32(np.log(128 / 16))
                  * np.float32(16)).astype(np.int32)
    bucket = np.where(n < 16, n, np.minimum(large, 31))
    oh = np.zeros((33, GW), np.float32)
    oh[bucket[S - 1 - np.arange(S)], np.arange(S)] = 1.0
    oh[32, S:] = NEG
    return oh


GW = 640
N_CMP = 31
HD = 64


def rel_bias(nc, K, A):
    K.bias_rows = nc.dram_tensor("bias_rows", (16, GW), F32, kind="Internal").ap()
    oh_dram = nc.inline_tensor(rel_bias_constants(), name="bucket_onehot").ap()
    with ExitStack() as mem:
        sb = lambda n, s: mem.enter_context(nc.sbuf_tensor(n, s, F32))
        oh, table, rows = sb("bucket_oh", [33, GW]), sb("rel_table33", [33, 16]), sb("bias_sb", [16, GW])
        with stage(nc, "loaded", "set", "products", "copied", "stored") as (block, (loaded, is_set, products, copied, stored)):
            @block.vector
            def _(dve):
                nc.vector.memset(table[:, :], 1.0).then_inc(is_set, 1)

            @block.sync
            def _(sp):
                sp.dma_start(oh[:, :], oh_dram).then_inc(loaded, 16)
                sp.wait_ge(is_set, 1)
                sp.dma_start(table[0:32, :], A.rel_table).then_inc(loaded, 16)
                sp.wait_ge(copied, 2)
                sp.dma_start(K.bias_rows, rows[:, :]).then_inc(stored, 16)
                sp.wait_ge(stored, 16)

            @block.tensor
            def _(pe):
                pe.wait_ge(loaded, 32)
                for b, (lo, hi) in enumerate(((0, S), (S, GW))):
                    nc.tensor.matmul(K.bank[b][0:16, 0:hi - lo], table[:, :], oh[:, lo:hi], start=True, stop=True).then_inc(products, 1)

            @block.scalar
            def _(act):
                for b, (lo, hi) in enumerate(((0, S), (S, GW))):
                    act.wait_ge(products, b + 1)
                    nc.scalar.activation(rows[:, lo:hi], K.bank[b][0:16, 0:hi - lo], ACT.Copy).then_inc(copied, 1)


def compressed(nc, K, A, src, kcT, vc):
    J = 16
    HJ = J // 2
    NC16 = S // 16
    with ExitStack() as mem:
        tmp = lambda n, s: mem.enter_context(nc.sbuf_tensor(f"cmp_{n}", s, F32))
        w1 = tmp("w1", [P, 2, J, 256])
        w2 = tmp("w2", [P, 2, 2, HD])
        pos_rows, pos = tmp("pos_rows", [2 * J, P]), tmp("pos", [P, 2, J])
        offsets = tmp("offsets", [P, 2, 4, NC16, HJ])
        withpos = tmp("withpos", [P, 2, 2, 4, NC16, HJ])
        hid = tmp("hid", [P, 2, 2, 2, 2, N_CMP])
        with stage(nc, "loaded", "w1_loaded0", "w1_loaded1", "turned", "vec_step", "moved", "added", "products", "acted", "outputs", "stored") as (
                block, (loaded, w1_loaded0, w1_loaded1, turned, vec_step, moved, added, products, acted, outputs, stored)):
            w1_loaded = (w1_loaded0, w1_loaded1)

            @block.sync
            def _(sp):
                sp.dma_start(pos_rows[:, :], A.cmp_pos[0].rearrange("k (j q) d -> (k j) (q d)", q=2)).then_inc(loaded, 16)
                for kind in range(2):
                    sp.dma_start(w1[:, kind], A.cmp_w1[0, kind].rearrange("(j p) m -> p j m", p=P)).then_inc(w1_loaded[kind], 16)
                    sp.dma_start(w2[:, kind], A.cmp_w2[0, kind].rearrange("(h p) d -> p h d", p=P)).then_inc(w1_loaded[kind], 16)

            @block.tensor
            def _(pe):
                pe.wait_ge(loaded, 16)
                nc.tensor.transpose(K.bank[0][:, 0:2 * J], pos_rows[:, :], K.ident[0:2 * J, 0:2 * J]).then_inc(turned, 1)
                for kind in range(2):
                    pe.wait_ge(w1_loaded[kind], 32)
                    pe.wait_ge(added, 2 * kind + 2)
                    for h in range(2):
                        for j in range(J):
                            half = j // HJ
                            last = nc.tensor.matmul(K.bank[1 + 2 * kind + h][:, 0:4 * N_CMP].rearrange("p (g c) -> p g c", g=4),
                                                    w1[:, kind, j, h * P:(h + 1) * P], withpos[:, kind, half, :, half:half + N_CMP, j % HJ],
                                                    start=(j == 0), stop=(j == J - 1))
                        last.then_inc(products, 1)
                for kind in range(2):
                    pe.wait_ge(acted, 2 * kind + 2)
                    for a in range(2):
                        if kind == 0:
                            for h in range(2):
                                last = nc.tensor.matmul(K.bank[5 + a][a * HD:(a + 1) * HD, 0:2 * N_CMP], w2[:, kind, h, :],
                                                        hid[:, kind, h, a, :, :].rearrange("p g c -> p (g c)"), start=(h == 0), stop=(h == 1))
                        else:
                            for g in range(2):
                                for h in range(2):
                                    last = nc.tensor.matmul(K.bank[(7 + a) % 8][0:N_CMP, g * HD:(g + 1) * HD], hid[:, kind, h, a, g, :],
                                                            w2[:, kind, h, :], start=(h == 0), stop=(h == 1))
                        last.then_inc(outputs, 1)

            @block.vector
            def _(dve):
                done = Settle(dve, vec_step)
                dve.wait_ge(turned, 1)
                done(nc.vector.tensor_copy(pos[:, :, :].rearrange("p k j -> p (k j)"), K.bank[0][:, 0:2 * J]))
                for kind in range(2):
                    dve.wait_ge(moved, 4 * (kind + 1))
                    for half in range(2):
                        shape = [P, 4 * NC16, HJ]
                        nc.vector.tensor_tensor(withpos[:, kind, half].rearrange("p g c j -> p (g c) j"),
                                                offsets[:, kind].rearrange("p g c j -> p (g c) j"),
                                                pos[:, kind, half * HJ:(half + 1) * HJ].unsqueeze(1).broadcast_to(shape), ALU.add).then_inc(added, 1)

            @block.scalar
            def _(act):
                for kind in range(2):
                    for a in range(2):
                        for q in range(2):
                            nc.scalar.activation(offsets[q * HD:(q + 1) * HD, kind, 2 * a:2 * a + 2].rearrange("p g c j -> p g (c j)"),
                                                 src[a * HD:(a + 1) * HD, 2 * kind:2 * kind + 2, q:S:2], ACT.Copy).then_inc(moved, 1)
                for kind in range(2):
                    for h in range(2):
                        act.wait_ge(products, 2 * kind + h + 1)
                        nc.scalar.activation(hid[:, kind, h].rearrange("p a g c -> p (a g c)"), K.bank[1 + 2 * kind + h][:, 0:4 * N_CMP],
                                             ACT.Gelu_apprx_tanh).then_inc(acted, 1)
                for a in range(2):
                    act.wait_ge(outputs, a + 1)
                    nc.scalar.activation(kcT[a * HD:(a + 1) * HD, :, :].rearrange("p g c -> p (g c)"),
                                         K.bank[5 + a][a * HD:(a + 1) * HD, 0:2 * N_CMP], ACT.Copy).then_inc(stored, 1)
                for a in range(2):
                    act.wait_ge(outputs, a + 3)
                    nc.scalar.activation(vc[:, a, :, :].rearrange("c g d -> c (g d)"), K.bank[(7 + a) % 8][0:N_CMP, 0:2 * HD],
                                         ACT.Copy).then_inc(stored, 1)


def nsa(nc, K, A, y):
    w = A.w_in[0].rearrange("(k p) m -> p k m", p=P)
    rel_bias(nc, K, A)
    with ExitStack() as mem:
        sb = lambda n, s: mem.enter_context(nc.sbuf_tensor(n, s, F32))
        qT = sb("nsa_q", [P, 8, S])
        kT = sb("nsa_k", [P, 4, S])
        v = sb("nsa_v", [P, TT, 2 * CW])
        gate = sb("nsa_gate", [P, TT, 48])
        kcT = sb("nsa_kc", [P, 2, N_CMP])
        vc = sb("nsa_vc", [N_CMP, 2, 2, HD])
        with ExitStack() as inner:
            cmpT = inner.enter_context(nc.sbuf_tensor("nsa_cmp", [P, 4, S], F32))
            jobs = []
            for c in range(2):
                jobs.append(channels_job(nc, K.hT, KD, columns(w, lambda i, c=c: C_KV + c * CW),
                                         lambda bank, m, i, c=c: nc.scalar.activation(cmpT[:, 2 * c + m, :], bank, ACT.Copy)))
            for c in range(2):
                jobs.append(channels_job(nc, K.hT, KD, columns(w, lambda i, c=c: C_KV + 512 + c * 512),
                                         lambda bank, m, i, c=c: nc.scalar.activation(kT[:, 2 * c + m, :], bank, ACT.Copy)))
            for c in range(2):
                jobs.append(tokens_job(nc, K.hT, KD, columns(w, lambda i, c=c: C_KV + 768 + c * 512),
                                       lambda bank, t, i, c=c: nc.scalar.activation(v[:, t, c * CW:(c + 1) * CW], bank, ACT.Copy)))
            project(nc, K, KD, jobs)
            compressed(nc, K, A, cmpT, kcT, vc)
        nsa_queries(nc, K, w, qT)
        nsa_gates(nc, K, w, gate)
        for gp in range(2):
            nsa_attend(nc, K, gp, qT, kT, v, gate, kcT, vc, y)


def backwards(ap):
    (step, n), axes = ap.ap[-1], list(ap.ap[:-1])
    return bass.AP(ap.tensor, ap.offset + step * (n - 1), [*axes, [-step, n]])


def nsa_queries(nc, K, w, qT):
    def load_heads(pair):
        def load(sp, raw, gp, sem):
            for r in range(2):
                for a in range(2):
                    first = C_Q + a * CW + (2 * pair + r) * HD
                    to = (2 * r + a) * HD
                    sp.dma_start(raw[:, :, to:to + HD], w[:, :, ds(gp * 512 + first, HD)]).then_inc(sem, 16)
        return load

    project(nc, K, KD, [
        channels_job(nc, K.hT, KD, load_heads(pair),
                     lambda bank, m, gp, pair=pair: nc.scalar.activation(qT[:, ds(gp * 4 + 2 * pair + m, 1), :], bank, ACT.Copy, scale=HD ** -0.5),
                     loads=4)
        for pair in range(2)], passes=2)


def nsa_gates(nc, K, w, gate):
    with ExitStack() as mem:
        sb = lambda n, s: mem.enter_context(nc.sbuf_tensor(f"gates_{n}", s, F32))
        raw, turn, before = sb("raw", [P, KD, 48]), sb("turn", [P, P]), sb("before", [P, TT * 48])
        cut = Pair(mem, nc, "gates_cut", [P, KD, 48])
        with stage(nc, "loaded", "rounded", "is_split", "turn_set", "product", "squashed", "reversed", "kept") as (
                block, (loaded, rounded, is_split, turn_set, product_ready, squashed, is_reversed, kept)):
            @block.sync
            def _(sp):
                sp.dma_start(raw[:, :, :], w[:, :, C_GATE:C_GATE + 48]).then_inc(loaded, 16)

            @block.gpsimd
            def _(pool):
                nc.gpsimd.memset(turn[:, :], 0.0).then_inc(turn_set, 1)
                pool.wait_ge(turn_set, 1)
                nc.gpsimd.affine_select(out=turn[:, :], in_=turn[:, :], compare_op=ALU.not_equal, fill=1.0, base=1 - P,
                                        pattern=[[1, P]], channel_multiplier=1).then_inc(turn_set, 1)

            @block.vector
            def _(dve):
                dve.wait_ge(loaded, 16)
                split_weights(nc, dve, raw[:, :, :], cut.hi[:, :, :], cut.lo[:, :, :], rounded, 1).then_inc(is_split, 1)

            @block.tensor
            def _(pe):
                pe.wait_ge(is_split, 1)
                for t in range(TT):
                    last = product(nc, K.bank[0][:, t * 48:(t + 1) * 48], lambda part, k: part_of(K.hT, part)[:, k, t * P:(t + 1) * P],
                                   lambda part, k: part_of(cut, part)[:, k, :], KD)
                last.then_inc(product_ready, 1)
                pe.wait_ge(turn_set, 2)
                pe.wait_ge(squashed, 1)
                nc.tensor.matmul(K.bank[1][:, 0:TT * 48], turn[:, :], before[:, :], start=True, stop=True).then_inc(is_reversed, 1)

            @block.scalar
            def _(act):
                act.wait_ge(product_ready, 1)
                nc.scalar.activation(before[:, :], K.bank[0][:, 0:TT * 48], ACT.Sigmoid).then_inc(squashed, 1)
                act.wait_ge(is_reversed, 1)
                nc.scalar.activation(gate[:, :, :].rearrange("p t c -> p (t c)"), K.bank[1][:, 0:TT * 48], ACT.Copy).then_inc(kept, 1)


def nsa_attend(nc, K, gp, qT, kT, v, gate, kcT, vc, y):
    UNITS = [(it, a, i) for it in range(4) for a in range(2) for i in range(TT)]
    U = 2 * TT
    N = len(UNITS)
    with ExitStack() as mem:
        sb = lambda n, s: mem.enter_context(nc.sbuf_tensor(f"at{gp}_{n}", s, F32))
        bias = sb("bias", [P, 8, S])
        wbias = sb("wbias", [P, 8, 3 * P])
        pair = sb("pair", [P, 2, 2, S + 3 * P])
        far = sb("far", [P, P])
        seen = sb("seen", [P, 1])
        q = sb("q", [P, 2, S])
        logit = sb("logit", [P, 2, 2 * S])
        prob = sb("prob", [P, 3, 2 * S])
        probT = sb("probT", [P, 2, 2 * S])
        stat = sb("stat", [P, 2, 4, 3])
        CB = 896
        with stage(nc, "loaded", "masked", "prepared", "staged", "scored", "biased", "exped", "weighted", "turned", "copied",
                   "valued", "kept", "vec_step", "paired", "opened") as (
                block, (loaded, masked, prepared, staged, scored, biased, exped, weighted, turned, copied, valued, kept, vec_step,
                        paired, opened)):
            def shape(i):
                n = (i + 1) * P
                return n, min(n, 3 * P), 7 + 8 * i

            @block.sync
            def _(sp):
                src = bass.AP(K.bias_rows.tensor, gp * 8 * GW, [[1, P], [GW, 8], [1, S]])
                sp.dma_start(bias[:, :, :], src).then_inc(loaded, 16)

            @block.gpsimd
            def _(pool):
                nc.gpsimd.memset(far[:, :], 0.0).then_inc(masked, 1)
                nc.gpsimd.memset(seen[:, :], 1.0).then_inc(masked, 1)
                pool.wait_ge(masked, 2)
                nc.gpsimd.affine_select(out=far[:, :], in_=far[:, :], compare_op=ALU.is_gt, fill=NEG, base=1 - P,
                                        pattern=[[1, P]], channel_multiplier=1).then_inc(masked, 1)
                nc.gpsimd.affine_select(out=seen[:, :], in_=seen[:, :], compare_op=ALU.is_ge, fill=0.0,
                                        base=(P - 1) - (2 * 16 - 1), pattern=[[0, 1]], channel_multiplier=-1).then_inc(masked, 1)
                pool.wait_ge(prepared, 2)
                for it in range(4):
                    for a in range(2):
                        if it >= 2:
                            pool.wait_ge(biased, (it - 2) * U + TT * (a + 1))
                        nc.gpsimd.tensor_copy(pair[:, it % 2, a, 0:S], bias[:, it + a * 4, :])
                        nc.gpsimd.tensor_copy(pair[:, it % 2, a, S:], wbias[:, it + a * 4, :]).then_inc(paired, 1)

            @block.tensor
            def _(pe):
                pe.wait_ge(prepared, 2)
                for step in range(N + 3):
                    if step < N:
                        u = step
                        it, a, i = UNITS[u]
                        n, nw, ncmp = shape(i)
                        rows = slice(a * HD, (a + 1) * HD)
                        b0, b1 = K.bank[2 * (u % 2)], K.bank[2 * (u % 2) + 1]
                        if u % U == 0:
                            pe.wait_ge(staged, it + 1)
                        if u >= 2:
                            pe.wait_ge(biased, u - 1)
                        qs = q[rows, it % 2, i * P:(i + 1) * P]
                        nc.tensor.matmul(b0[:, 0:n], qs, kT[rows, gp, 0:n], start=True, stop=True)
                        nc.tensor.matmul(b1[:, 0:nw], qs, kT[rows, 2 + gp, n - nw:n], start=True, stop=True)
                        nc.tensor.matmul(b1[:, CB - S:CB - S + ncmp], qs, kcT[rows, gp, 0:ncmp], start=True, stop=True).then_inc(scored, 1)
                    if 2 <= step <= N + 1:
                        u = step - 2
                        it, a, i = UNITS[u]
                        n, nw, ncmp = shape(i)
                        pr = prob[:, u % 3, :]
                        pe.wait_ge(weighted, u + 1)
                        if u >= 1:
                            pe.wait_ge(copied, u)
                        for j in range(n // P):
                            nc.tensor.transpose(K.bank[4][:, j * P:(j + 1) * P], pr[:, j * P:(j + 1) * P], K.ident[:, :])
                        for j in range(nw // P):
                            nc.tensor.transpose(K.bank[5][:, j * P:(j + 1) * P], pr[:, S + j * P:S + (j + 1) * P], K.ident[:, :])
                        nc.tensor.transpose(K.bank[5][0:ncmp, 3 * P:S], pr[:, CB:CB + ncmp], K.ident[:, :]).then_inc(turned, 1)
                    if step >= 3:
                        u = step - 3
                        it, a, i = UNITS[u]
                        n, nw, ncmp = shape(i)
                        rows = slice(a * HD, (a + 1) * HD)
                        g = 2 * gp + a
                        pt = probT[:, u % 2, :]
                        pe.wait_ge(copied, u + 1)
                        if u % U == 0 and it >= 2:
                            pe.wait_ge(kept, it - 1)
                        o = K.bank[6 + it % 2][rows, i * P:(i + 1) * P]
                        for j in range(n // P):
                            nc.tensor.matmul(o, v[:, j, g * HD:(g + 1) * HD], pt[:, j * P:(j + 1) * P], start=(j == 0), stop=False)
                        for j in range(nw // P):
                            nc.tensor.matmul(o, v[:, (n - nw) // P + j, CW + g * HD:CW + (g + 1) * HD],
                                             pt[:, S + j * P:S + (j + 1) * P], start=False, stop=False)
                        nc.tensor.matmul(o, vc[0:ncmp, a, gp, :], pt[0:ncmp, S + 3 * P:2 * S], start=False, stop=True).then_inc(valued, 1)

            @block.vector
            def _(dve):
                dve.wait_ge(loaded, 16)
                dve.wait_ge(masked, 4)
                nc.vector.tensor_copy(wbias[:, :, :], bias[:, :, P:S]).then_inc(prepared, 1)
                dve.wait_ge(prepared, 1)
                nc.vector.tensor_tensor(wbias[:, :, 0:P], bias[:, :, P:2 * P], far[:, :].unsqueeze(1).broadcast_to([P, 8, P]), ALU.add).then_inc(prepared, 1)
                dve.wait_ge(prepared, 2)
                done = Settle(dve, vec_step)
                for step in range(N + 1):
                    if step < N:
                        u = step
                        it, a, i = UNITS[u]
                        n, nw, ncmp = shape(i)
                        b0, b1 = K.bank[2 * (u % 2)], K.bank[2 * (u % 2) + 1]
                        lg, st = logit[:, u % 2, :], stat[:, u % 2]
                        dve.wait_ge(scored, u + 1)
                        if i == 0:
                            dve.wait_ge(paired, it * 2 + a + 1)
                        dve.sem_inc(opened, 1)
                        cc = 415 - P * i
                        for k, (dst, src, bb) in enumerate((
                                (lg[:, 0:n], b0[:, 0:n], pair[:, it % 2, a, S - n:S]),
                                (lg[:, S:S + nw], b1[:, 0:nw], pair[:, it % 2, a, S + 3 * P - nw:S + 3 * P]),
                                (lg[:, CB:CB + ncmp], b1[:, CB - S:CB - S + ncmp], pair[:, it % 2, a, cc:cc + 16 * (ncmp - 1) + 1:16]))):
                            ins = nc.vector.tensor_tensor_reduce(out=dst, in0=src, in1=bb, scale=1.0, scalar=-3e38,
                                                                 op0=ALU.add, op1=ALU.max, accum_out=st[:, 0, k:k + 1])
                        done(ins)
                        nc.vector.tensor_scalar(st[:, 1, :], st[:, 0, :], -1.0, None, ALU.mult).then_inc(biased, 1)
                    if step >= 1:
                        u = step - 1
                        it, a, i = UNITS[u]
                        n, nw, ncmp = shape(i)
                        pr, st = prob[:, u % 3, :], stat[:, u % 2]
                        dve.wait_ge(exped, u + 1)
                        done(nc.vector.reciprocal(st[:, 2, :], st[:, 2, :]))
                        gcol = gate[:, i, :].rearrange("p (b h) -> p b h", b=3)[:, :, it + (2 * gp + a) * 4]
                        done(nc.vector.tensor_tensor(st[:, 3, :], st[:, 2, :], gcol, ALU.mult))
                        if i == 0:
                            done(nc.vector.tensor_tensor(st[:, 3, 0:1], st[:, 3, 0:1], seen[:, :], ALU.mult))
                        nc.vector.tensor_scalar(pr[:, 0:n], pr[:, 0:n], st[:, 3, 1:2], None, ALU.mult)
                        nc.vector.tensor_scalar(pr[:, S:S + nw], pr[:, S:S + nw], st[:, 3, 2:3], None, ALU.mult)
                        nc.vector.tensor_scalar(pr[:, CB:CB + ncmp], pr[:, CB:CB + ncmp], st[:, 3, 0:1], None, ALU.mult).then_inc(weighted, 1)

            @block.scalar
            def _(act):
                def stage_queries(it):
                    nc.scalar.activation(backwards(q[:, it % 2, :].rearrange("p (t n) -> p t n", t=TT)),
                                         qT[:, it + gp * 4, :].rearrange("p (t n) -> p t n", t=TT), ACT.Copy).then_inc(staged, 1)

                def keep_outputs(it):
                    act.wait_ge(valued, it * U + U)
                    nc.scalar.activation(y[:, it + gp * 4, :].rearrange("p (t n) -> p t n", t=TT),
                                         backwards(K.bank[6 + it % 2][:, :].rearrange("p (t n) -> p t n", t=TT)), ACT.Copy).then_inc(kept, 1)

                stage_queries(0)
                for step in range(N + 2):
                    if step < N:
                        u = step
                        it, a, i = UNITS[u]
                        n, nw, ncmp = shape(i)
                        lg, pr, st = logit[:, u % 2, :], prob[:, u % 3, :], stat[:, u % 2]
                        act.wait_ge(biased, u + 1)
                        if u >= 3:
                            act.wait_ge(turned, u - 2)
                        nc.scalar.activation(pr[:, 0:n], lg[:, 0:n], ACT.Exp, bias=st[:, 1, 0:1], accum_out=st[:, 2, 1:2])
                        nc.scalar.activation(pr[:, S:S + nw], lg[:, S:S + nw], ACT.Exp, bias=st[:, 1, 1:2], accum_out=st[:, 2, 2:3])
                        nc.scalar.activation(pr[:, CB:CB + ncmp], lg[:, CB:CB + ncmp], ACT.Exp, bias=st[:, 1, 2:3],
                                             accum_out=st[:, 2, 0:1]).then_inc(exped, 1)
                        if u % U == TT and it < 3:
                            stage_queries(it + 1)
                    if step >= 2:
                        u = step - 2
                        it, a, i = UNITS[u]
                        n, nw, ncmp = shape(i)
                        pt = probT[:, u % 2, :]
                        act.wait_ge(turned, u + 1)
                        if u >= 2:
                            act.wait_ge(valued, u - 1)
                        nc.scalar.activation(pt[:, 0:n], K.bank[4][:, 0:n], ACT.Copy)
                        nc.scalar.activation(pt[:, S:S + nw], K.bank[5][:, 0:nw], ACT.Copy)
                        nc.scalar.activation(pt[0:ncmp, S + 3 * P:2 * S], K.bank[5][0:ncmp, 3 * P:S], ACT.Copy).then_inc(copied, 1)
                    if step % U == 3 and step > U:
                        keep_outputs(step // U - 1)
                keep_outputs(3)


GH, GC = 4, 32
DV = 256
NC = S // GC
PER_TILE = P // GC


def chunk_mask():
    i = np.arange(P)
    return ((i[:, None] // GC == i[None, :] // GC) & (i[:, None] <= i[None, :])).astype(np.float32)


def gla(nc, K, A, y):
    w = A.w_in[0].rearrange("(k p) m -> p k m", p=P)
    mask_dram = nc.inline_tensor(chunk_mask(), name="gla_chunk_mask").ap()
    with ExitStack() as mem:
        sb = lambda n, s: mem.enter_context(nc.sbuf_tensor(f"gla_{n}", s, F32))
        qt, kt = sb("qt", [P, GH, S]), sb("kt", [P, GH, S])
        ke = sb("ke", [P, GH, S])
        decay = sb("decay", [P, GH, NC])
        gla_keys(nc, K, A, w, qt, kt, ke, decay)
        vog = sb("vog", [P, TT, 2 * D])
        project(nc, K, KD, [
            tokens_job(nc, K.hT, KD, columns(w, lambda i, c=c: i * (2 * CW) + (C_GLA_V + c * CW)),
                       lambda bank, t, i, c=c: nc.scalar.activation(vog[:, t, ds(i * (2 * CW) + c * CW, CW)], bank, ACT.Copy))
            for c in range(2)], passes=4)
        mask = sb("mask", [P, P])
        attm = sb("attm", [P, 2, GH, P])
        keT = sb("keT", [P, 2, GH, P])
        state = sb("state", [P, 2, GH, DV])
        o = sb("o", [P, TT, D])
        ss = sb("ss", [P, 2, TT, GH])
        junk = sb("junk", [P, DV])
        with stage(nc, "loaded", "zeroed", "attended", "masked", "turned", "copied", "outer", "updated", "inter", "squared",
                   "kept", "gated", "vec_step", "rooted") as (
                block, (loaded, zeroed, attended, masked, turned, copied, outer, updated, inter, squared, kept, gated, vec_step, rooted)):
            @block.sync
            def _(sp):
                sp.dma_start(mask[:, :], mask_dram).then_inc(loaded, 16)

            @block.tensor
            def _(pe):
                for t in range(TT):
                    toks = slice(t * P, (t + 1) * P)
                    if t:
                        pe.wait_ge(masked, t)
                    for h in range(GH):
                        last = nc.tensor.matmul(K.bank[0][:, h * P:(h + 1) * P], kt[:, h, toks], qt[:, h, toks], start=True, stop=True)
                    last.then_inc(attended, 1)
                    if t:
                        pe.wait_ge(copied, t)
                    for h in range(GH):
                        last = nc.tensor.transpose(K.bank[1][:, h * P:(h + 1) * P], ke[:, h, toks], K.ident[:, :])
                    last.then_inc(turned, 1)
                    pe.wait_ge(masked, t + 1)
                    if t:
                        pe.wait_ge(kept, t)
                    for h in range(GH):
                        nc.tensor.matmul(K.bank[2 + h // 2][:, (h % 2) * DV:(h % 2 + 1) * DV], attm[:, t % 2, h, :],
                                         vog[:, t, h * DV:(h + 1) * DV], start=(h % 2 == 0), stop=False, skip_group_check=True)
                    pe.wait_ge(copied, t + 1)
                    for j in range(PER_TILE):
                        n = t * PER_TILE + j
                        rows = slice(j * GC, (j + 1) * GC)
                        if n:
                            pe.wait_ge(updated, n)
                        for h in range(GH):
                            last = nc.tensor.matmul(K.bank[4 + h // 2][:, (h % 2) * DV:(h % 2 + 1) * DV], keT[rows, t % 2, h, :],
                                                    vog[rows, t, h * DV:(h + 1) * DV], start=True, stop=True)
                        last.then_inc(outer, 1)
                        if n:
                            for h in range(GH):
                                last = nc.tensor.matmul(K.bank[2 + h // 2][rows, (h % 2) * DV:(h % 2 + 1) * DV],
                                                        qt[:, h, n * GC:(n + 1) * GC], state[:, n % 2, h, :],
                                                        start=False, stop=(j == PER_TILE - 1), skip_group_check=True)
                            last.then_inc(inter, 1)

            @block.vector
            def _(dve):
                done = Settle(dve, vec_step)
                dve.wait_ge(loaded, 16)
                nc.vector.memset(state[:, 0], 0.0).then_inc(zeroed, 1)
                dve.wait_ge(zeroed, 1)
                for t in range(TT):
                    dve.wait_ge(attended, t + 1)
                    nc.vector.tensor_tensor(attm[:, t % 2], K.bank[0][:, :].rearrange("p (h c) -> p h c", h=GH),
                                            mask[:, :].unsqueeze(1).broadcast_to([P, GH, P]), ALU.mult).then_inc(masked, 1)
                    for j in range(PER_TILE):
                        n = t * PER_TILE + j
                        dve.wait_ge(outer, n + 1)
                        if n:
                            dve.wait_ge(updated, n)
                        if n >= 2:
                            dve.wait_ge(inter, n - 1)
                        for h in range(GH):
                            last = nc.vector.scalar_tensor_tensor(out=state[:, (n + 1) % 2, h, :], in0=state[:, n % 2, h, :],
                                                                  scalar=decay[:, h, n:n + 1],
                                                                  in1=K.bank[4 + h // 2][:, (h % 2) * DV:(h % 2 + 1) * DV],
                                                                  op0=ALU.mult, op1=ALU.add)
                        last.then_inc(updated, 1)
                    dve.wait_ge(inter, t * PER_TILE + PER_TILE - 1)
                    for b in range(2):
                        last = nc.vector.tensor_copy(o[:, t, b * 2 * DV:(b + 1) * 2 * DV], K.bank[2 + b][:, :])
                    last.then_inc(kept, 1)
                dve.wait_ge(squared, TT * GH)
                done(nc.vector.tensor_scalar(ss[:, 1], ss[:, 0], 1.0 / DV, EPS, ALU.mult, ALU.add))
                dve.wait_ge(rooted, 1)
                done(nc.vector.reciprocal(ss[:, 1], ss[:, 0]))
                dve.wait_ge(gated, 1)
                dve.wait_ge(kept, TT)
                for t in range(TT):
                    for h in range(GH):
                        cols = slice(h * DV, (h + 1) * DV)
                        nc.vector.scalar_tensor_tensor(out=o[:, t, cols], in0=o[:, t, cols], scalar=ss[:, 1, t, h:h + 1],
                                                       in1=vog[:, t, h * DV + D:h * DV + D + DV], op0=ALU.mult, op1=ALU.mult)

            @block.scalar
            def _(act):
                nc.scalar.activation(vog[:, :, D:2 * D], vog[:, :, D:2 * D], ACT.Silu).then_inc(gated, 1)
                for t in range(TT):
                    act.wait_ge(turned, t + 1)
                    nc.scalar.activation(keT[:, t % 2].rearrange("p h d -> p (h d)"), K.bank[1][:, :], ACT.Copy).then_inc(copied, 1)
                    act.wait_ge(kept, t + 1)
                    for h in range(GH):
                        if t + h:
                            act.wait_ge(squared, t * GH + h)
                        nc.scalar.activation(junk[:, :], o[:, t, h * DV:(h + 1) * DV], ACT.Square,
                                             accum_out=ss[:, 0, t, h:h + 1]).then_inc(squared, 1)
                act.wait_ge(vec_step, 1)
                nc.scalar.activation(ss[:, 0], ss[:, 1], ACT.Sqrt).then_inc(rooted, 1)
        to_channels(nc, K, o, y, KD, lambda k: vcol(K, "gla_norm", k % 2))


def gla_keys(nc, K, A, w, qt, kt, ke, decay):
    with ExitStack() as mem:
        sb = lambda n, s: mem.enter_context(nc.sbuf_tensor(f"glak_{n}", s, F32))
        qk = sb("qk", [P, 2 * GH, S])
        project(nc, K, KD, [
            channels_job(nc, K.hT, KD, columns(w, lambda i, c=c: i * (2 * CW) + (C_GLA_Q + c * CW)),
                         lambda bank, m, i, c=c: nc.scalar.activation(qk[:, ds(i * 4 + 2 * c + m, 1), :], bank, ACT.Copy))
            for c in range(2)], passes=2)
        wlr, lr, wa2 = sb("wlr", [P, KD, 16]), sb("lr", [16, S]), sb("wa2", [16, GH * P])
        b, e, la, keep = (sb(n, [P, GH, S]) for n in ("b", "e", "la", "keep"))
        with stage(nc, "loaded", "set", "lr_ready", "lr_kept", "products", "act_step", "logged", "vec_step", "summed", "exped", "used") as (
                block, (loaded, is_set, lr_ready, lr_kept, products, act_step, logged, vec_step, summed, exped, used)):
            @block.sync
            def _(sp):
                sp.dma_start(wlr[:, :, :], w[:, :, C_GLA_LR:C_GLA_LR + 16]).then_inc(loaded, 16)
                sp.dma_start(wa2[:, :], A.gla_wa2[0]).then_inc(loaded, 16)

            @block.gpsimd
            def _(pool):
                nc.gpsimd.memset(keep[:, 0, :], 1.0).then_inc(is_set, 1)
                pool.wait_ge(is_set, 1)
                nc.gpsimd.memset(keep[:, 0, 0:S:GC], 0.0).then_inc(is_set, 1)

            @block.tensor
            def _(pe):
                pe.wait_ge(loaded, 32)
                narrow_product(nc, K.bank[4][0:16, :], wlr, K.hT).then_inc(lr_ready, 1)
                pe.wait_ge(lr_kept, 1)
                for h in range(GH):
                    nc.tensor.matmul(K.bank[h][:, :], wa2[:, h * P:(h + 1) * P], lr[:, :], start=True, stop=True).then_inc(products, 1)

            @block.scalar
            def _(act):
                done = Settle(act, act_step)
                act.wait_ge(lr_ready, 1)
                nc.scalar.activation(lr[:, :], K.bank[4][0:16, :], ACT.Copy).then_inc(lr_kept, 1)
                for h in range(GH):
                    act.wait_ge(products, h + 1)
                    done(nc.scalar.activation(e[:, h, :], K.bank[h][:, :], ACT.Abs, bias=vcol(K, "gla_ba", h)))
                done(nc.scalar.activation(e[:, :, :], e[:, :, :], ACT.Exp, scale=-1.0))
                nc.scalar.activation(e[:, :, :], e[:, :, :], ACT.Ln, bias=1.0).then_inc(logged, 1)
                act.wait_ge(summed, 1)
                nc.scalar.activation(decay[:, :, :], b[:, :, GC - 1:S:GC], ACT.Exp, scale=1 / 16.0).then_inc(exped, 1)
                nc.scalar.activation(e[:, :, :], b[:, :, :], ACT.Exp, scale=1 / 16.0).then_inc(exped, 1)
                act.wait_ge(used, 1)
                nc.scalar.activation(e[:, :, :], b[:, :, :], ACT.Exp, scale=-1 / 16.0).then_inc(exped, 1)
                act.wait_ge(used, 2)
                nc.scalar.activation(e[:, :, :], la[:, :, :], ACT.Exp, scale=1 / 16.0).then_inc(exped, 1)

            @block.vector
            def _(dve):
                done = Settle(dve, vec_step)
                for h in range(GH):
                    dve.wait_ge(act_step, h + 1)
                    done(nc.vector.tensor_scalar(la[:, h, :], K.bank[h][:, :], vcol(K, "gla_ba", h), 0.0, ALU.add, ALU.min))
                dve.wait_ge(logged, 1)
                done(nc.vector.tensor_tensor(la[:, :, :], la[:, :, :], e[:, :, :], ALU.subtract))
                dve.wait_ge(is_set, 2)
                for h in range(GH):
                    done(nc.vector.tensor_tensor_scan(b[:, h, :], keep[:, 0, :], la[:, h, :], 0.0, ALU.mult, ALU.add))
                chunks = lambda x: x[:, :, :].rearrange("p h (n c) -> p (h n) c", c=GC)
                nc.vector.tensor_tensor(chunks(la), chunks(b)[:, :, GC - 1:GC].broadcast_to([P, GH * NC, GC]), chunks(b), ALU.subtract).then_inc(summed, 1)
                dve.wait_ge(exped, 2)
                nc.vector.scalar_tensor_tensor(out=qt[:, :, :], in0=qk[:, 0:GH, :], scalar=float(P) ** -0.5, in1=e[:, :, :],
                                               op0=ALU.mult, op1=ALU.mult).then_inc(used, 1)
                dve.wait_ge(exped, 3)
                nc.vector.tensor_tensor(kt[:, :, :], qk[:, GH:, :], e[:, :, :], ALU.mult).then_inc(used, 1)
                dve.wait_ge(exped, 4)
                nc.vector.tensor_tensor(ke[:, :, :], qk[:, GH:, :], e[:, :, :], ALU.mult).then_inc(used, 1)


def gated(nc, K, tiles, load, n_loads, x_gate, x_value, func, combine, n_combine):
    with ExitStack() as mem:
        raw = mem.enter_context(nc.sbuf_tensor(f"raw_{nc.next_id()}", [P, 2, 2, KD, P], F32))
        cut = Pair(mem, nc, f"cut_{nc.next_id()}", [P, 2, 2, KD, P])
        act_out = mem.enter_context(nc.sbuf_tensor(f"gate_{nc.next_id()}", [P, 2, S], F32))
        with stage(nc, "w_loaded0", "w_loaded1", "asked", "w_rounded", "w_split", "products", "acted", "combined", "vec_step") as (
                block, (w0, w1, asked, w_rounded, w_split, products, acted, combined, vec_step)):
            w_loaded = [w0, w1]

            @block.sync
            def _(sp):
                for s in range(2):
                    load(sp, raw[:, s], s, w_loaded[s])
                with sp.Fori(1, tiles // 2) as i:
                    for s in range(2):
                        sp.wait_ge(w_split, i * 2 + s - 1)
                        load(sp, raw[:, s], i * 2 + s, w_loaded[s])

            @block.gpsimd
            def _(pool):
                with pool.Fori(0, tiles // 2) as i:
                    for s in range(2):
                        pool.wait_ge(w_rounded, i * 2 + s + 1)
                        pool.sem_inc(asked, 1)
                        nc.gpsimd.tensor_tensor(cut.lo[:, s], raw[:, s], cut.hi[:, s].bitcast(F32), ALU.subtract).then_inc(w_split, 1)

            @block.tensor
            def _(pe):
                pe.sem_inc(products, 4)
                pe.sem_inc(combined, 2)
                with pe.Fori(0, tiles // 2) as i:
                    for s in range(2):
                        pe.wait_ge(w_split, i * 2 + s + 1)
                        pe.wait_ge(combined, i * 2 + s + 1)
                        for side, x in enumerate((x_gate, x_value)):
                            product(nc, K.bank[2 * s + side][:, :], lambda part, k: part_of(cut, part)[:, s, side, k, :],
                                    lambda part, k: part_of(x, part)[:, k, :], KD).then_inc(products, 1)

            @block.scalar
            def _(act):
                def round_weights(i, s):
                    act.wait_ge(w_loaded[s], i * (16 * n_loads) + 16 * n_loads)
                    act.wait_ge(products, i * 4 + 2 * s + 2)
                    nc.scalar.activation(cut.hi[:, s], raw[:, s], ACT.Copy).then_inc(w_rounded, 1)

                def make_gate(i, s):
                    act.wait_ge(products, i * 4 + 2 * s + 5)
                    act.wait_ge(combined, i * 2 + s + 1)
                    nc.scalar.activation(act_out[:, s, :], K.bank[2 * s][:, :], func).then_inc(acted, 1)

                round_weights(0, 0)
                with act.Fori(0, tiles // 2 - 1) as i:
                    round_weights(i, 1)
                    make_gate(i, 0)
                    round_weights(i + 1, 0)
                    make_gate(i, 1)
                round_weights(tiles // 2 - 1, 1)
                make_gate(tiles // 2 - 1, 0)
                make_gate(tiles // 2 - 1, 1)

            @block.vector
            def _(dve):
                with dve.Fori(0, tiles // 2) as i:
                    done = Settle(dve, vec_step, i * (2 * n_combine))
                    for s in range(2):
                        dve.wait_ge(acted, i * 2 + s + 1)
                        dve.wait_ge(products, (i * 2 + s) * 2 + 6)
                        combine(done, i * 2 + s, act_out[:, s, :], K.bank[2 * s + 1][:, :])
                        dve.sem_inc(combined, 1)
                    assert done.n == 2 * n_combine


def broadcast_row(ap):
    return bass.AP(ap.tensor, ap.offset, [[0, P], [1, int(np.prod(ap.shape))]])


def residual_norm(nc, K, o, g_row):
    with ExitStack() as mem:
        sb = lambda n, s: mem.enter_context(nc.sbuf_tensor(f"rn_{n}_{nc.next_id()}", s, F32))
        g, junk, stat = sb("g", [P, D]), sb("sq", [P, D]), sb("stat", [P, 3, TT])
        with stage(nc, "loaded", "squared", "meaned", "rooted", "inverted", "scaled", "added") as (
                block, (loaded, squared, meaned, rooted, inverted, scaled, added)):
            @block.sync
            def _(sp):
                sp.dma_start(g[:, :], broadcast_row(g_row)).then_inc(loaded, 16)

            @block.scalar
            def _(act):
                for t in range(TT):
                    if t:
                        act.wait_ge(squared, t)
                    nc.scalar.activation(junk[:, :], o[:, t, :], ACT.Square, accum_out=stat[:, 0, t:t + 1]).then_inc(squared, 1)
                act.wait_ge(meaned, 1)
                nc.scalar.activation(stat[:, 2, :], stat[:, 1, :], ACT.Sqrt).then_inc(rooted, 1)

            @block.vector
            def _(dve):
                dve.wait_ge(squared, TT)
                nc.vector.tensor_scalar(stat[:, 1, :], stat[:, 0, :], 1.0 / D, EPS, ALU.mult, ALU.add).then_inc(meaned, 1)
                dve.wait_ge(rooted, 1)
                nc.vector.reciprocal(stat[:, 0, :], stat[:, 2, :]).then_inc(inverted, 1)
                dve.wait_ge(inverted, 1)
                dve.wait_ge(loaded, 16)
                for t in range(TT):
                    nc.vector.scalar_tensor_tensor(out=o[:, t, :], in0=o[:, t, :], scalar=stat[:, 0, t:t + 1], in1=g[:, :],
                                                   op0=ALU.mult, op1=ALU.mult).then_inc(scaled, 1)
                for t in range(TT):
                    dve.wait_ge(scaled, t + 1)
                    nc.vector.tensor_tensor(K.x[:, t, :], K.x[:, t, :], o[:, t, :], ALU.add).then_inc(added, 1)


def merge(nc, K, A, y, merged):
    w_gate = A.w_in[0].rearrange("(k p) m -> p k m", p=P)
    with ExitStack() as mem:
        term = mem.enter_context(nc.sbuf_tensor("merge_term", [P, S], F32))
        ypair = Pair(mem, nc, "branch", [P, KD, S])
        for b in range(3):
            def load(sp, weights, m, sem):
                sp.dma_start(weights[:, 0], w_gate[:, :, ds(m * P + (C_MERGE + b * D), P)]).then_inc(sem, 16)
                if b != 1:
                    sp.dma_start(weights[:, 1], A.w_branch[0, b].rearrange("(k p) m -> p k m", p=P)[:, :, ds(m * P, P)]).then_inc(sem, 16)
                    return
                src = A.w_branch[0, b].rearrange("(gp a r d) m -> gp a d r m", gp=2, a=2, r=4)
                for gp in range(2):
                    for a in range(2):
                        sp.dma_start(weights[a * HD:(a + 1) * HD, 1, gp * 4:gp * 4 + 4, :], src[gp, a][:, :, ds(m * P, P)]).then_inc(sem, 16)

            def combine(done, m, gate, value):
                if b == 0:
                    done(nc.vector.tensor_tensor(merged[:, ds(m, 1), :].rearrange("p o n -> p (o n)"), gate, value, ALU.mult))
                    return
                row = merged[:, ds(m, 1), :].rearrange("p o n -> p (o n)")
                done(nc.vector.tensor_tensor(term[:, :], gate, value, ALU.mult))
                done(nc.vector.tensor_tensor(row, row, term[:, :], ALU.add))

            split(nc, ypair, y[b], KD, "y")
            gated(nc, K, KD, load, 5 if b == 1 else 2, K.hT, ypair, ACT.Sigmoid, combine, 1 if b == 0 else 2)


def ffn(nc, K, A):
    w = A.w_ffn_in[0].rearrange("(k p) m -> p k m", p=P)
    with ExitStack() as mem:
        hidden = Pair(mem, nc, "ffn_hidden", [P, KF, S])
        whole = mem.enter_context(nc.sbuf_tensor("ffn_whole", [P, S], F32))
        row = lambda part, m: part[:, ds(m, 1), :].rearrange("p o n -> p (o n)")

        def load(sp, weights, m, sem):
            for side in range(2):
                sp.dma_start(weights[:, side], w[:, :, ds(m * P + side * D_FF, P)]).then_inc(sem, 16)

        def combine(done, m, gate, value):
            done(nc.vector.tensor_tensor(whole[:, :], gate, value, ALU.mult))
            done(nc.vector.tensor_copy(row(hidden.hi, m), whole[:, :]))
            done(nc.vector.tensor_tensor(row(hidden.lo, m), whole[:, :], row(hidden.hi, m).bitcast(F32), ALU.subtract))

        gated(nc, K, KF, load, 2, K.hT, K.hT, ACT.Silu, combine, 3)
        o = mem.enter_context(nc.sbuf_tensor("ffn_o", [P, TT, D], F32))
        project_model(nc, K, A.w_ffn_out[0], KF, hidden, o)
        residual_norm(nc, K, o, A.norm_g[0, 3])


ALPHA = 4 ** 0.25
LN_EPS = 1e-5
SI = 2048
SG, SE, SP, SN = 4, 8, 64, 128
SH = SG * SE


def layer_norm(nc, K, mix, g_row, b_row):
    with ExitStack() as mem:
        sb = lambda n, s: mem.enter_context(nc.sbuf_tensor(f"ln_{n}_{nc.next_id()}", s, F32))
        g, b = sb("g", [P, D]), sb("b", [P, D])
        parts, stat = sb("parts", [P, TT, 2, 6]), sb("stat", [P, TT, 2])
        std, rstd = sb("std", [P, TT]), sb("rstd", [P, TT])
        with stage(nc, "loaded", "vec_step", "varied", "rooted") as (block, (loaded, vec_step, varied, rooted)):
            @block.sync
            def _(sp):
                sp.dma_start(g[:, :], broadcast_row(g_row)).then_inc(loaded, 16)
                sp.dma_start(b[:, :], broadcast_row(b_row)).then_inc(loaded, 16)

            @block.scalar
            def _(act):
                act.wait_ge(varied, 1)
                nc.scalar.activation(std[:, :], rstd[:, :], ACT.Sqrt).then_inc(rooted, 1)

            @block.vector
            def _(dve):
                done = Settle(dve, vec_step)
                for t in range(TT):
                    last = nc.vector.scalar_tensor_tensor(out=mix[:, t, :], in0=K.x[:, t, :], scalar=ALPHA, in1=mix[:, t, :],
                                                          op0=ALU.mult, op1=ALU.add)
                done(last)
                for t in range(TT):
                    for h in range(2):
                        last = nc.vector.bn_stats(parts[:, t, h, :], mix[:, t, h * 512:(h + 1) * 512])
                done(last)
                for t in range(TT):
                    last = nc.vector.bn_aggr(stat[:, t, :], parts[:, t, :, :].rearrange("p h s -> p (h s)"))
                done(last)
                nc.vector.tensor_scalar(rstd[:, :], stat[:, :, 1], LN_EPS, None, ALU.add).then_inc(varied, 1)
                dve.wait_ge(loaded, 32)
                for t in range(TT):
                    last = nc.vector.scalar_tensor_tensor(out=mix[:, t, :], in0=mix[:, t, :], scalar=stat[:, t, 0:1], in1=g[:, :],
                                                          op0=ALU.subtract, op1=ALU.mult)
                dve.wait_ge(rooted, 1)
                done(nc.vector.reciprocal(rstd[:, :], std[:, :]))
                for t in range(TT):
                    last = nc.vector.scalar_tensor_tensor(out=K.x[:, t, :], in0=mix[:, t, :], scalar=rstd[:, t:t + 1], in1=b[:, :],
                                                          op0=ALU.mult, op1=ALU.add)
                done(last)


def ssd_steps(nc, K, A, w, rows):
    csT = K.csT
    with ExitStack() as mem:
        sb = lambda n, s: mem.enter_context(nc.sbuf_tensor(f"dt_{n}", s, F32))
        wdt, vec = sb("w", [P, KD, SH]), sb("vec", [SH, 4])
        e, dt, ecs, keep = (sb(n, [SH, S]) for n in ("e", "dt", "ecs", "keep"))
        with stage(nc, "loaded", "made", "act_step", "vec_step", "turned", "copied", "stepped", "summed", "exped") as (
                block, (loaded, made, act_step, vec_step, turned, copied, stepped, summed, exped)):
            @block.sync
            def _(sp):
                sp.dma_start(wdt[:, :, :], w[:, :, SI + 3072:SI + 3072 + SH]).then_inc(loaded, 16)
                sp.dma_start(vec[:, 0:1], A.ssd_dt_bias_2.rearrange("a h -> h a")).then_inc(loaded, 16)
                sp.dma_start(vec[:, 1:2], A.ssd_a_log_2.rearrange("a h -> h a")).then_inc(loaded, 16)

            @block.tensor
            def _(pe):
                pe.wait_ge(loaded, 48)
                narrow_product(nc, K.bank[0][0:SH, :], wdt, K.hT).then_inc(made, 1)
                pe.wait_ge(stepped, 1)
                for n, src in enumerate((csT, dt, e, ecs)):
                    for t in range(TT):
                        c = (n * TT + t) * SH
                        last = nc.tensor.transpose(K.bank[1][:, c:c + SH], src[:, t * P:(t + 1) * P], K.ident[0:SH, 0:SH])
                last.then_inc(turned, 1)

            @block.scalar
            def _(act):
                done = Settle(act, act_step)
                act.wait_ge(made, 1)
                done(nc.scalar.activation(e[:, :], K.bank[0][0:SH, :], ACT.Abs, bias=vec[:, 0:1]))
                done(nc.scalar.activation(e[:, :], e[:, :], ACT.Exp, scale=-1.0))
                done(nc.scalar.activation(e[:, :], e[:, :], ACT.Ln, bias=1.0))
                done(nc.scalar.activation(vec[:, 2:3], vec[:, 1:2], ACT.Exp))
                act.wait_ge(summed, 1)
                nc.scalar.activation(ecs[:, :], csT[:, :], ACT.Exp).then_inc(exped, 1)
                nc.scalar.activation(e[:, :], e[:, :], ACT.Exp).then_inc(exped, 1)
                act.wait_ge(turned, 1)
                nc.scalar.activation(rows[:, :, :, :].rearrange("p n t h -> p (n t h)"), K.bank[1][:, :], ACT.Copy).then_inc(copied, 1)

            @block.vector
            def _(dve):
                done = Settle(dve, vec_step)
                done(nc.vector.memset(keep[:, :], 1.0))
                done(nc.vector.memset(keep[:, 0:S:P], 0.0))
                dve.wait_ge(act_step, 4)
                done(nc.vector.tensor_scalar(dt[:, :], K.bank[0][0:SH, :], vec[:, 0:1], 0.0, ALU.add, ALU.max))
                done(nc.vector.tensor_tensor(dt[:, :], dt[:, :], e[:, :], ALU.add))
                done(nc.vector.tensor_scalar(ecs[:, :], dt[:, :], vec[:, 2:3], -1.0, ALU.mult, ALU.mult))
                done(nc.vector.tensor_tensor_scan(csT[:, :], keep[:, :], ecs[:, :], 0.0, ALU.mult, ALU.add))
                chunks = lambda x: x[:, :].rearrange("h (n c) -> h n c", c=P)
                nc.vector.tensor_tensor(chunks(e), chunks(csT)[:, :, P - 1:P].broadcast_to([SH, TT, P]), chunks(csT), ALU.subtract).then_inc(summed, 1)
                dve.wait_ge(exped, 2)
                nc.vector.tensor_tensor(e[:, :], e[:, :], dt[:, :], ALU.mult).then_inc(stepped, 1)


class Convolution(Beside):

    GROUP, PAD = 3, 3
    names = ("conv_zeroed", "conv_opened", "conv_tapped", "conv_done", "conv_acted")

    def __init__(self, nc, K, xbc, acc):
        self.nc, self.K, self.xbc, self.acc = nc, K, xbc, acc
        self.n_tiles = xbc.shape[1]

    def scalar_before(self, act, c):
        zeroed, opened, tapped, conv_done, acted = self.sems
        if c == 0:
            act.wait_ge(zeroed, 1)
        else:
            act.wait_ge(acted, self.GROUP * c)
        for q in range(self.GROUP):
            n = c * self.GROUP + q
            self.nc.scalar.activation(self.acc[:, q, :], self.xbc[:, n, 0:S], ACT.Identity, scale=vcol(self.K, "ssd_conv_w", n),
                                      bias=vcol(self.K, "ssd_conv_b", n)).then_inc(opened, 1)

    def vector(self, dve, c):
        zeroed, opened, tapped, conv_done, acted = self.sems
        if c == 0:
            self.nc.vector.memset(self.xbc[:, :, 0:self.PAD], 0.0).then_inc(zeroed, 1)
        dve.wait_ge(opened, self.GROUP * (c + 1))
        for j in range(1, self.PAD + 1):
            for q in range(self.GROUP):
                n = c * self.GROUP + q
                if j > 1:
                    dve.wait_ge(tapped, (c * (self.PAD - 1) + j - 2) * self.GROUP + q + 1)
                ins = self.nc.vector.scalar_tensor_tensor(out=self.acc[:, q, :], in0=self.xbc[:, n, j:j + S],
                                                          scalar=vcol(self.K, "ssd_conv_w", j * self.n_tiles + n),
                                                          in1=self.acc[:, q, :], op0=ALU.mult, op1=ALU.add)
                ins.then_inc(tapped if j < self.PAD else conv_done, 1)

    def scalar_after(self, act, c):
        zeroed, opened, tapped, conv_done, acted = self.sems
        for q in range(self.GROUP):
            n = c * self.GROUP + q
            act.wait_ge(conv_done, n + 1)
            self.nc.scalar.activation(self.xbc[:, n, self.PAD:], self.acc[:, q, :], ACT.Silu).then_inc(acted, 1)


def to_tokens(nc, K, src, col, dst, n):
    with stage(nc, "turned", "copied") as (block, (turned, copied)):
        @block.tensor
        def _(pe):
            for k in range(n):
                if k >= 8:
                    pe.wait_ge(copied, k - 7)
                for t in range(TT):
                    last = nc.tensor.transpose(K.bank[k % 8][:, t * P:(t + 1) * P], src(k)[:, t * P:(t + 1) * P], K.ident[:, :])
                last.then_inc(turned, 1)

        @block.scalar
        def _(act):
            for k in range(n):
                act.wait_ge(turned, k + 1)
                nc.scalar.activation(dst[:, :, (col + k) * P:(col + k + 1) * P], K.bank[k % 8][:, :].rearrange("p (t c) -> p t c", t=TT),
                                     ACT.Copy).then_inc(copied, 1)


def ssd(nc, K, A, o):
    PAD = 3
    w = A.ssd_w_in_2[0].rearrange("(k p) m -> p k m", p=P)
    with ExitStack() as mem:
        sb = lambda n, s: mem.enter_context(nc.sbuf_tensor(f"ssd_{n}", s, F32))
        z = sb("z", [P, TT, SI])
        with ExitStack() as inner:
            sb2 = lambda n, s: inner.enter_context(nc.sbuf_tensor(f"ssd_{n}", s, F32))
            xbc = sb2("xbc", [P, 24, S + PAD])
            rows = sb2("rows", [P, 4, TT, SH])
            K.csT = sb2("csT", [SH, S])
            with ExitStack() as early:
                K.hT = xT = Pair(early, nc, "ssd_xT", [P, KD, S])
                to_channels(nc, K, K.x, xT, KD)
                project(nc, K, KD, [
                    channels_job(nc, xT, KD, columns(w, lambda i, c=c: i * (2 * CW) + (SI + c * CW)),
                                 lambda bank, m, i, c=c: nc.scalar.activation(xbc[:, ds(i * 4 + 2 * c + m, 1), PAD:], bank, ACT.Copy))
                    for c in range(2)], passes=6)
                with nc.sbuf_tensor("conv_acc", [P, Convolution.GROUP, S], F32) as acc:
                    conv = Convolution(nc, K, xbc, acc)
                    project(nc, K, KD, [
                        tokens_job(nc, xT, KD, columns(w, lambda i, c=c: c * CW),
                                   lambda bank, t, i, c=c: nc.scalar.activation(z[:, t, c * CW:(c + 1) * CW], bank, ACT.Copy))
                        for c in range(8)], beside=conv)
                ssd_steps(nc, K, A, w, rows)
            xtok = sb2("xtok", [P, TT, SI + SG * SN])
            to_tokens(nc, K, lambda k: xbc[:, k, PAD:], 0, xtok, 20)
            ssd_scan(nc, K, A, xbc[:, :, PAD:], xtok, z, rows)
        with ExitStack() as late:
            yT = Pair(late, nc, "ssd_yT", [P, SI // P, S])
            to_channels(nc, K, z, yT, SI // P, lambda k: vcol(K, "ssd_norm", k))
            project_model(nc, K, A.ssd_w_out_2[0], SI // P, yT, o)


def ssd_scan(nc, K, A, xbc, xtok, z, rows):
    UNITS = [(t, g) for t in range(TT) for g in range(SG)]
    GWID = SE * SP
    with ExitStack() as mem:
        sb = lambda n, s: mem.enter_context(nc.sbuf_tensor(f"scan_{n}", s, F32))
        cmask, nmask = sb("cmask", [P, P]), sb("nmask", [P, P])
        dskip = sb("dskip", [P, SH])
        cb = sb("cb", [P, 2, P])
        dec = sb("dec", [P, 2, SE, P])
        last_dec = sb("last", [P, 2, SE])
        xr, xe = sb("xr", [P, 2, GWID]), sb("xe", [P, 2, GWID])
        state = sb("state", [P, SG, GWID])
        off, skip = sb("off", [P, 2, GWID]), sb("skip", [P, 2, GWID])
        ss = sb("ss", [P, 2, TT, SG])
        junk = sb("junk", [P, GWID])
        heads = lambda x: x.rearrange("p (e q) -> p e q", e=SE)
        with stage(nc, "loaded", "masked", "spread", "shifted", "exped", "mixed", "scaled", "produced", "moved", "finished",
                   "vec_step", "pool_step", "gated", "squared", "rooted") as (
                block, (loaded, masked, spread, shifted, exped, mixed, scaled, produced, moved, finished, vec_step, pool_step, gated, squared, rooted)):
            @block.sync
            def _(sp):
                sp.dma_start(dskip[:, :], broadcast_row(A.ssd_d_2[0])).then_inc(loaded, 16)

            @block.gpsimd
            def _(pool):
                nc.gpsimd.memset(cmask[:, :], 1.0).then_inc(masked, 1)
                nc.gpsimd.memset(nmask[:, :], 0.0).then_inc(masked, 1)
                pool.wait_ge(masked, 2)
                nc.gpsimd.affine_select(out=cmask[:, :], in_=cmask[:, :], compare_op=ALU.is_ge, fill=0.0, base=0,
                                        pattern=[[1, P]], channel_multiplier=-1).then_inc(masked, 1)
                nc.gpsimd.affine_select(out=nmask[:, :], in_=nmask[:, :], compare_op=ALU.is_ge, fill=NEG, base=0,
                                        pattern=[[1, P]], channel_multiplier=-1).then_inc(masked, 1)
                for u, (t, g) in enumerate(UNITS):
                    if u >= 2:
                        pool.wait_ge(finished, u - 1)
                    xs = heads(xtok[:, t, g * GWID:(g + 1) * GWID])
                    hs = slice(g * SE, (g + 1) * SE)
                    per_head = lambda r: r.unsqueeze(2).broadcast_to([P, SE, SP])
                    nc.gpsimd.tensor_tensor(heads(xr[:, u % 2, :]), xs, per_head(rows[:, 1, t, hs]), ALU.mult)
                    nc.gpsimd.tensor_tensor(heads(xe[:, u % 2, :]), xs, per_head(rows[:, 2, t, hs]), ALU.mult)
                    if u == 0:
                        pool.wait_ge(loaded, 16)
                    nc.gpsimd.tensor_tensor(heads(skip[:, u % 2, :]), xs, per_head(dskip[:, hs]), ALU.mult).then_inc(scaled, 1)

            @block.tensor
            def _(pe):
                for step in range(len(UNITS) + 1):
                    if step < len(UNITS):
                        u = step
                        t, g = UNITS[u]
                        toks = slice(t * P, (t + 1) * P)
                        if u >= 1:
                            pe.wait_ge(shifted, u)
                            pe.wait_ge(exped, u)
                        for e in range(SE):
                            h = g * SE + e
                            nc.tensor.matmul(K.bank[e // 4][:, (e % 4) * P:(e % 4 + 1) * P], K.ident[0:SH, h:h + 1].broadcast_to([SH, P]),
                                             K.csT[:, toks], start=True, stop=True)
                        nc.tensor.matmul(K.bank[2][:, 0:P], xbc[:, 16 + g, toks], xbc[:, 20 + g, toks], start=True, stop=True).then_inc(spread, 1)
                    if step >= 1:
                        u = step - 1
                        t, g = UNITS[u]
                        toks = slice(t * P, (t + 1) * P)
                        pe.wait_ge(mixed, u + 1)
                        pe.wait_ge(scaled, u + 1)
                        if u >= 1:
                            pe.wait_ge(moved, u)
                        if t:
                            nc.tensor.matmul(K.bank[4][:, :], xbc[:, 20 + g, toks], state[:, g, :], start=True, stop=True)
                        nc.tensor.matmul(K.bank[5][:, :], xtok[:, t, SI + g * SN:SI + (g + 1) * SN], xe[:, u % 2, :], start=True, stop=True)
                        for e in range(SE):
                            last = nc.tensor.matmul(K.bank[3][:, e * SP:(e + 1) * SP], dec[:, u % 2, e, :], xr[:, u % 2, e * SP:(e + 1) * SP],
                                                    start=True, stop=True)
                        last.then_inc(produced, 1)

            @block.scalar
            def _(act):
                nc.scalar.activation(z[:, :, :], z[:, :, :], ACT.Silu).then_inc(gated, 1)
                for u in range(len(UNITS)):
                    act.wait_ge(shifted, u + 1)
                    nc.scalar.activation(last_dec[:, u % 2, 0:4], K.bank[0][:, P - 1:S:P], ACT.Exp)
                    nc.scalar.activation(last_dec[:, u % 2, 4:8], K.bank[1][:, P - 1:S:P], ACT.Exp)
                    nc.scalar.activation(dec[:, u % 2], dec[:, u % 2], ACT.Exp).then_inc(exped, 1)
                for u, (t, g) in enumerate(UNITS):
                    act.wait_ge(finished, u + 1)
                    if u:
                        act.wait_ge(squared, u)
                    nc.scalar.activation(junk[:, :], z[:, t, g * GWID:(g + 1) * GWID], ACT.Square, accum_out=ss[:, 0, t, g:g + 1]).then_inc(squared, 1)
                act.wait_ge(rooted, 1)
                nc.scalar.activation(ss[:, 0], ss[:, 1], ACT.Sqrt).then_inc(rooted, 1)

            @block.vector
            def _(dve):
                done = Settle(dve, vec_step)
                dve.wait_ge(masked, 4)
                dve.wait_ge(gated, 1)
                for step in range(len(UNITS) + 1):
                    if step < len(UNITS):
                        u = step
                        t, g = UNITS[u]
                        dve.wait_ge(spread, u + 1)
                        if u >= 2:
                            dve.wait_ge(produced, u - 1)
                        for b in range(2):
                            last = nc.vector.tensor_tensor(dec[:, u % 2, b * 4:(b + 1) * 4, :], K.bank[b][:, :].rearrange("p (e l) -> p e l", e=4),
                                                           nmask[:, :].unsqueeze(1).broadcast_to([P, 4, P]), ALU.add)
                        done(nc.vector.tensor_tensor(cb[:, u % 2, :], K.bank[2][:, 0:P], cmask[:, :], ALU.mult))
                        nc.vector.tensor_tensor(dec[:, u % 2], dec[:, u % 2],
                                                rows[:, 0, t, g * SE:(g + 1) * SE].unsqueeze(2).broadcast_to([P, SE, P]), ALU.subtract).then_inc(shifted, 1)
                        dve.wait_ge(exped, u + 1)
                        nc.vector.tensor_tensor(dec[:, u % 2], dec[:, u % 2], cb[:, u % 2, :].unsqueeze(1).broadcast_to([P, SE, P]), ALU.mult).then_inc(mixed, 1)
                    if step >= 1:
                        u = step - 1
                        t, g = UNITS[u]
                        cols = slice(g * GWID, (g + 1) * GWID)
                        dve.wait_ge(produced, u + 1)
                        sk = skip[:, u % 2, :]
                        if t:
                            nc.vector.tensor_tensor(heads(off[:, u % 2, :]), heads(K.bank[4][:, :]),
                                                    rows[:, 3, t, g * SE:(g + 1) * SE].unsqueeze(2).broadcast_to([P, SE, SP]), ALU.mult)
                            done(nc.vector.tensor_tensor(heads(state[:, g, :]), heads(state[:, g, :]),
                                                         last_dec[:, u % 2, :].unsqueeze(2).broadcast_to([P, SE, SP]), ALU.mult))
                            done(nc.vector.tensor_tensor(sk, sk, off[:, u % 2, :], ALU.add))
                            nc.vector.tensor_tensor(state[:, g, :], state[:, g, :], K.bank[5][:, :], ALU.add)
                        else:
                            nc.vector.tensor_copy(state[:, g, :], K.bank[5][:, :])
                        ins = nc.vector.tensor_tensor(sk, sk, K.bank[3][:, :], ALU.add)
                        ins.then_inc(moved, 1)
                        dve.wait_ge(moved, u + 1)
                        nc.vector.tensor_tensor(z[:, t, cols], z[:, t, cols], sk, ALU.mult).then_inc(finished, 1)
                dve.wait_ge(squared, len(UNITS))
                nc.vector.tensor_scalar(ss[:, 1], ss[:, 0], 1.0 / GWID, LN_EPS, ALU.mult, ALU.add).then_inc(rooted, 1)
                dve.wait_ge(rooted, 2)
                done(nc.vector.reciprocal(ss[:, 1], ss[:, 0]))
                for t, g in UNITS:
                    cols = slice(g * GWID, (g + 1) * GWID)
                    nc.vector.tensor_scalar(z[:, t, cols], z[:, t, cols], ss[:, 1, t, g:g + 1], None, ALU.mult)


EG, EE, NE = 4, 8, 32
HID = 512
KH = HID // P
NB = -(-((2 * S + NE * (P - 1)) // P) // 2) * 2
FAR_INDEX = 100.0


def moe(nc, K, A, layer, o):
    with ExitStack() as mem:
        sb = lambda n, s, dt=F32: mem.enter_context(nc.sbuf_tensor(f"moe{layer}_{n}", s, dt))
        weight = sb("weight", [P, 2, TT])
        dest = sb("dest", [P, 2, TT], U32)
        expert = sb("expert", [1, NB], I32)
        pairs = sb("pairs", [1, 1], I32)
        idx = sb("idx", [P, NB + 2], U32)
        K.scattered = nc.alloc_semaphore(f"scattered{layer}")
        K.x_gathered = [nc.alloc_semaphore(f"x_gathered{layer}_{s}") for s in range(2)]
        K.picked = [nc.alloc_semaphore(f"picked{layer}_{n}") for n in range(2 * TT)]
        moe_route(nc, K, A, layer, weight, dest, expert, pairs, idx)
        moe_experts(nc, K, A, layer, expert, pairs, idx)
        moe_combine(nc, K, layer, weight, dest, o)


def moe_route(nc, K, A, layer, weight, dest, expert, pairs, idx):
    K.x_rows = nc.dram_tensor(f"x_rows{layer}", (S, D), F32, kind="Internal").ap()
    K.y_rows = nc.dram_tensor(f"y_rows{layer}", ((NB + 2) * P, D), F32, kind="Internal").ap()
    tokens_of = nc.dram_tensor(f"tokens_of_rows{layer}", ((NB + 2) * P, 1), F32, kind="Internal").ap()
    with ExitStack() as mem:
        sb = lambda n, s, dt=F32: mem.enter_context(nc.sbuf_tensor(f"rt{layer}_{n}", s, dt))
        xT = sb("xT", [P, KD, S])
        to_channels(nc, K, K.x, xT, KD)
        NL = EG + NE
        wr, br = sb("w", [P, KD, NL]), sb("b", [P, NL])
        lg = sb("logit", [P, TT, NL])
        before, ones = sb("before", [P, P]), sb("ones", [P, P])
        iota_e, iota_b, iota_t = sb("iota_e", [P, NE]), sb("iota_b", [P, NB]), sb("iota_t", [P, TT])
        zero = sb("zero", [NB + 2, P])
        g4, e4 = sb("g4", [P, TT, 3, EG]), sb("e4", [P, TT, EG])
        el, cand = sb("el", [P, TT, NE]), sb("cand", [P, TT, NE])
        oh = sb("oh", [P, 3, TT, NE])
        st = sb("st", [P, 12, TT])
        rank = sb("rank", [P, TT, NE])
        cnt, nblk, bend, tmp32 = (sb(n, [P, NE]) for n in ("cnt", "nblk", "bend", "tmp32"))
        cmpb, fexp, npairs = sb("cmpb", [1, NB, NE]), sb("fexp", [1, NB]), sb("npairs", [1, 1])
        destf = sb("destf", [P, 2, TT])
        tok_rows = sb("tok_rows", [NB + 2, P])
        MX, EX, SM, GI, GW1, M1, I1, M2, I2, DN, T1, T2 = range(12)
        col = lambda i: st[:, i, :]
        wide = lambda i, n: st[:, i, :].unsqueeze(2).broadcast_to([P, TT, n])
        with stage(nc, "loaded", "made", "logits", "vec_step", "asked", "exped", "counted", "zeroed", "x_stored",
                   "reloaded", "turned", "placed") as (
                block, (loaded, made, logits, vec_step, asked, exped, counted, zeroed, x_stored, reloaded, turned, placed)):
            scattered = K.scattered

            @block.sync
            def _(sp):
                sp.dma_start(wr[:, :, 0:EG], A.moe_w_router_group_2[layer].rearrange("(k p) m -> p k m", p=P)).then_inc(loaded, 16)
                sp.dma_start(wr[:, :, EG:NL], A.moe_w_router_expert_2[layer].rearrange("(k p) m -> p k m", p=P)).then_inc(loaded, 16)
                sp.dma_start(br[:, 0:EG], broadcast_row(A.moe_b_router_group_2[layer])).then_inc(loaded, 16)
                sp.dma_start(br[:, EG:NL], broadcast_row(A.moe_b_router_expert_2[layer])).then_inc(loaded, 16)
                sp.dma_start(K.x_rows.rearrange("(t p) d -> p t d", p=P), K.x[:, :, :]).then_inc(x_stored, 16)
                sp.wait_ge(made, 8)
                sp.dma_start(tokens_of.rearrange("(b p) a -> b (p a)", p=P), zero[:, :]).then_inc(zeroed, 16)
                sp.wait_ge(scattered, 16 * 2 * TT)
                sp.dma_start(tok_rows[:, :], tokens_of.rearrange("(b p) a -> b (p a)", p=P)).then_inc(reloaded, 16)
                sp.wait_ge(x_stored, 16)

            @block.gpsimd
            def _(pool):
                nc.gpsimd.memset(before[:, :], 1.0).then_inc(made, 1)
                nc.gpsimd.memset(ones[:, :], 1.0).then_inc(made, 1)
                pool.wait_ge(made, 2)
                nc.gpsimd.affine_select(out=before[:, :], in_=before[:, :], compare_op=ALU.is_gt, fill=0.0, base=0,
                                        pattern=[[1, P]], channel_multiplier=-1).then_inc(made, 1)
                nc.gpsimd.iota(iota_e[:, :], pattern=[[1, NE]], base=0, channel_multiplier=0, allow_small_or_imprecise_dtypes=True).then_inc(made, 1)
                nc.gpsimd.iota(iota_b[:, :], pattern=[[1, NB]], base=0, channel_multiplier=0, allow_small_or_imprecise_dtypes=True).then_inc(made, 1)
                nc.gpsimd.iota(iota_t[:, :], pattern=[[P, TT]], base=0, channel_multiplier=1, allow_small_or_imprecise_dtypes=True).then_inc(made, 1)
                nc.gpsimd.memset(zero[:, :], 0.0).then_inc(made, 1)
                pool.wait_ge(made, 7)
                nc.gpsimd.engine_nop().then_inc(made, 1)
                pool.wait_ge(placed, 1)
                pool.wait_ge(zeroed, 16)
                for k in range(2):
                    for t in range(TT):
                        nc.gpsimd.indirect_dma_start(out=tokens_of, out_offset=bass.IndirectOffsetOnAxis(ap=dest[:, k, t:t + 1], axis=0),
                                                     in_=iota_t[:, t:t + 1], in_offset=None).then_inc(scattered, 16)

            @block.tensor
            def _(pe):
                pe.wait_ge(loaded, 64)
                for t in range(TT):
                    for k in range(KD):
                        last = nc.tensor.matmul(K.bank[0][:, t * NL:(t + 1) * NL], xT[:, k, t * P:(t + 1) * P], wr[:, k, :],
                                                start=(k == 0), stop=(k == KD - 1))
                last.then_inc(logits, 1)
                pe.wait_ge(made, 8)
                pe.wait_ge(asked, 2)
                for t in range(TT):
                    for b in range(t + 1):
                        nc.tensor.matmul(K.bank[1][:, t * NE:(t + 1) * NE], (before if b == t else ones)[:, :], oh[:, 2, b, :],
                                         start=(b == 0), stop=(b == t))
                for b in range(TT):
                    last = nc.tensor.matmul(K.bank[1][:, TT * NE:(TT + 1) * NE], ones[:, :], oh[:, 2, b, :], start=(b == 0), stop=(b == TT - 1))
                last.then_inc(counted, 1)
                pe.wait_ge(reloaded, 16)
                nc.tensor.transpose(K.bank[2][:, 0:NB + 2], tok_rows[:, :], K.ident[0:NB + 2, 0:NB + 2]).then_inc(turned, 1)

            @block.scalar
            def _(act):
                act.wait_ge(asked, 1)
                nc.scalar.activation(g4[:, :, 1, :], g4[:, :, 0, :], ACT.Exp).then_inc(exped, 1)
                act.wait_ge(asked, 2)
                nc.scalar.activation(col(EX), col(T1), ACT.Exp).then_inc(exped, 1)

            @block.vector
            def _(dve):
                done = Settle(dve, vec_step)

                def first_equal(values, best, iota, n, scratch, index, out):
                    shape = [P, TT, n]
                    done(nc.vector.tensor_tensor(scratch, values, wide(best, n), ALU.is_equal))
                    done(nc.vector.tensor_scalar(scratch, scratch, -FAR_INDEX, FAR_INDEX, ALU.mult, ALU.add))
                    done(nc.vector.tensor_tensor(scratch, scratch, iota[:, 0:n].unsqueeze(1).broadcast_to(shape), ALU.add))
                    done(nc.vector.tensor_reduce(col(index), scratch, AX, ALU.min))
                    done(nc.vector.tensor_tensor(out, wide(index, n), iota[:, 0:n].unsqueeze(1).broadcast_to(shape), ALU.is_equal))

                dve.wait_ge(logits, 1)
                dve.wait_ge(made, 8)
                done(nc.vector.tensor_tensor(lg[:, :, :], K.bank[0][:, 0:TT * NL].rearrange("p (t n) -> p t n", t=TT),
                                             br[:, :].unsqueeze(1).broadcast_to([P, TT, NL]), ALU.add))
                gl = lg[:, :, 0:EG]
                done(nc.vector.tensor_reduce(col(MX), gl, AX, ALU.max))
                nc.vector.tensor_tensor(g4[:, :, 0, :], gl, wide(MX, EG), ALU.subtract).then_inc(asked, 1)
                first_equal(gl, MX, iota_e, EG, g4[:, :, 2, :], GI, e4[:, :, :])
                dve.wait_ge(exped, 1)
                done(nc.vector.tensor_reduce(col(SM), g4[:, :, 1, :], AX, ALU.add))
                done(nc.vector.reciprocal(col(GW1), col(SM)))
                done(nc.vector.tensor_scalar(e4[:, :, :], e4[:, :, :], -NEG, NEG, ALU.mult, ALU.add))
                done(nc.vector.tensor_tensor(el[:, :, :].rearrange("p t (g e) -> p t g e", g=EG),
                                             lg[:, :, EG:].rearrange("p t (g e) -> p t g e", g=EG),
                                             e4[:, :, :].unsqueeze(3).broadcast_to([P, TT, EG, EE]), ALU.add))
                done(nc.vector.tensor_reduce(col(M1), el[:, :, :], AX, ALU.max))
                first_equal(el[:, :, :], M1, iota_e, NE, cand[:, :, :], I1, oh[:, 0])
                done(nc.vector.scalar_tensor_tensor(out=el[:, :, :], in0=oh[:, 0], scalar=4 * NEG, in1=el[:, :, :], op0=ALU.mult, op1=ALU.add))
                done(nc.vector.tensor_reduce(col(M2), el[:, :, :], AX, ALU.max))
                first_equal(el[:, :, :], M2, iota_e, NE, cand[:, :, :], I2, oh[:, 1])
                done(nc.vector.tensor_tensor(col(T1), col(M2), col(M1), ALU.subtract))
                nc.vector.tensor_tensor(oh[:, 2], oh[:, 0], oh[:, 1], ALU.add).then_inc(asked, 1)
                dve.wait_ge(exped, 2)
                done(nc.vector.tensor_scalar(col(DN), col(EX), 1.0, None, ALU.add))
                done(nc.vector.reciprocal(col(T2), col(DN)))
                done(nc.vector.tensor_tensor(weight[:, 0, :], col(T2), col(GW1), ALU.mult))
                done(nc.vector.tensor_tensor(weight[:, 1, :], weight[:, 0, :], col(EX), ALU.mult))
                dve.wait_ge(counted, 1)
                done(nc.vector.tensor_copy(cnt[:, :], K.bank[1][:, TT * NE:(TT + 1) * NE]))
                done(nc.vector.tensor_scalar(nblk[:, :], cnt[:, :], 0.0, None, ALU.is_gt))
                for j in range(1, S // P):
                    done(nc.vector.scalar_tensor_tensor(out=nblk[:, :], in0=cnt[:, :], scalar=float(j * P), in1=nblk[:, :], op0=ALU.is_gt, op1=ALU.add))
                done(nc.vector.tensor_tensor_scan(bend[:, :], ones[:, 0:NE], nblk[:, :], 0.0, ALU.mult, ALU.add))
                done(nc.vector.tensor_tensor(tmp32[:, :], bend[:, :], nblk[:, :], ALU.subtract))
                done(nc.vector.tensor_scalar(tmp32[:, :], tmp32[:, :], float(P), None, ALU.mult))
                done(nc.vector.tensor_tensor(rank[:, :, :], K.bank[1][:, 0:TT * NE].rearrange("p (t e) -> p t e", t=TT),
                                             tmp32[:, :].unsqueeze(1).broadcast_to([P, TT, NE]), ALU.add))
                for k in range(2):
                    done(nc.vector.tensor_tensor(cand[:, :, :], rank[:, :, :], oh[:, k], ALU.mult))
                    done(nc.vector.tensor_reduce(destf[:, k, :], cand[:, :, :], AX, ALU.add))
                nc.vector.tensor_copy(dest[:, :, :], destf[:, :, :]).then_inc(placed, 1)
                done(nc.vector.tensor_tensor(cmpb[:, :, :], iota_b[0:1, :].unsqueeze(2).broadcast_to([1, NB, NE]),
                                             bend[0:1, :].unsqueeze(1).broadcast_to([1, NB, NE]), ALU.is_ge))
                done(nc.vector.tensor_reduce(fexp[:, :], cmpb[:, :, :], AX, ALU.add))
                done(nc.vector.tensor_scalar(expert[:, :], fexp[:, :], float(NE - 1), None, ALU.min))
                done(nc.vector.tensor_scalar(fexp[:, 0:NB // 2], iota_b[0:1, 0:NB:2], bend[0:1, NE - 1:NE], None, ALU.is_lt))
                done(nc.vector.tensor_reduce(npairs[:, :], fexp[:, 0:NB // 2], AX, ALU.add))
                done(nc.vector.tensor_copy(pairs[:, :], npairs[:, :]))
                dve.wait_ge(turned, 1)
                done(nc.vector.tensor_copy(idx[:, :], K.bank[2][:, 0:NB + 2]))


def moe_experts(nc, K, A, layer, expert, pairs, idx):
    weights_d = (A.moe_w_gate_2[layer].rearrange("e (k p) m -> e p k m", p=P), A.moe_w_up_2[layer].rearrange("e (k p) m -> e p k m", p=P),
                 A.moe_w_down_2[layer].rearrange("e (k p) m -> e p k m", p=P))
    GATE, UP, DOWN = range(3)
    WN = KD * HID
    HALF = WN // 2
    PER_BLOCK = 6
    with ExitStack() as mem:
        sb = lambda n, s, dt=F32: mem.enter_context(nc.sbuf_tensor(f"ex{layer}_{n}", s, dt))
        raw = sb("raw", [P, 3, WN])
        cut = Pair(mem, nc, f"ex{layer}_cut", [P, 2, WN])
        col = sb("col", [P, 2], U32)
        x = sb("x", [P, 2, D])
        xT = Pair(mem, nc, f"ex{layer}_xT", [P, 2, D])
        gate, h = sb("gate", [P, 2, HID]), sb("h", [P, 2, HID])
        hT = Pair(mem, nc, f"ex{layer}_hT", [P, 2, HID])
        y = sb("y", [P, 2, D])
        zero = sb("zero", [P, D])
        TX, GB, UB, HB, DB = K.bank[0:2], K.bank[2], K.bank[3], K.bank[4], K.bank[5:7]
        slot_of = lambda s, which: (s + which) % 2
        with stage(nc, "g_loaded", "u_loaded", "d_loaded", "w_rounded", "w_split", "named", "asked", "x_turned", "x_rounded", "x_split",
                   "gate_ready", "up_ready", "down_ready", "gate_done", "h_ready", "h_turned", "h_rounded", "h_split", "y_kept",
                   "y_stored0", "y_stored1", "zeroed", "filled") as (
                block, (g_loaded, u_loaded, d_loaded, w_rounded, w_split, named, asked, x_turned, x_rounded, x_split,
                        gate_ready, up_ready, down_ready, gate_done, h_ready, h_turned, h_rounded, h_split, y_kept, y_stored0, y_stored1,
                        zeroed, filled)):
            w_loaded, x_loaded, y_stored = (g_loaded, u_loaded, d_loaded), K.x_gathered, (y_stored0, y_stored1)

            def pairs_used(eng):
                return eng.value_load(pairs[0:1, 0:1], min_val=S * 2 // P // 2, max_val=NB // 2)

            @block.sync
            def _(sp):
                n = pairs_used(sp)
                sp.wait_ge(x_loaded[0], 16)
                with sp.Fori(0, n) as i:
                    for s in range(2):
                        b = i * 2 + s
                        e = sp.value_load(expert[0:1, ds(b, 1)], min_val=0, max_val=NE - 1)
                        for which in range(3):
                            sp.wait_ge(w_split, b * PER_BLOCK + 2 * which + 2)
                            sp.dma_start(raw[:, which].rearrange("p (k m) -> p k m", m=HID if which < DOWN else D),
                                         weights_d[which][ds(e, 1)].rearrange("e p k m -> p (e k) m")).then_inc(w_loaded[which], 16)
                    sp.sem_inc(filled, 32)
                sp.wait_ge(zeroed, 1)
                with sp.Fori(n, NB // 2 + 1) as i:
                    for s in range(2):
                        sp.dma_start(K.y_rows[ds((i * 2 + s) * P, P), :], zero[:, :]).then_inc(filled, 16)
                    sp.wait_ge(filled, i * 32 + 32)
                    sp.sem_inc(asked, 1)

            @block.gpsimd
            def _(pool):
                def gather(s, b):
                    nc.gpsimd.tensor_copy(col[:, s:s + 1], idx[:, ds(b, 1)]).then_inc(named, 1)
                    pool.wait_ge(named, b + 1)
                    pool.sem_inc(asked, 1)
                    nc.gpsimd.indirect_dma_start(out=x[:, s, :], out_offset=None, in_=K.x_rows,
                                                 in_offset=bass.IndirectOffsetOnAxis(ap=col[:, s:s + 1], axis=0)).then_inc(x_loaded[s], 16)

                gather(0, 0)
                nc.gpsimd.memset(zero[:, :], 0.0).then_inc(zeroed, 1)
                with pool.Fori(0, pairs_used(pool)) as i:
                    for s in range(2):
                        b = i * 2 + s
                        pool.wait_ge(x_turned, b + 1)
                        gather(1 - s, b + 1)

            @block.tensor
            def _(pe):
                def turn_x(s, loads):
                    pe.wait_ge(x_loaded[s], loads)
                    for k in range(KD):
                        last = nc.tensor.transpose(TX[k // 4][:, (k % 4) * P:(k % 4 + 1) * P], x[:, s, k * P:(k + 1) * P], K.ident[:, :])
                    last.then_inc(x_turned, 1)

                def multiply(out, rows, weights, tiles, first, total):
                    return product(nc, out, lambda part, k: part_of(rows, part)[:, s, k * P:(k + 1) * P], weights, tiles, first, total)

                pe.sem_inc(up_ready, 1)
                pe.sem_inc(down_ready, 1)
                pe.sem_inc(x_turned, 1)
                turn_x(0, 16)
                with pe.Fori(0, pairs_used(pe)) as i:
                    for s in range(2):
                        b = i * 2 + s
                        pe.wait_ge(x_split, b + 1)
                        pe.wait_ge(gate_done, b + 1)
                        for which, bank, ready in ((GATE, GB, gate_ready), (UP, UB, up_ready)):
                            if which == UP:
                                pe.wait_ge(h_ready, b + 1)
                            for half in range(2):
                                pe.wait_ge(w_split, b * PER_BLOCK + (PER_BLOCK + 2 * which + half + 1))
                                last = multiply(bank[:, :], xT, lambda part, k: part_of(cut, part)[:, slot_of(s, which), k * HID:(k + 1) * HID],
                                                KD // 2, half * KD // 2, KD)
                            last.then_inc(ready, 1)
                        turn_x(1 - s, i * 16 + 16 * (s + 1))
                        pe.wait_ge(h_ready, b + 2)
                        for k in range(KH):
                            last = nc.tensor.transpose(HB[:, k * P:(k + 1) * P], h[:, s, k * P:(k + 1) * P], K.ident[:, :])
                        last.then_inc(h_turned, 1)
                        pe.wait_ge(h_split, b + 1)
                        pe.wait_ge(y_kept, b + 1)
                        for half in range(2):
                            pe.wait_ge(w_split, b * PER_BLOCK + (PER_BLOCK + 2 * DOWN + half + 1))
                            for cols in range(2):
                                last = multiply(DB[cols][:, :], hT, lambda part, k: part_of(cut, part)[:, slot_of(s, DOWN), k * D + cols * 512:k * D + cols * 512 + 512],
                                                KH // 2, half * KH // 2, KH)
                        last.then_inc(down_ready, 1)

            @block.scalar
            def _(act):
                def round_x(s, b):
                    act.wait_ge(x_turned, b + 2)
                    nc.scalar.activation(xT.hi[:, s, 0:512], TX[0][:, :], ACT.Copy)
                    nc.scalar.activation(xT.hi[:, s, 512:D], TX[1][:, :], ACT.Copy).then_inc(x_rounded, 1)

                def round_weights(s, b, which):
                    act.wait_ge(w_loaded[which], b * 16 + 16)
                    for half in range(2):
                        part = slice(half * HALF, (half + 1) * HALF)
                        nc.scalar.activation(cut.hi[:, slot_of(s, which), part], raw[:, which, part], ACT.Copy).then_inc(w_rounded, 1)

                def store(s, i_next, b):
                    act.wait_ge(y_stored[s], i_next * 16 + 16)
                    nc.scalar.activation(y[:, s, 0:512], DB[0][:, :], ACT.Copy)
                    nc.scalar.activation(y[:, s, 512:D], DB[1][:, :], ACT.Copy).then_inc(y_kept, 1)
                    act.wait_ge(y_kept, b + 2)
                    act.dma_start(K.y_rows[ds(b * P, P), :], y[:, s, :]).then_inc(y_stored[s], 16)

                def run_block(i, s, first=False):
                    b = i * 2 + s
                    act.wait_ge(up_ready, b + 1)
                    round_weights(s, b, GATE)
                    act.wait_ge(down_ready, b + 1)
                    round_weights(s, b, UP)
                    if not first:
                        store(1 - s, i + s, b - 1)
                    act.wait_ge(gate_ready, b + 1)
                    nc.scalar.activation(gate[:, s, :], GB[:, :], ACT.Silu).then_inc(gate_done, 1)
                    round_weights(s, b, DOWN)
                    round_x(1 - s, b + 1)
                    act.wait_ge(h_turned, b + 1)
                    nc.scalar.activation(hT.hi[:, s, :], HB[:, :], ACT.Copy).then_inc(h_rounded, 1)

                act.sem_inc(gate_done, 1)
                act.sem_inc(y_kept, 1)
                for s in range(2):
                    act.sem_inc(y_stored[s], 32)
                n = pairs_used(act)
                round_x(0, 0)
                run_block(0, 0, first=True)
                run_block(0, 1)
                with act.Fori(1, n) as i:
                    run_block(i, 0)
                    run_block(i, 1)
                act.wait_ge(down_ready, n * 2 + 1)
                store(1, n, n * 2 - 1)
                for s in range(2):
                    act.wait_ge(y_stored[s], n * 16 + 32)
                act.sem_inc(asked, 1)

            @block.vector
            def _(dve):
                def split_x(s, b):
                    dve.wait_ge(x_rounded, b + 1)
                    for half in range(2):
                        part = slice(half * 512, (half + 1) * 512)
                        last = nc.vector.tensor_tensor(xT.lo[:, s, part], TX[half][:, :], xT.hi[:, s, part].bitcast(F32), ALU.subtract)
                    last.then_inc(x_split, 1)

                def split_part(which):
                    for half in range(2):
                        part = slice(half * HALF, (half + 1) * HALF)
                        dve.wait_ge(w_rounded, b * PER_BLOCK + (2 * which + half + 1))
                        nc.vector.tensor_tensor(cut.lo[:, slot_of(s, which), part], raw[:, which, part],
                                                cut.hi[:, slot_of(s, which), part].bitcast(F32), ALU.subtract).then_inc(w_split, 1)

                dve.sem_inc(w_split, PER_BLOCK)
                dve.sem_inc(h_ready, 1)
                split_x(0, 0)
                with dve.Fori(0, pairs_used(dve)) as i:
                    for s in range(2):
                        b = i * 2 + s
                        split_part(GATE)
                        split_part(UP)
                        split_part(DOWN)
                        dve.wait_ge(gate_done, b + 2)
                        dve.wait_ge(up_ready, b + 2)
                        nc.vector.tensor_tensor(h[:, s, :], gate[:, s, :], UB[:, :], ALU.mult).then_inc(h_ready, 1)
                        split_x(1 - s, b + 1)
                        dve.wait_ge(h_rounded, b + 1)
                        nc.vector.tensor_tensor(hT.lo[:, s, :], HB[:, :], hT.hi[:, s, :].bitcast(F32), ALU.subtract).then_inc(h_split, 1)


def moe_combine(nc, K, layer, weight, dest, o):
    with nc.sbuf_tensor(f"picked{layer}", [P, 2, TT, D], F32) as picked:
        with stage(nc, "weighed", "summed") as (block, (weighed, summed)):
            @block.gpsimd
            def _(pool):
                for t in range(TT):
                    for k in range(2):
                        nc.gpsimd.indirect_dma_start(out=picked[:, k, t, :], out_offset=None, in_=K.y_rows,
                                                     in_offset=bass.IndirectOffsetOnAxis(ap=dest[:, k, t:t + 1], axis=0)).then_inc(K.picked[2 * t + k], 16)

            @block.vector
            def _(dve):
                for t in range(TT):
                    dve.wait_ge(K.picked[2 * t], 16)
                    nc.vector.tensor_scalar(o[:, t, :], picked[:, 0, t, :], weight[:, 0, t:t + 1], None, ALU.mult).then_inc(weighed, 1)
                    dve.wait_ge(K.picked[2 * t + 1], 16)
                    dve.wait_ge(weighed, t + 1)
                    nc.vector.scalar_tensor_tensor(out=o[:, t, :], in0=picked[:, 1, t, :], scalar=weight[:, 1, t:t + 1], in1=o[:, t, :],
                                                   op0=ALU.mult, op1=ALU.add).then_inc(summed, 1)


AH = 8
AR = 4
ROPE = 16


def attention_constants():
    half = ROPE // 2
    inv = (500000.0 ** (-np.arange(0, ROPE, 2, dtype=np.float32) / ROPE)).astype(np.float32)
    rot, freq = np.zeros((P, P), np.float32), np.zeros((P, 1), np.float32)
    for base in (0, HD):
        for i in range(half):
            rot[base + half + i, base + i] = -1.0
            rot[base + i, base + half + i] = 1.0
            freq[base + i] = freq[base + half + i] = inv[i]
    j = np.arange(P)
    dist = (4 * j[:, None, None] + np.arange(AR)[None, :, None]) - np.arange(S)[None, None, :]
    near = np.where((dist >= 0) & (dist <= 128), 0.0, NEG)
    causal = np.where(j[:, None] >= j[None, :], 0.0, NEG)
    sparse = np.where((j[:, None] >= j[None, :]) & ((j[:, None] - j[None, :]) % 4 == 0), 0.0, NEG)
    masks = np.concatenate([near.reshape(P, AR * S), causal, sparse], 1)
    return np.concatenate([rot, freq, masks], 1).astype(np.float32)


def rope_tables(nc, A, const, cos, sin):
    TWO_PI = 2 * np.pi
    C1 = 6.28125
    C2 = float(np.float32(TWO_PI - C1))
    C3 = float(TWO_PI - C1 - C2)
    MAGIC = 1.5 * 2.0 ** 23
    PI = float(np.nextafter(np.float32(np.pi), np.float32(0)))
    with ExitStack() as mem:
        posi = mem.enter_context(nc.sbuf_tensor("pos_i", [P, S], I32))
        ang, n, r = (mem.enter_context(nc.sbuf_tensor(f"rope_{x}", [P, S], F32)) for x in ("ang", "n", "r"))
        with stage(nc, "loaded", "vec_step", "reduced", "taken") as (block, (loaded, vec_step, reduced, taken)):
            @block.sync
            def _(sp):
                sp.dma_start(posi[:, :], broadcast_row(A.positions_2)).then_inc(loaded, 16)

            @block.vector
            def _(dve):
                done = Settle(dve, vec_step)
                dve.wait_ge(loaded, 16)
                done(nc.vector.tensor_copy(ang[:, :], posi[:, :]))
                done(nc.vector.tensor_scalar(ang[:, :], ang[:, :], const[:, P:P + 1], None, ALU.mult))
                for k, (turn, shift) in enumerate(((0.0, 0.0), (0.25, np.pi / 2))):
                    done(nc.vector.tensor_scalar(n[:, :], ang[:, :], float(1 / TWO_PI), turn, ALU.mult, ALU.add))
                    done(nc.vector.tensor_scalar(n[:, :], n[:, :], MAGIC, MAGIC, ALU.add, ALU.subtract))
                    if k:
                        dve.wait_ge(taken, k)
                    done(nc.vector.scalar_tensor_tensor(out=r[:, :], in0=n[:, :], scalar=-C1, in1=ang[:, :], op0=ALU.mult, op1=ALU.add))
                    done(nc.vector.scalar_tensor_tensor(out=r[:, :], in0=n[:, :], scalar=-C2, in1=r[:, :], op0=ALU.mult, op1=ALU.add))
                    done(nc.vector.scalar_tensor_tensor(out=r[:, :], in0=n[:, :], scalar=-C3, in1=r[:, :], op0=ALU.mult, op1=ALU.add))
                    done(nc.vector.tensor_scalar(r[:, :], r[:, :], float(shift), PI, ALU.add, ALU.min))
                    nc.vector.tensor_scalar(r[:, :], r[:, :], -PI, None, ALU.max).then_inc(reduced, 1)
                    dve.wait_ge(reduced, k + 1)

            @block.scalar
            def _(act):
                for k, out in enumerate((sin, cos)):
                    act.wait_ge(reduced, k + 1)
                    nc.scalar.activation(out[:, :], r[:, :], ACT.Sin).then_inc(taken, 1)


def attention(nc, K, A, o):
    w = A.attn_w_qkv_2[0].rearrange("(k p) m -> p k m", p=P)
    HW = AH * HD
    const_dram = nc.inline_tensor(attention_constants(), name="attention_constants").ap()
    with ExitStack() as mem:
        sb = lambda n, s: mem.enter_context(nc.sbuf_tensor(f"dil_{n}", s, F32))
        ores = sb("ores", [P, AR, HW])
        with ExitStack() as inner:
            sb2 = lambda n, s: inner.enter_context(nc.sbuf_tensor(f"dil_{n}", s, F32))
            qk = sb2("qk", [P, 3, 8, S])
            v = sb2("v", [P, 3, TT, HW])
            with ExitStack() as early:
                xT = Pair(early, nc, "dil_xT", [P, KD, S])
                to_channels(nc, K, K.x, xT, KD)
                def group_jobs(rows):
                    jobs = []
                    for part in range(3):
                        for c in range(2):
                            load = columns(w, lambda i, first=part * HW + c * CW: i * (3 * HW) + first)
                            if part < 2:
                                jobs.append(channels_job(nc, xT, KD, load, lambda bank, m, i, part=part, c=c: nc.scalar.activation(
                                    qk[:, i, 4 * part + 2 * c + m, :] if isinstance(i, int) else
                                    qk[:, ds(i, 1), 4 * part + 2 * c + m, :].rearrange("p o n -> p (o n)"),
                                    bank, ACT.Copy, scale=1.0 if part else HD ** -0.5)))
                            else:
                                jobs.append(tokens_job(nc, xT, KD, load, lambda bank, t, i, c=c: nc.scalar.activation(
                                    v[:, i, t, c * CW:(c + 1) * CW] if isinstance(i, int) else
                                    v[:, ds(i, 1), t, c * CW:(c + 1) * CW].rearrange("p o n -> p (o n)"), bank, ACT.Copy), rows))
                    return jobs

                project(nc, K, KD, group_jobs(lambda r: slice(r, S, AR)), passes=2, lead=group_jobs(lambda t: slice(t * P, (t + 1) * P)))
            const = sb2("const", [P, P + 1 + AR * S + 2 * P])
            cos, sin = sb2("cos", [P, S]), sb2("sin", [P, S])
            with stage(nc, "loaded") as (block, (loaded,)):
                @block.sync
                def _(sp):
                    sp.dma_start(const[:, :], const_dram).then_inc(loaded, 16)
                    sp.wait_ge(loaded, 16)
            rope_tables(nc, A, const, cos, sin)
            attend_residues(nc, K, const, cos, sin, qk, v, ores)
        oT = Pair(mem, nc, "dil_oT", [P, HW // P, S])
        to_channels(nc, K, ores, oT, HW // P, residues=True)
        project_model(nc, K, A.attn_w_o_2[0], HW // P, oT, o)


def attend_residues(nc, K, const, cos, sin, qk, v, ores):
    PAIRS = AH // 2
    UNITS = [(it, a, r) for it in range(PAIRS) for a in range(2) for r in range(AR)]
    U = 2 * AR
    N = len(UNITS)
    ROLES = 6
    W = S + 2 * P
    rot = const[:, 0:P]
    near = const[:, P + 1:P + 1 + AR * S].rearrange("p (r n) -> p r n", r=AR)
    sparse = const[:, P + 1 + AR * S:]
    source = lambda it, n: qk[:, n % 3, it + 4 * (n // 3), :]
    with ExitStack() as mem:
        sb = lambda n, s: mem.enter_context(nc.sbuf_tensor(f"ar_{n}", s, F32))
        by_sin, by_cos = sb("by_sin", [P, 2, S]), sb("by_cos", [P, 2, S])
        ready = sb("ready", [P, 2, ROLES, S])
        logit, prob, probT = sb("logit", [P, 2, W]), sb("prob", [P, 3, W]), sb("probT", [P, 2, W])
        st = sb("st", [P, 2, 4])
        recips = sb("recips", [P, N])
        SPUN, OUT = K.bank[7], K.bank[6]
        with stage(nc, "spun", "spun_read", "vec_step", "prepared", "scored", "biased", "exped", "turned", "copied", "valued", "kept") as (
                block, (spun, spun_read, vec_step, prepared, scored, biased, exped, turned, copied, valued, kept)):

            @block.tensor
            def _(pe):
                def spin(it, n):
                    if it or n:
                        pe.wait_ge(spun_read, it * ROLES + n)
                    nc.tensor.matmul(SPUN[:, :], rot, source(it, n), start=True, stop=True).then_inc(spun, 1)

                for n in range(ROLES):
                    spin(0, n)
                for step in range(N + 3):
                    if step < N:
                        u = step
                        it, a, r = UNITS[u]
                        rows = slice(a * HD, (a + 1) * HD)
                        b0, b1 = K.bank[2 * (u % 2)], K.bank[2 * (u % 2) + 1]
                        if u % U == 0:
                            pe.wait_ge(prepared, it + 1)
                        if u >= 2:
                            pe.wait_ge(biased, u - 1)
                        toks = slice(r * P, (r + 1) * P)
                        role = ready[rows, it % 2]
                        nc.tensor.matmul(b0[:, :], role[:, 0, toks], role[:, 3, :], start=True, stop=True)
                        nc.tensor.matmul(b1[:, 0:P], role[:, 1, toks], role[:, 4, toks], start=True, stop=True)
                        nc.tensor.matmul(b1[:, P:2 * P], role[:, 2, toks], role[:, 5, toks], start=True, stop=True).then_inc(scored, 1)
                        if u % U < ROLES and it + 1 < PAIRS:
                            spin(it + 1, u % U)
                    if 2 <= step <= N + 1:
                        u = step - 2
                        pe.wait_ge(exped, u + 1)
                        if u >= 1:
                            pe.wait_ge(copied, u)
                        for j in range(W // P):
                            last = nc.tensor.transpose(K.bank[4 + j // 4][:, (j % 4) * P:(j % 4 + 1) * P], prob[:, u % 3, j * P:(j + 1) * P], K.ident[:, :])
                        last.then_inc(turned, 1)
                    if step >= 3:
                        u = step - 3
                        it, a, r = UNITS[u]
                        pe.wait_ge(copied, u + 1)
                        if u >= 1:
                            pe.wait_ge(kept, u)
                        cols = slice((2 * it + a) * HD, (2 * it + a + 1) * HD)
                        for j in range(W // P):
                            g, t = (0, j) if j < TT else (j - TT + 1, r)
                            last = nc.tensor.matmul(OUT[:, 0:HD], probT[:, u % 2, j * P:(j + 1) * P], v[:, g, t, cols],
                                                    start=(j == 0), stop=(j == W // P - 1))
                        last.then_inc(valued, 1)

            @block.scalar
            def _(act):
                for step in range(N + 2):
                    if step < N:
                        u = step
                        act.wait_ge(biased, u + 1)
                        if u >= 3:
                            act.wait_ge(turned, u - 2)
                        nc.scalar.activation(prob[:, u % 3, :], logit[:, u % 2, :], ACT.Exp, bias=st[:, u % 2, 2:3],
                                             accum_out=st[:, u % 2, 3:4]).then_inc(exped, 1)
                    if step >= 2:
                        u = step - 2
                        act.wait_ge(turned, u + 1)
                        if u >= 2:
                            act.wait_ge(valued, u - 1)
                        nc.scalar.activation(probT[:, u % 2, 0:S], K.bank[4][:, :], ACT.Copy)
                        nc.scalar.activation(probT[:, u % 2, S:W], K.bank[5][:, 0:W - S], ACT.Copy).then_inc(copied, 1)

            @block.vector
            def _(dve):
                done = Settle(dve, vec_step)

                def rotate(it, n):
                    dve.wait_ge(spun, it * ROLES + n + 1)
                    nc.vector.tensor_tensor(by_sin[:, n % 2, :], SPUN[:, :], sin[:, :], ALU.mult).then_inc(spun_read, 1)
                    done(nc.vector.tensor_tensor(by_cos[:, n % 2, :], source(it, n), cos[:, :], ALU.mult))
                    dve.wait_ge(spun_read, it * ROLES + n + 1)
                    out, c, s = ready[:, it % 2, n, :], by_cos[:, n % 2, :], by_sin[:, n % 2, :]
                    if n != 3:
                        out = out.rearrange("p (r j) -> p r j", r=AR)
                        c, s = (x.rearrange("p (j r) -> p r j", r=AR) for x in (c, s))
                    ins = nc.vector.tensor_tensor(out, c, s, ALU.add)
                    if n == ROLES - 1:
                        ins.then_inc(prepared, 1)

                for n in range(ROLES):
                    rotate(0, n)
                for step in range(N + 4):
                    if step >= 4:
                        u = step - 4
                        it, a, r = UNITS[u]
                        dve.wait_ge(valued, u + 1)
                        nc.vector.tensor_scalar(ores[:, r, (2 * it + a) * HD:(2 * it + a + 1) * HD], OUT[:, 0:HD], recips[:, u:u + 1], None,
                                                ALU.mult).then_inc(kept, 1)
                    if step < N:
                        u = step
                        it, a, r = UNITS[u]
                        s = st[:, u % 2]
                        dve.wait_ge(scored, u + 1)
                        if u >= 2:
                            dve.wait_ge(exped, u - 1)
                        nc.vector.tensor_tensor_reduce(out=logit[:, u % 2, 0:S], in0=K.bank[2 * (u % 2)][:, :], in1=near[:, r, :], scale=1.0,
                                                       scalar=-3e38, op0=ALU.add, op1=ALU.max, accum_out=s[:, 0:1])
                        done(nc.vector.tensor_tensor_reduce(out=logit[:, u % 2, S:W], in0=K.bank[2 * (u % 2) + 1][:, 0:2 * P], in1=sparse, scale=1.0,
                                                            scalar=-3e38, op0=ALU.add, op1=ALU.max, accum_out=s[:, 1:2]))
                        nc.vector.tensor_reduce(s[:, 2:3], s[:, 0:2], AX, ALU.max, negate=True).then_inc(biased, 1)
                        if u % U < ROLES and it + 1 < PAIRS:
                            rotate(it + 1, u % U)
                    if 1 <= step <= N:
                        u = step - 1
                        dve.wait_ge(exped, u + 1)
                        done(nc.vector.reciprocal(recips[:, u:u + 1], st[:, u % 2, 3:4]))


def second_block(nc, K, A):
    with nc.sbuf_tensor("mix", [P, TT, D], F32) as o:
        ssd(nc, K, A, o)
        layer_norm(nc, K, o, A.ln_g_2[0, 0], A.ln_b_2[0, 0])
        moe(nc, K, A, 0, o)
        layer_norm(nc, K, o, A.ln_g_2[0, 1], A.ln_b_2[0, 1])
        attention(nc, K, A, o)
        layer_norm(nc, K, o, A.ln_g_2[1, 0], A.ln_b_2[1, 0])
        moe(nc, K, A, 1, o)
        layer_norm(nc, K, o, A.ln_g_2[1, 1], A.ln_b_2[1, 1])


def program(nc, A, out):
    RESTING.clear()
    K = Names()
    K.bank = [nc.alloc_psum_tensor(f"bank{i}", [P, S], F32) for i in range(8)]
    K.x = nc.alloc_sbuf_tensor("x_tok", [P, TT, D], F32)
    constants(nc, K, A)
    with stage(nc, "x_loaded") as (block, (x_loaded,)):
        @block.sync
        def _(sp):
            sp.dma_start(K.x[:, :, :], A.x[0].rearrange("(t p) d -> p t d", p=P)).then_inc(x_loaded, 16)
            sp.wait_ge(x_loaded, 16)
    first_block(nc, K, A)
    second_block(nc, K, A)
    with stage(nc, "x_stored") as (block, (x_stored,)):
        @block.sync
        def _(sp):
            sp.dma_start(out[0].rearrange("(t p) d -> p t d", p=P), K.x[:, :, :]).then_inc(x_stored, 16)
            sp.wait_ge(x_stored, 16)


def first_block(nc, K, A):
    with ExitStack() as mem:
        sb = lambda n, s: mem.enter_context(nc.sbuf_tensor(n, s, F32))
        K.hT = Pair(mem, nc, "hT", [P, KD, S])
        with ExitStack() as inner:
            h = inner.enter_context(nc.sbuf_tensor("h_tok", [P, TT, D], F32))
            rms_scale(nc, K, K.x, h)
            to_channels(nc, K, h, K.hT, KD, lambda k: vcol(K, "g0", k))
        y = [sb("y0", [P, KD, S])]
        lru(nc, K, A, y[0])
        y.append(sb("y1", [P, KD, S]))
        nsa(nc, K, A, y[1])
        y.append(sb("y2", [P, KD, S]))
        gla(nc, K, A, y[2])
        merged = sb("merged", [P, KD, S])
        merge(nc, K, A, y, merged)
        o = sb("mixed", [P, TT, D])
        with ExitStack() as inner:
            mpair = Pair(inner, nc, "merged", [P, KD, S])
            split(nc, mpair, merged, KD, "merged")
            project_model(nc, K, A.w_out[0], KD, mpair, o)
        residual_norm(nc, K, o, A.norm_g[0, 1])
    with ExitStack() as mem:
        K.hT = Pair(mem, nc, "h2T", [P, KD, S])
        with nc.sbuf_tensor("h2_tok", [P, TT, D], F32) as h:
            rms_scale(nc, K, K.x, h)
            to_channels(nc, K, h, K.hT, KD, lambda k: vcol(K, "g2", k))
        ffn(nc, K, A)


_INS = ["x", "rel_table", "norm_g", "w_in", "conv_w", "conv_b", "lru_w_gates", "lru_b_gates", "lru_lambda", "cmp_pos", "cmp_w1",
        "cmp_w2", "gla_wa2", "gla_ba", "gla_norm", "w_branch", "w_out", "w_ffn_in", "w_ffn_out", "positions_2", "ssd_w_in_2",
        "ssd_conv_w_2", "ssd_conv_b_2", "ssd_dt_bias_2", "ssd_a_log_2", "ssd_d_2", "ssd_norm_w_2", "ssd_w_out_2", "attn_w_qkv_2",
        "attn_w_o_2", "ln_g_2", "ln_b_2", "moe_w_router_group_2", "moe_b_router_group_2", "moe_w_router_expert_2",
        "moe_b_router_expert_2", "moe_w_gate_2", "moe_w_up_2", "moe_w_down_2"]


def kernel(**inputs):
    import concourse.bacc as bacc
    from concourse.bass_utils import run_bass_kernel_spmd

    nc = bacc.Bacc("TRN2", target_bir_lowering=False, num_devices=1)
    arrays, A = {}, Names()
    for name in _INS:
        a = np.ascontiguousarray(inputs[name])
        arrays[f"in_{name}"] = a
        A.__dict__[name] = nc.dram_tensor(f"in_{name}", a.shape, mybir.dt.from_np(a.dtype), kind="ExternalInput").ap()
    out = nc.dram_tensor("out", (1, S, D), F32, kind="ExternalOutput").ap()
    program(nc, A, out)
    result = run_bass_kernel_spmd(nc, [arrays], core_ids=[0])
    return result.results[0]["out"]
```
